# Optimizing a Trainium2 kernel written in Bass

```python
import math
import jax
import jax.numpy as jnp
from jax import lax
import numpy as np

D_MODEL = 1024
BATCH = 1
SEQ = 1024
DEPTH = 1
DEC_BATCH = 8
DEC_SEQ = 8
PAST_LEN = 4096
PAGE_SIZE = 128

ATTN_HEADS = 4
QK_DIM = 64
V_DIM = 2 * QK_DIM
ATTN_WIDTH = ATTN_HEADS * V_DIM
QK_COLS = ATTN_HEADS * 2 * QK_DIM
ROT_DIM = QK_DIM // 4
ROPE_THETA = 500000.0
Q_BLOCK = 128
RG_WIDTH = D_MODEL - ATTN_WIDTH
RG_BLOCKS = 8
RG_BLOCK_W = RG_WIDTH // RG_BLOCKS
RG_C = 8.0
CONV_WIDTH = 4
MIX_WIDTH = ATTN_WIDTH + RG_WIDTH
IN_WIDTH = 2 * QK_COLS + ATTN_WIDTH + 2 * RG_WIDTH
PEER_HEADS = 8
PEER_KEYS = 128
PEER_EXPERTS = PEER_KEYS * PEER_KEYS
PEER_TOPK = 16
PEER_QHALF = 128
PEER_BLOCK = 128
PLE_DIM = 256
LN_EPS = 1e-5
DEEPNORM_ALPHA = (2.0 * DEPTH) ** 0.25
DEEPNORM_BETA = (8.0 * DEPTH) ** -0.25

kernel_name = 'hybrid_diffattn_rglru_peer_step'

def layer_norm(x, g, b):
    xf = x.astype(jnp.float32)
    mu = jnp.mean(xf, -1, keepdims=True)
    var = jnp.mean(jnp.square(xf - mu), -1, keepdims=True)
    return ((xf - mu) * lax.rsqrt(var + LN_EPS)).astype(x.dtype) * g + b

def rotary(x, pos):
    half = ROT_DIM // 2
    inv_freq = jnp.float32(ROPE_THETA) ** (-jnp.arange(0, ROT_DIM, 2, dtype=jnp.float32) / ROT_DIM)
    ang = pos.astype(jnp.float32)[:, None] * inv_freq[None, :]
    cos = jnp.cos(ang)[:, None, None, :]
    sin = jnp.sin(ang)[:, None, None, :]
    xr = x[..., :ROT_DIM].astype(jnp.float32)
    x1, x2 = xr[..., :half], xr[..., half:]
    rot = jnp.concatenate([x1 * cos - x2 * sin, x2 * cos + x1 * sin], -1).astype(x.dtype)
    return jnp.concatenate([rot, x[..., ROT_DIM:]], -1)

def diff_attention(q, k, v, q_pos, k_pos, lam):
    s = jnp.einsum('bqhmd,bkhmd->bhmqk', q, k).astype(jnp.float32) * (QK_DIM ** -0.5)
    mask = k_pos[None, :] <= q_pos[:, None]
    p = jax.nn.softmax(jnp.where(mask, s, -jnp.inf), axis=-1)
    w = (p[:, :, 0] - lam * p[:, :, 1]).astype(v.dtype)
    return jnp.einsum('bhqk,bkhd->bqhd', w, v)

def prompt_attention(q, k, v, pos, lam):
    b, s = q.shape[:2]
    nb = s // Q_BLOCK
    qb = jnp.moveaxis(q.reshape(b, nb, Q_BLOCK, ATTN_HEADS, 2, QK_DIM), 1, 0)
    pb = pos.reshape(nb, Q_BLOCK)
    o = lax.map(lambda a: diff_attention(a[0], k, v, a[1], pos, lam), (qb, pb))
    return jnp.moveaxis(o, 0, 1).reshape(b, s, ATTN_HEADS, V_DIM)

def sample_attention(q, k, v, pos, past_k, past_v, lam):
    k_all = jnp.concatenate([past_k.astype(k.dtype), k], 1)
    v_all = jnp.concatenate([past_v.astype(v.dtype), v], 1)
    k_pos = jnp.arange(k_all.shape[1])
    return diff_attention(q, k_all, v_all, pos, k_pos, lam)

def _lin_combine(e1, e2):
    a1, b1 = e1
    a2, b2 = e2
    return a1 * a2, a2 * b1 + b2

def rg_lru_branch(xr, gate, h0, conv_buf, conv_w, conv_b, wa, ba, wx, bx, lam):
    b, s, c = xr.shape
    xp = jnp.concatenate([conv_buf.astype(xr.dtype), xr], 1)
    xc = conv_b + sum(xp[:, j:j + s] * conv_w[j] for j in range(CONV_WIDTH))
    conv_new = xp[:, -(CONV_WIDTH - 1):]
    xb = xc.reshape(b, s, RG_BLOCKS, RG_BLOCK_W)
    r = jax.nn.sigmoid(jnp.einsum('bsnc,ncd->bsnd', xb, wa).reshape(b, s, c) + ba)
    i = jax.nn.sigmoid(jnp.einsum('bsnc,ncd->bsnd', xb, wx).reshape(b, s, c) + bx)
    log_a = -RG_C * jax.nn.softplus(-lam.astype(jnp.float32)) * r.astype(jnp.float32)
    a = jnp.exp(log_a)
    u = jnp.sqrt(-jnp.expm1(2.0 * log_a)) * (i * xc).astype(jnp.float32)
    u = u.at[:, 0].add(a[:, 0] * h0.astype(jnp.float32))
    _, h = lax.associative_scan(_lin_combine, (a, u), axis=1)
    y = h.astype(xr.dtype) * jax.nn.gelu(gate)
    return y, h[:, -1].astype(xr.dtype), conv_new

def peer_ffn(x, wq, keys, u_tab, v_tab):
    b, s, d = x.shape
    t = x.reshape(b * s, d)
    n_tok = t.shape[0]
    n_blk = -(-n_tok // PEER_BLOCK)
    t = jnp.pad(t, ((0, n_blk * PEER_BLOCK - n_tok), (0, 0))).reshape(n_blk, PEER_BLOCK, d)

    def block(tb):
        q = (tb @ wq).reshape(PEER_BLOCK, PEER_HEADS, 2, PEER_QHALF)
        sc = jnp.einsum('thpd,hpnd->thpn', q, keys).astype(jnp.float32)
        s1, i1 = lax.top_k(sc[:, :, 0], PEER_TOPK)
        s2, i2 = lax.top_k(sc[:, :, 1], PEER_TOPK)
        cand = (s1[..., :, None] + s2[..., None, :]).reshape(PEER_BLOCK, PEER_HEADS, PEER_TOPK * PEER_TOPK)
        cidx = (i1[..., :, None] * PEER_KEYS + i2[..., None, :]).reshape(PEER_BLOCK, PEER_HEADS, PEER_TOPK * PEER_TOPK)
        top_s, top_p = lax.top_k(cand, PEER_TOPK)
        eidx = jnp.take_along_axis(cidx, top_p, axis=-1)
        g = jax.nn.softmax(top_s, axis=-1)
        act = jax.nn.gelu(jnp.einsum('td,thkd->thk', tb, u_tab[eidx]))
        w = (g * act.astype(jnp.float32)).astype(tb.dtype)
        return jnp.einsum('thk,thkd->td', w, v_tab[eidx])

    out = lax.map(block, t).reshape(n_blk * PEER_BLOCK, d)[:n_tok]
    return out.reshape(b, s, d)

def decoder_layer(x, pe, pos, h0, conv_buf, attend, lam_init, w):
    b, s, _ = x.shape
    proj = x @ w['w_in']
    c1 = QK_COLS
    c2 = 2 * QK_COLS
    c3 = c2 + ATTN_WIDTH
    c4 = c3 + RG_WIDTH
    q, k, v, xr, gate = proj[..., :c1], proj[..., c1:c2], proj[..., c2:c3], proj[..., c3:c4], proj[..., c4:]
    q = rotary(q.reshape(b, s, ATTN_HEADS, 2, QK_DIM), pos)
    k = rotary(k.reshape(b, s, ATTN_HEADS, 2, QK_DIM), pos)
    v = v.reshape(b, s, ATTN_HEADS, V_DIM)
    o = attend(q, k, v).astype(jnp.float32)
    o = o * lax.rsqrt(jnp.mean(o * o, -1, keepdims=True) + LN_EPS) * (1.0 - lam_init)
    o = (o.astype(x.dtype) * w['subln_g']).reshape(b, s, ATTN_WIDTH)
    yr, h_last, conv_new = rg_lru_branch(xr, gate, h0, conv_buf, w['conv_w'], w['conv_b'],
                                         w['rg_wa'], w['rg_ba'], w['rg_wx'], w['rg_bx'], w['rg_lambda'])
    mix = jnp.concatenate([o, yr], -1) @ w['w_out']
    x1 = layer_norm(DEEPNORM_ALPHA * x + mix, w['ln1_g'], w['ln1_b'])
    ffn = peer_ffn(x1, w['peer_wq'], w['peer_keys'], w['peer_u'], w['peer_v'])
    x2 = layer_norm(DEEPNORM_ALPHA * x1 + ffn, w['ln2_g'], w['ln2_b'])
    gate_ple = jax.nn.sigmoid(x2 @ w['ple_gate_w'] + w['ple_gate_b'])
    y = x2 + gate_ple * (pe.astype(x.dtype) @ w['ple_w'])
    return y, k.reshape(b, s, ATTN_HEADS, 2 * QK_DIM), v, h_last, conv_new

def setup_inputs(seed: int = 0) -> dict:
    key = jax.random.key(seed)
    ks = iter(jax.random.split(key, 40))
    n_pages = PAST_LEN // PAGE_SIZE
    n_pool = (DEC_BATCH * n_pages * 5) // 4

    def nrm(shape, scale):
        return jax.random.normal(next(ks), shape, jnp.float32) * scale

    x_prompt = nrm((BATCH, SEQ, D_MODEL), 1.0)
    x_sample = nrm((DEC_BATCH, DEC_SEQ, D_MODEL), 1.0)
    p_prompt = nrm((DEPTH, BATCH, SEQ, PLE_DIM), 1.0)
    p_sample = nrm((DEPTH, DEC_BATCH, DEC_SEQ, PLE_DIM), 1.0)
    cache_k = nrm((DEPTH, n_pool, PAGE_SIZE, ATTN_HEADS, 2 * QK_DIM), 1.0)
    cache_v = nrm((DEPTH, n_pool, PAGE_SIZE, ATTN_HEADS, V_DIM), 1.0)
    state_h = nrm((DEPTH, DEC_BATCH, RG_WIDTH), 0.5)
    state_conv = nrm((DEPTH, DEC_BATCH, CONV_WIDTH - 1, RG_WIDTH), 1.0)
    page_table = jax.random.permutation(next(ks), n_pool)[:DEC_BATCH * n_pages].reshape(DEC_BATCH, n_pages).astype(jnp.int32)
    w_in = nrm((DEPTH, D_MODEL, IN_WIDTH), D_MODEL ** -0.5)
    lambda_q1 = nrm((DEPTH, QK_DIM), 0.1)
    lambda_k1 = nrm((DEPTH, QK_DIM), 0.1)
    lambda_q2 = nrm((DEPTH, QK_DIM), 0.1)
    lambda_k2 = nrm((DEPTH, QK_DIM), 0.1)
    subln_g = 1.0 + nrm((DEPTH, V_DIM), 0.01)
    conv_w = nrm((DEPTH, CONV_WIDTH, RG_WIDTH), CONV_WIDTH ** -0.5)
    conv_b = nrm((DEPTH, RG_WIDTH), 0.01)
    rg_wa = nrm((DEPTH, RG_BLOCKS, RG_BLOCK_W, RG_BLOCK_W), RG_BLOCK_W ** -0.5)
    rg_ba = nrm((DEPTH, RG_WIDTH), 0.01)
    rg_wx = nrm((DEPTH, RG_BLOCKS, RG_BLOCK_W, RG_BLOCK_W), RG_BLOCK_W ** -0.5)
    rg_bx = nrm((DEPTH, RG_WIDTH), 0.01)
    a_pow = jax.random.uniform(next(ks), (DEPTH, RG_WIDTH), jnp.float32, 0.9, 0.999)
    sig = a_pow ** (1.0 / RG_C)
    rg_lambda = jnp.log(sig) - jnp.log1p(-sig)
    w_out = nrm((DEPTH, MIX_WIDTH, D_MODEL), DEEPNORM_BETA * MIX_WIDTH ** -0.5)
    ln1_g = 1.0 + nrm((DEPTH, D_MODEL), 0.01)
    ln1_b = nrm((DEPTH, D_MODEL), 0.01)
    peer_wq = nrm((DEPTH, D_MODEL, PEER_HEADS * 2 * PEER_QHALF), D_MODEL ** -0.5)
    peer_keys = nrm((DEPTH, PEER_HEADS, 2, PEER_KEYS, PEER_QHALF), PEER_QHALF ** -0.5)
    peer_u = nrm((DEPTH, PEER_EXPERTS, D_MODEL), D_MODEL ** -0.5)
    peer_v = nrm((DEPTH, PEER_EXPERTS, D_MODEL), DEEPNORM_BETA * PEER_HEADS ** -0.5)
    ln2_g = 1.0 + nrm((DEPTH, D_MODEL), 0.01)
    ln2_b = nrm((DEPTH, D_MODEL), 0.01)
    ple_w = nrm((DEPTH, PLE_DIM, D_MODEL), DEEPNORM_BETA * PLE_DIM ** -0.5)
    ple_gate_w = nrm((DEPTH, D_MODEL, D_MODEL), D_MODEL ** -0.5)
    ple_gate_b = nrm((DEPTH, D_MODEL), 0.01)
    return {'x_prompt': x_prompt, 'x_sample': x_sample, 'p_prompt': p_prompt, 'p_sample': p_sample,
            'cache_k': cache_k, 'cache_v': cache_v, 'state_h': state_h, 'state_conv': state_conv,
            'page_table': page_table, 'w_in': w_in, 'lambda_q1': lambda_q1, 'lambda_k1': lambda_k1,
            'lambda_q2': lambda_q2, 'lambda_k2': lambda_k2, 'subln_g': subln_g, 'conv_w': conv_w,
            'conv_b': conv_b, 'rg_wa': rg_wa, 'rg_ba': rg_ba, 'rg_wx': rg_wx, 'rg_bx': rg_bx,
            'rg_lambda': rg_lambda, 'w_out': w_out, 'ln1_g': ln1_g, 'ln1_b': ln1_b,
            'peer_wq': peer_wq, 'peer_keys': peer_keys, 'peer_u': peer_u, 'peer_v': peer_v,
            'ln2_g': ln2_g, 'ln2_b': ln2_b, 'ple_w': ple_w, 'ple_gate_w': ple_gate_w,
            'ple_gate_b': ple_gate_b}

def reference(x_prompt, x_sample, p_prompt, p_sample, cache_k, cache_v, state_h, state_conv,
              page_table, w_in, lambda_q1, lambda_k1, lambda_q2, lambda_k2, subln_g, conv_w,
              conv_b, rg_wa, rg_ba, rg_wx, rg_bx, rg_lambda, w_out, ln1_g, ln1_b, peer_wq,
              peer_keys, peer_u, peer_v, ln2_g, ln2_b, ple_w, ple_gate_w, ple_gate_b):
    bp, s = x_prompt.shape[:2]
    bd, t = x_sample.shape[:2]
    past = page_table.shape[1] * cache_k.shape[2]
    pos_p = jnp.arange(s)
    pos_d = past + jnp.arange(t)
    xp, xd = x_prompt, x_sample
    kp_l, vp_l, hp_l, cp_l, kd_l, vd_l, hd_l, cd_l = [], [], [], [], [], [], [], []
    for l in range(DEPTH):
        lam_init = 0.8 - 0.6 * math.exp(-0.3 * l)
        lam = (jnp.exp(jnp.sum(lambda_q1[l].astype(jnp.float32) * lambda_k1[l].astype(jnp.float32)))
               - jnp.exp(jnp.sum(lambda_q2[l].astype(jnp.float32) * lambda_k2[l].astype(jnp.float32)))
               + lam_init)
        w = {'w_in': w_in[l], 'subln_g': subln_g[l], 'conv_w': conv_w[l], 'conv_b': conv_b[l],
             'rg_wa': rg_wa[l], 'rg_ba': rg_ba[l], 'rg_wx': rg_wx[l], 'rg_bx': rg_bx[l],
             'rg_lambda': rg_lambda[l], 'w_out': w_out[l], 'ln1_g': ln1_g[l], 'ln1_b': ln1_b[l],
             'peer_wq': peer_wq[l], 'peer_keys': peer_keys[l], 'peer_u': peer_u[l],
             'peer_v': peer_v[l], 'ln2_g': ln2_g[l], 'ln2_b': ln2_b[l], 'ple_w': ple_w[l],
             'ple_gate_w': ple_gate_w[l], 'ple_gate_b': ple_gate_b[l]}
        h0_p = jnp.zeros((bp, RG_WIDTH), xp.dtype)
        cb_p = jnp.zeros((bp, CONV_WIDTH - 1, RG_WIDTH), xp.dtype)
        xp, kp, vp, hp, cp = decoder_layer(
            xp, p_prompt[l], pos_p, h0_p, cb_p,
            lambda q, k, v: prompt_attention(q, k, v, pos_p, lam), lam_init, w)
        past_k = cache_k[l][page_table].reshape(bd, past, ATTN_HEADS, 2, QK_DIM)
        past_v = cache_v[l][page_table].reshape(bd, past, ATTN_HEADS, V_DIM)
        xd, kd, vd, hd, cd = decoder_layer(
            xd, p_sample[l], pos_d, state_h[l], state_conv[l],
            lambda q, k, v: sample_attention(q, k, v, pos_d, past_k, past_v, lam), lam_init, w)
        kp_l.append(kp)
        vp_l.append(vp)
        hp_l.append(hp)
        cp_l.append(cp)
        kd_l.append(kd)
        vd_l.append(vd)
        hd_l.append(hd)
        cd_l.append(cd)
    k_prompt = jnp.stack(kp_l)
    v_prompt = jnp.stack(vp_l)
    h_prompt = jnp.stack(hp_l)
    conv_prompt = jnp.stack(cp_l)
    k_sample = jnp.stack(kd_l)
    v_sample = jnp.stack(vd_l)
    h_sample = jnp.stack(hd_l)
    conv_sample = jnp.stack(cd_l)
    return (xp, xd, k_prompt, v_prompt, h_prompt, conv_prompt, k_sample, v_sample, h_sample, conv_sample)


_drawn_inputs = setup_inputs


def setup_inputs(seed=0):
    import zlib

    import numpy as np

    out = dict(_drawn_inputs(seed))
    spreads = {}
    factors = {'lambda_q1': 8.0,
     'subln_g': 120.328,
     'rg_ba': 21.35,
     'rg_bx': 8.0,
     'ln1_g': 62.777,
     'ln1_b': 63.878,
     'ln2_g': 200.0,
     'ln2_b': 198.054,
     'ple_gate_b': 200.0,
     'lambda_q2': 2.85,
     'p_prompt': 4.88,
     'p_sample': 4.79,
     'ple_w': 4.805,
     'ple_gate_w': 6.945}
    for name, (base, spread) in spreads.items():
        noise = np.random.default_rng([zlib.crc32(name.encode()), seed]).standard_normal(out[name].shape)
        drawn = base * np.exp(spread * noise) if base else spread * noise
        out[name] = jnp.asarray(drawn.astype(out[name].dtype))
    for name, factor in factors.items():
        out[name] = (out[name] * factor).astype(out[name].dtype)
    return out
```

```python
import math
from contextlib import ExitStack

import concourse.bass as bass
from concourse import mybir

F32 = mybir.dt.float32
I32 = mybir.dt.int32
U32 = mybir.dt.uint32
ALU = mybir.AluOpType
ACT = mybir.ActivationFunctionType
AX_X = mybir.AxisListType.X

P = 128
D = 1024
KC = D // P
SEQ = 1024
NT = SEQ // P
DB, DS = 8, 8
SR = DB * DS
PAST, PAGE = 4096, 128
NPG = PAST // PAGE
H, QK, VD = 4, 64, 128
AW = H * VD
RW = D - AW
RC = RW // P
IN = 3 * AW + 2 * RW
ROT = QK // 4
HALF = ROT // 2
CW = 4
PH, PK, TOPK = 8, 128, 16
PLE = 256
EPS = 1e-5
ALPHA = 2.0 ** 0.25
LAM_INIT = 0.8 - 0.6 * math.exp(0.0)
NEG = -1e30
GELU_A, GELU_B = 0.044715, math.sqrt(2.0 / math.pi)


class Chain:

    def __init__(self, eng, sem):
        self.eng, self.sem, self.n = eng, sem, 0

    def add(self, ins):
        ins.then_inc(self.sem, 1)
        self.n += 1

    def sync(self):
        self.eng.wait_ge(self.sem, self.n)

    def restart(self):
        self.sync()
        self.eng.sem_clear(self.sem)
        self.n = 0


def rows(dram, start, n):
    return dram[bass.ds(start, n), :]


def program(nc, a, o, upto=99):
    top = ExitStack()

    def maker(ctx):
        def sb(name, shape, dt=F32):
            return ctx.enter_context(nc.sbuf_tensor(name, shape, dt))

        def ps(name, shape=(P, 512)):
            return ctx.enter_context(nc.psum_tensor(name, list(shape), F32))

        sems = []

        def sem(name):
            sems.append(nc.alloc_semaphore(name=name))
            return sems[-1]

        def give_back():
            if sems:
                nc.clear_and_free_semaphores(sems)
                nc.all_engine_barrier()

        ctx.callback(give_back)
        return sb, ps, sem

    with top:
        sb, _, _ = maker(top)
        ident = sb("ident", [P, P])
        nlam = sb("nlam", [P, 1])
        g_row = sb("g_row", [P, VD])
        causal = sb("causal", [P, P])
        smask = sb("smask", [SR, DS])
        cbase = sb("cbase", [SR, H * DS])
        hmask = sb("hmask", [H * DS, H])
        rgp = sb("rgp", [P, 8 * RC])
        hba = sb("hba", [P, 2, RC])
        sp4 = sb("sp4", [P, 2, RC])
        rope = sb("rope", [P, NT + 1, 2, HALF])
        qTs = sb("qTs", [P, H, SR])
        kTs = sb("kTs", [P, H, SR])
        mixS = sb("mixS", [P, KC, SR])
        x1_d = nc.dram_tensor("x1_scratch", (SEQ + P, D), F32, kind="Internal").ap()
        ffn_d = nc.dram_tensor("ffn_scratch", (SEQ + SR, D), F32, kind="Internal").ap()

        constants(nc, a, maker, ident, nlam, g_row, causal, smask, cbase, hmask, rgp, hba, sp4, rope, x1_d)
        with ExitStack() as c1:
            sb1, _, _ = maker(c1)
            mixR = sb1("mixR", [P, RC, SEQ])
            kT = sb1("kT", [P, H, SEQ])
            qT = sb1("qT", [P, H, SEQ])
            v_all = sb1("v_all", [P, NT, AW])
            projection(nc, a, o, maker, ident, rgp, hba, sp4, rope, qTs, kTs, mixS, mixR, kT, qT, v_all)
            if upto > 2:
                mixA = sb1("mixA", [P, H, SEQ])
                prompt_attention(nc, maker, ident, nlam, g_row, causal, kT, qT, v_all, mixA)
                if upto > 3:
                    prompt_mix(nc, a, maker, mixA, mixR, x1_d)
        if upto > 4:
            peer(nc, a, o, maker, ident, cbase, smask, hmask, g_row, qTs, kTs, mixS, x1_d, ffn_d, upto)
        if upto > 7:
            output(nc, a, o, maker, ident, x1_d, ffn_d)


def constants(nc, a, maker, ident, nlam, g_row, causal, smask, cbase, hmask, rgp, hba, sp4, rope, x1_d):
    with ExitStack() as ctx:
        sb, ps, sem = maker(ctx)
        lq = sb("lq", [P, 4, QK])
        raw = sb("raw", [8 * RC, P])
        smT = sb("smT", [DS, SR])
        w = sb("w", [P, 12, RC])
        e = sb("e", [P, 4])
        zero = sb("zero", [P, D])
        bank = ps("c_bank")
        bank2 = ps("c_bank2")
        s_ld = sem("s_ld")
        s_rope = sem("s_rope")
        s_pool = sem("s_pool")
        s_ch = sem("s_ch")
        s_pe = sem("s_pe")
        s_act = sem("s_act")
        s_dve = sem("s_dve")
        s_pad = sem("s_pad")
        with nc.Block() as block:
            @block.sync
            def _(sp):
                for n, name in enumerate(("lambda_q1", "lambda_k1", "lambda_q2", "lambda_k2")):
                    sp.dma_start(lq[:, n, :], a[name].to_broadcast([P, QK])).then_inc(s_ld, 16)
                sp.dma_start(g_row[:], a["subln_g"].to_broadcast([P, VD])).then_inc(s_ld, 16)
                sp.dma_start(raw[0:CW * RC, :], a["conv_w"].rearrange("j (c p) -> (j c) p", p=P)).then_inc(s_ld, 16)
                for n, name in enumerate(("conv_b", "rg_ba", "rg_bx", "rg_lambda")):
                    sp.dma_start(raw[(CW + n) * RC:(CW + n + 1) * RC, :],
                                 a[name].rearrange("o (c p) -> (o c) p", p=P)).then_inc(s_ld, 16)
                table = a["rope"]
                sp.dma_start(rope[:, 0:NT, :, :], table[0:SEQ].rearrange("(t p) a c -> p t a c", p=P)).then_inc(s_rope, 16)
                sp.dma_start(rope[0:SR, NT, :, :], table[SEQ:SEQ + SR]).then_inc(s_rope, 16)
                sp.wait_ge(s_rope, 32)
                sp.wait_ge(s_pool, 7)
                sp.dma_start(x1_d[SEQ:SEQ + P, :], zero[:]).then_inc(s_pad, 16)
                sp.wait_ge(s_pad, 16)

            @block.gpsimd
            def _(pool):
                pool.memset(ident[:], 0.0).then_inc(s_pool, 1)
                pool.memset(causal[:], 0.0).then_inc(s_pool, 1)
                pool.memset(smT[:], 0.0).then_inc(s_pool, 1)
                pool.memset(hmask[:], 1.0).then_inc(s_pool, 1)
                pool.wait_ge(s_pool, 4)
                pool.affine_select(out=ident[:], in_=ident[:], compare_op=ALU.not_equal, fill=1.0, base=0,
                                   pattern=[[-1, P]], channel_multiplier=1).then_inc(s_pool, 1)
                pool.affine_select(out=causal[:], in_=causal[:], compare_op=ALU.is_ge, fill=NEG, base=0,
                                   pattern=[[-1, P]], channel_multiplier=1)
                pool.affine_select(out=smT[:], in_=smT[:], compare_op=ALU.is_ge, fill=NEG, base=0,
                                   pattern=[[0, 2 * H], [1, DS]], channel_multiplier=-1)
                pool.affine_select(out=hmask[:], in_=hmask[:], compare_op=ALU.is_ge, fill=0.0, base=0,
                                   pattern=[[-DS, H]], channel_multiplier=1).then_inc(s_pool, 1)
                pool.memset(zero[:], 0.0).then_inc(s_pool, 1)
                pool.wait_ge(s_pool, 7)
                pool.affine_select(out=hmask[:], in_=hmask[:], compare_op=ALU.is_ge, fill=0.0, base=DS - 1,
                                   pattern=[[DS, H]], channel_multiplier=-1).then_inc(s_pool, 1)

            @block.tensor
            def _(pe):
                pe.wait_ge(s_pool, 8)
                pe.wait_ge(s_ld, 160)
                pe.transpose(bank[:, 0:8 * RC], raw[:], ident[0:8 * RC, 0:8 * RC]).then_inc(s_pe, 1)
                pe.transpose(bank2[0:SR, 0:DS], smT[:], ident[0:DS, 0:DS]).then_inc(s_pe, 1)

            @block.scalar
            def _(act):
                act.wait_ge(s_dve, 1)
                act.activation(e[:, 2:4], e[:, 0:2], ACT.Exp).then_inc(s_act, 1)
                act.wait_ge(s_dve, 2)
                act.activation(w[:, 1, :], w[:, 0, :], ACT.Exp).then_inc(s_act, 1)
                act.wait_ge(s_dve, 3)
                act.activation(w[:, 3, :], w[:, 2, :], ACT.Ln).then_inc(s_act, 1)

            @block.vector
            def _(dve):
                ch = Chain(dve, s_ch)
                dve.wait_ge(s_ld, 160)
                for n in range(2):
                    last = dve.tensor_tensor_reduce(lq[:, 2 * n, :], lq[:, 2 * n, :], lq[:, 2 * n + 1, :],
                                                    1.0, 0.0, ALU.mult, ALU.add, e[:, n:n + 1])
                last.then_inc(s_dve, 1)
                ch.add(dve.tensor_scalar(g_row[:], g_row[:], 1.0 - LAM_INIT, None, ALU.mult))
                dve.wait_ge(s_pe, 2)
                ch.add(dve.tensor_copy(rgp[:], bank[:, 0:8 * RC]))
                ch.add(dve.tensor_copy(smask[:], bank2[0:SR, 0:DS]))
                ch.sync()
                dve.tensor_scalar(hba[:, 0, :], rgp[:, 5 * RC:6 * RC], 0.5, None, ALU.mult)
                dve.tensor_scalar(hba[:, 1, :], rgp[:, 6 * RC:7 * RC], 0.5, None, ALU.mult)
                lam = rgp[:, 7 * RC:8 * RC]
                ch.add(dve.tensor_scalar(w[:, 4, :], lam, -1.0, None, ALU.mult))
                ch.sync()
                dve.tensor_scalar(w[:, 5, :], w[:, 4, :], 0.0, None, ALU.max)
                dve.tensor_tensor(w[:, 0, :], lam, w[:, 4, :], ALU.min).then_inc(s_dve, 1)
                dve.wait_ge(s_act, 2)
                dve.tensor_scalar(w[:, 2, :], w[:, 1, :], 1.0, None, ALU.add).then_inc(s_dve, 1)
                dve.wait_ge(s_act, 3)
                ch.add(dve.tensor_scalar(w[:, 6, :], w[:, 2, :], 1.0, None, ALU.subtract))
                ch.add(dve.tensor_tensor(w[:, 7, :], w[:, 3, :], w[:, 1, :], ALU.mult))
                ch.sync()
                ch.add(dve.tensor_scalar(w[:, 8, :], w[:, 6, :], 0.0, None, ALU.is_equal))
                ch.sync()
                ch.add(dve.tensor_tensor(w[:, 6, :], w[:, 6, :], w[:, 8, :], ALU.add))
                ch.add(dve.tensor_tensor(w[:, 9, :], w[:, 8, :], w[:, 1, :], ALU.mult))
                ch.sync()
                ch.add(dve.reciprocal(w[:, 10, :], w[:, 6, :]))
                ch.sync()
                ch.add(dve.tensor_tensor(w[:, 7, :], w[:, 7, :], w[:, 10, :], ALU.mult))
                ch.sync()
                ch.add(dve.tensor_tensor(w[:, 7, :], w[:, 7, :], w[:, 9, :], ALU.add))
                ch.sync()
                ch.add(dve.tensor_tensor(w[:, 7, :], w[:, 7, :], w[:, 5, :], ALU.add))
                ch.sync()
                dve.tensor_scalar(sp4[:, 0, :], w[:, 7, :], 4.0, None, ALU.mult)
                dve.tensor_scalar(sp4[:, 1, :], w[:, 7, :], -4.0, None, ALU.mult)
                ch.add(dve.tensor_tensor(nlam[:], e[:, 3:4], e[:, 2:3], ALU.subtract))
                ch.sync()
                ch.add(dve.tensor_scalar(nlam[:], nlam[:], LAM_INIT, None, ALU.subtract))
                ch.sync()
                i4 = ident[0:SR, 0:SR].rearrange("p (h m q) -> p h m q", h=H, m=2)
                dve.scalar_tensor_tensor(out=cbase[:].rearrange("p (h q) -> p h q", h=H), in0=i4[:, :, 1, :],
                                         scalar=nlam[0:SR, :], in1=i4[:, :, 0, :], op0=ALU.mult, op1=ALU.add)


def projection(nc, a, o, maker, ident, rgp, hba, sp4, rope, qTs, kTs, mixS, mixR, kT, qT, v_all):
    with ExitStack() as ctx:
        sb, ps, sem = maker(ctx)
        w_in = sb("w_in", [P, KC, IN])
        wab = sb("wab", [P, 2, RC, P])
        xrow = sb("xrow", [P, D])
        xT = sb("xT", [P, KC, P])
        qk = sb("qk", [P, 2 * AW])
        rt = sb("rt", [P, 4, 16, HALF])
        xrb = sb("xrb", [P, RC, 1, CW - 1 + P])
        xrs = sb("xrs", [P, RC, DB, CW - 1 + DS])
        gate = sb("gate", [P, RC, P])
        xc = sb("xc", [P, RC, P])
        thr = sb("thr", [P, RC, P])
        thi = sb("thi", [P, RC, P])
        tu = sb("tu", [P, RC, P])
        gin = sb("gin", [P, RC, P])
        dec = sb("dec", [P, RC, 1, 1 + P])
        inp = sb("inp", [P, RC, 1, 1 + P])
        hb = sb("hb", [P, RC, 1, 1 + P])
        decs = sb("decs", [P, RC, DB, 1 + DS])
        inps = sb("inps", [P, RC, DB, 1 + DS])
        hbs = sb("hbs", [P, RC, DB, 1 + DS])
        tail = sb("tail", [DB * (CW - 1), 4, RW])
        tail_v = sb("tail_v", [SR, AW])
        cst = sb("cst", [P, RC, DB * (CW - 1)])
        hst = sb("hst", [P, RC, DB])
        B = [ps(f"p_bank{n}") for n in range(8)]
        s_w = [sem(f"s_w{n}") for n in range(KC)]
        s_rg = sem("s_rg")
        s_zero = sem("s_zero")
        s_st = sem("s_st")
        names = ("x", "xps", "xTa", "xTd", "gate", "xr", "q", "k", "v", "xrev", "gev", "kev", "vev", "rope",
                 "qTp", "kTp", "qTev", "kTev", "xc", "carry", "r", "i", "thr", "thi", "tu", "in", "tg", "s2",
                 "sq", "y", "kout", "vout", "stT", "stc", "hT", "hc", "tout", "gdone", "dch", "ach", "tick")
        s = {n: sem("s_p_" + n) for n in names}
        GATE, XR, Rb, Ib = B[4], B[3], B[7], B[3]
        t4 = lambda x, R: x[:].rearrange("p (c t) -> p c t", c=RC)[:, :, 0:R]
        xrow_d = (a["x_prompt"], a["x_sample"])

        with nc.Block() as block:
            @block.sync
            def _(sp):
                sp.dma_start(xrow[:], rows(xrow_d[0], 0, P)).then_inc(s["x"], 16)
                win = a["w_in"].rearrange("(k p) n -> p k n", p=P)
                for k in range(KC):
                    sp.dma_start(w_in[:, k, :], win[:, k, :]).then_inc(s_w[k], 16)
                sp.wait_ge(s_zero, 2)
                for m, name in enumerate(("rg_wa", "rg_wx")):
                    src = a[name].rearrange("(c two) i j -> two i c j", two=2)
                    for h in range(2):
                        sp.dma_start(wab[64 * h:64 * h + 64, m, :, 64 * h:64 * h + 64], src[h]).then_inc(s_rg, 16)
                sp.dma_start(tail[:, 0, :], a["state_conv"]).then_inc(s_st, 16)
                sp.dma_start(tail[0:DB, 1, :], a["state_h"]).then_inc(s_st, 16)

                def out_tile(t, R, kd, vd, v_src, at):
                    sp.wait_ge(s["rope"], t + 1)
                    sp.dma_start(rows(kd, at, R), qk[0:R, AW:2 * AW]).then_inc(s["kout"], 16)
                    sp.wait_ge(s["vev"], t + 1)
                    sp.dma_start(rows(vd, at, R), v_src).then_inc(s["vout"], 16)

                def prompt_tile(t):
                    sp.wait_ge(s["xps"], 2 * t + 2)
                    sp.dma_start(xrow[:], rows(xrow_d[0], t * P + P, P)).then_inc(s["x"], 16)
                    out_tile(t, P, o["k_prompt"], o["v_prompt"], v_all[:, bass.ds(t, 1), :], t * P)

                with sp.Fori(0, NT - 1) as t:
                    prompt_tile(t)
                sp.wait_ge(s["xps"], 2 * NT)
                sp.dma_start(xrow[0:SR, :], xrow_d[1]).then_inc(s["x"], 16)
                out_tile(NT - 1, P, o["k_prompt"], o["v_prompt"], v_all[:, NT - 1:NT, :], (NT - 1) * P)
                out_tile(NT, SR, o["k_sample"], o["v_sample"], tail_v[:], 0)
                sp.wait_ge(s["hc"], 2)
                sp.dma_start(o["conv_prompt"], tail[0:CW - 1, 2, :]).then_inc(s["tout"], 16)
                sp.dma_start(o["h_prompt"], tail[0:1, 3, :]).then_inc(s["tout"], 16)
                sp.wait_ge(s["tout"], 32)
                sp.sem_inc(s["gdone"], 1)
                sp.wait_ge(s["hc"], 4)
                sp.dma_start(o["conv_sample"], tail[:, 2, :]).then_inc(s["tout"], 16)
                sp.dma_start(o["h_sample"], tail[0:DB, 3, :]).then_inc(s["tout"], 16)
                sp.wait_ge(s["tout"], 64)
                sp.wait_ge(s["kout"], 16 * (NT + 1))
                sp.wait_ge(s["vout"], 16 * (NT + 1))

            @block.gpsimd
            def _(pool):
                pool.memset(wab[:], 0.0).then_inc(s_zero, 1)
                pool.memset(xrb[:], 0.0)
                pool.memset(dec[:], 0.0)
                pool.memset(decs[:], 0.0)
                pool.memset(hb[:], 0.0).then_inc(s_zero, 1)

            @block.tensor
            def _(pe):
                def turn_x(t, R):
                    pe.wait_ge(s["qTev"], t)
                    pe.wait_ge(s["kTev"], t)
                    pe.wait_ge(s["x"], 16 * t + 16)
                    for half in range(2):
                        for c in range(4):
                            k = 4 * half + c
                            last = pe.transpose(B[5 + half][:, c * P:c * P + R], xrow[0:R, k * P:k * P + P],
                                                ident[0:R, 0:R])
                        last.then_inc(s["xps"], 1)

                def rg_gates(t, R):
                    pe.wait_ge(s["thr"], t)
                    pe.wait_ge(s["thi"], t)
                    pe.wait_ge(s["xrev"], t + 1)
                    pe.wait_ge(s["xc"], t + 1)
                    for m, (bank, done) in enumerate(((Rb, "r"), (Ib, "i"))):
                        for c in range(RC):
                            last = pe.matmul(bank[:, c * P:c * P + R], wab[:, m, c, :], xc[:, c, 0:R],
                                             start=True, stop=True)
                        last.then_inc(s[done], 1)

                def channel_major(t, R, bank, col, done):
                    for c in range(RC):
                        for k in range(KC):
                            last = pe.matmul(bank[:, c * P:c * P + R], w_in[:, k, col + c * P:col + c * P + P],
                                             xT[:, k, 0:R], start=(k == 0), stop=(k == KC - 1))
                    last.then_inc(s[done], 1)

                def token_major(R, bank, col, done):
                    for k in range(KC):
                        last = pe.matmul(bank[0:R, :], xT[:, k, 0:R], w_in[:, k, col:col + AW],
                                         start=(k == 0), stop=(k == KC - 1))
                    last.then_inc(s[done], 1)

                def tile(t, R, before):
                    turn_x(t, R)
                    if before:
                        rg_gates(t - 1, P)
                    pe.wait_ge(s["xTa"], t + 1)
                    pe.wait_ge(s["xTd"], t + 1)
                    if not before:
                        for k in range(KC):
                            pe.wait_ge(s_w[k], 16)
                    pe.wait_ge(s["gev"], t)
                    channel_major(t, R, GATE, 3 * AW + RW, "gate")
                    pe.wait_ge(s["thi"], t)
                    channel_major(t, R, XR, 3 * AW, "xr")
                    pe.wait_ge(s["kev"], t)
                    token_major(R, B[0], 0, "q")
                    token_major(R, B[1], AW, "k")
                    pe.wait_ge(s["vev"], t)
                    token_major(R, B[2], 2 * AW, "v")
                    pe.wait_ge(s["rope"], t + 1)
                    for bank, at, done in ((B[5], 0, "qTp"), (B[6], AW, "kTp")):
                        for h in range(H):
                            last = pe.transpose(bank[:, h * P:h * P + R], qk[0:R, at + h * P:at + h * P + P],
                                                ident[0:R, 0:R])
                        last.then_inc(s[done], 1)

                def states_out(src_x, src_h, G, n):
                    L = src_x.shape[3] - (CW - 1)
                    pe.wait_ge(s["y"], NT + n)
                    if n:
                        pe.wait_ge(s["hc"], 2)
                    for c in range(RC):
                        last = pe.transpose(B[0][0:G * (CW - 1), c * P:c * P + P], cst[:, c, 0:G * (CW - 1)],
                                            ident[:])
                    last.then_inc(s["hT"], 1)
                    for c in range(RC):
                        last = pe.transpose(B[1][0:G, c * P:c * P + P], hst[:, c, 0:G], ident[:])
                    last.then_inc(s["hT"], 1)

                pe.wait_ge(s_zero, 2)
                tile(0, P, False)
                pe.wait_ge(s_rg, 64)
                with pe.Fori(1, NT) as t:
                    tile(t, P, True)
                pe.wait_ge(s_st, 32)
                pe.wait_ge(s["thr"], NT - 1)
                for c in range(RC):
                    pe.transpose(Rb[:, c * 32:c * 32 + DB * (CW - 1)], tail[:, 0, c * P:c * P + P],
                                 ident[0:DB * (CW - 1), 0:DB * (CW - 1)])
                    last = pe.transpose(Rb[:, 256 + c * DB:256 + c * DB + DB], tail[0:DB, 1, c * P:c * P + P],
                                        ident[0:DB, 0:DB])
                last.then_inc(s["stT"], 1)
                pe.wait_ge(s["stc"], 1)
                tile(NT, SR, True)
                rg_gates(NT, SR)
                pe.wait_ge(s["stc"], 2)
                states_out(xrb, hb, 1, 0)
                pe.wait_ge(s["stc"], 3)
                states_out(xrs, hbs, DB, 1)

            @block.scalar
            def _(act):
                ch = Chain(act, s["ach"])

                def x_turned(t, R):
                    act.wait_ge(s["v"], t)
                    act.wait_ge(s["xps"], 2 * t + 1)
                    act.activation(xT[:, 0:4, 0:R], t4(B[5], R), ACT.Copy).then_inc(s["xTa"], 1)

                def rg_tail(t, R, L, dec_t):
                    G = R // L
                    act.wait_ge(s["r"], t + 1)
                    act.wait_ge(s["y"], t)
                    for c in range(RC):
                        last = act.activation(thr[:, c, 0:R], Rb[:, c * P:c * P + R], ACT.Tanh,
                                              bias=hba[:, 0, c:c + 1], scale=0.5)
                    last.then_inc(s["thr"], 1)
                    act.wait_ge(s["i"], t + 1)
                    for c in range(RC):
                        last = act.activation(thi[:, c, 0:R], Ib[:, c * P:c * P + R], ACT.Tanh,
                                              bias=hba[:, 1, c:c + 1], scale=0.5)
                    last.then_inc(s["thi"], 1)
                    act.wait_ge(s["thr"], t + 1)
                    for c in range(RC):
                        act.activation(tu[:, c, 0:R], thr[:, c, 0:R], ACT.Tanh,
                                       bias=sp4[:, 0, c:c + 1], scale=sp4[:, 0, c:c + 1])
                        last = act.activation(dec_t[:, c, :, 1:], thr[:, c, 0:R].rearrange("p (g l) -> p g l", g=G),
                                              ACT.Exp, bias=sp4[:, 1, c:c + 1], scale=sp4[:, 1, c:c + 1])
                    last.then_inc(s["tu"], 1)
                    act.wait_ge(s["in"], t + 1)
                    act.activation(gin[:, :, 0:R], gin[:, :, 0:R], ACT.Tanh, scale=GELU_B).then_inc(s["tg"], 1)
                    act.wait_ge(s["s2"], t + 1)
                    act.activation(tu[:, :, 0:R], tu[:, :, 0:R], ACT.Sqrt).then_inc(s["sq"], 1)

                def evacuate(t, R, L, xr_t, v_dst, q_dst, k_dst):
                    act.wait_ge(s["carry"], t)
                    act.wait_ge(s["xr"], t + 1)
                    src = XR[:].rearrange("p (c t) -> p c t", c=RC)[:, :, 0:R].rearrange("p c (g l) -> p c g l", l=L)
                    act.activation(xr_t[:, :, :, CW - 1:], src, ACT.Copy).then_inc(s["xrev"], 1)
                    act.wait_ge(s["y"], t)
                    act.wait_ge(s["gate"], t + 1)
                    act.activation(gate[:, :, 0:R], t4(GATE, R), ACT.Copy).then_inc(s["gev"], 1)
                    act.wait_ge(s["qTp"], t)
                    act.wait_ge(s["kTp"], t)
                    act.wait_ge(s["kout"], 16 * t)
                    act.wait_ge(s["k"], t + 1)
                    act.activation(qk[0:R, 0:AW], B[0][0:R, :], ACT.Copy)
                    act.activation(qk[0:R, AW:2 * AW], B[1][0:R, :], ACT.Copy).then_inc(s["kev"], 1)
                    act.wait_ge(s["v"], t + 1)
                    act.sem_inc(s["tick"], 1)
                    act.activation(v_dst, B[2][0:R, :], ACT.Copy).then_inc(s["vev"], 1)
                    act.wait_ge(s["qTp"], t + 1)
                    act.sem_inc(s["tick"], 1)
                    act.activation(q_dst, t4(B[5], R), ACT.Copy).then_inc(s["qTev"], 1)
                    act.wait_ge(s["kTp"], t + 1)
                    act.sem_inc(s["tick"], 1)
                    act.activation(k_dst, t4(B[6], R), ACT.Copy).then_inc(s["kTev"], 1)

                def prompt_evacuate(t):
                    evacuate(t, P, P, xrb, v_all[:, bass.ds(t, 1), :].rearrange("p o n -> p (o n)"),
                             qT[:, :, bass.ds(t * P, P)], kT[:, :, bass.ds(t * P, P)])

                act.wait_ge(s_zero, 2)
                x_turned(0, P)
                prompt_evacuate(0)
                with act.Fori(1, NT) as t:
                    x_turned(t, P)
                    rg_tail(t - 1, P, P, dec)
                    prompt_evacuate(t)
                x_turned(NT, SR)
                rg_tail(NT - 1, P, P, dec)
                evacuate(NT, SR, DS, xrs, tail_v[:], qTs[:], kTs[:])
                rg_tail(NT, SR, DS, decs)
                for n, G in enumerate((1, DB)):
                    act.wait_ge(s["hT"], 2 * n + 2)
                    if n:
                        act.wait_ge(s["gdone"], 1)
                    act.activation(tail[0:G * (CW - 1), 2, :], B[0][0:G * (CW - 1), :], ACT.Copy).then_inc(s["hc"], 1)
                    act.activation(tail[0:G, 3, :], B[1][0:G, :], ACT.Copy).then_inc(s["hc"], 1)

            @block.vector
            def _(dve):
                ch = Chain(dve, s["dch"])
                tap = lambda j, c: rgp[:, j * RC + c:j * RC + c + 1]

                def x_turned(t, R):
                    dve.wait_ge(s["v"], t)
                    dve.wait_ge(s["xps"], 2 * t + 2)
                    dve.tensor_copy(xT[:, 4:8, 0:R], t4(B[6], R)).then_inc(s["xTd"], 1)

                def rg_tail(t, R, L, dec_t, inp_t, hb_t, y_dst):
                    G = R // L
                    v = lambda x: x[:, :, 0:R]
                    g3 = lambda x, c: x[:, c, 0:R].rearrange("p (g l) -> p g l", g=G)
                    ch.sync()
                    dve.wait_ge(s["tu"], t + 1)
                    ch.add(dve.tensor_scalar(v(thr), v(tu), 1.0, None, ALU.add))
                    ch.add(dve.scalar_tensor_tensor(out=v(xc), in0=v(thi), scalar=1.0, in1=v(xc),
                                                    op0=ALU.add, op1=ALU.mult))
                    ch.sync()
                    ch.add(dve.reciprocal(v(thr), v(thr)))
                    ch.sync()
                    dve.scalar_tensor_tensor(out=v(tu), in0=v(tu), scalar=2.0, in1=v(thr),
                                             op0=ALU.mult, op1=ALU.mult).then_inc(s["s2"], 1)
                    dve.wait_ge(s["tg"], t + 1)
                    ch.add(dve.scalar_tensor_tensor(out=v(gate), in0=v(gin), scalar=1.0, in1=v(gate),
                                                    op0=ALU.add, op1=ALU.mult))
                    dve.wait_ge(s["sq"], t + 1)
                    for c in range(RC):
                        ch.add(dve.scalar_tensor_tensor(out=inp_t[:, c, :, 1:], in0=g3(xc, c), scalar=0.5,
                                                        in1=g3(tu, c), op0=ALU.mult, op1=ALU.mult))
                    ch.sync()
                    flat = lambda x: x[:].rearrange("p c g l -> p (c g l)")
                    ch.add(dve.tensor_tensor_scan(flat(hb_t), flat(dec_t), flat(inp_t), 0.0, ALU.mult, ALU.add))
                    ch.sync()
                    ch.add(dve.tensor_copy(inp_t[:, :, :, 0:1], hb_t[:, :, :, L:L + 1]))
                    for c in range(RC):
                        last = dve.scalar_tensor_tensor(out=y_dst(c), in0=hb_t[:, c, :, 1:], scalar=0.5,
                                                        in1=g3(gate, c), op0=ALU.mult, op1=ALU.mult)
                    last.then_inc(s["y"], 1)

                def conv(t, R, L, xr_t, carry):
                    G = R // L
                    g3 = lambda c: xc[:, c, 0:R].rearrange("p (g l) -> p g l", g=G)
                    dve.wait_ge(s["i"], t)
                    dve.wait_ge(s["xrev"], t + 1)
                    for c in range(RC):
                        ch.add(dve.tensor_scalar(g3(c), xr_t[:, c, :, 3:3 + L], tap(3, c), tap(4, c),
                                                 ALU.mult, ALU.add))
                    for j in range(CW - 1):
                        ch.sync()
                        for c in range(RC):
                            last = dve.scalar_tensor_tensor(out=g3(c), in0=xr_t[:, c, :, j:j + L], scalar=tap(j, c),
                                                            in1=g3(c), op0=ALU.mult, op1=ALU.add)
                            if (j, c) == (CW - 2, RC - 1):
                                last.then_inc(s["xc"], 1)
                            else:
                                ch.add(last)
                    dve.wait_ge(s["xc"], t + 1)
                    if carry:
                        dve.tensor_copy(xr_t[:, :, :, 0:CW - 1], xr_t[:, :, :, L:L + CW - 1]).then_inc(s["carry"], 1)

                def gelu_in(t, R):
                    v = lambda x: x[:, :, 0:R]
                    dve.wait_ge(s["gev"], t + 1)
                    ch.add(dve.tensor_tensor(v(gin), v(gate), v(gate), ALU.mult))
                    ch.sync()
                    ch.add(dve.tensor_scalar(v(gin), v(gin), GELU_A, 1.0, ALU.mult, ALU.add))
                    ch.sync()
                    dve.tensor_tensor(v(gin), v(gin), v(gate), ALU.mult).then_inc(s["in"], 1)

                def rotate(t, R):
                    x = qk[0:R, :].rearrange("p (g d) -> p g d", d=QK)
                    lo, hi = x[:, :, 0:HALF], x[:, :, HALF:ROT]
                    shape = [R, 16, HALF]
                    angle = lambda n: rope[0:R, bass.ds(t, 1), n, :].to_broadcast(shape)
                    cos, sin = angle(0), angle(1)
                    dve.wait_ge(s["kev"], t + 1)
                    for n, (half, f) in enumerate(((lo, cos), (hi, sin), (hi, cos), (lo, sin))):
                        ch.add(dve.tensor_tensor(rt[0:R, n], half, f, ALU.mult))
                    ch.sync()
                    ch.add(dve.tensor_tensor(lo, rt[0:R, 0], rt[0:R, 1], ALU.subtract))
                    dve.tensor_tensor(hi, rt[0:R, 2], rt[0:R, 3], ALU.add).then_inc(s["rope"], 1)

                def prompt_y(t):
                    return lambda c: mixR[:, c, bass.ds(t * P, P)].rearrange("p (g l) -> p g l", g=1)

                dve.wait_ge(s_zero, 2)
                ch.add(dve.memset(inp[:, :, :, 0:1], 0.0))
                x_turned(0, P)
                conv(0, P, P, xrb, True)
                gelu_in(0, P)
                rotate(0, P)
                ch.restart()
                with dve.Fori(1, NT) as t:
                    x_turned(t, P)
                    rg_tail(t - 1, P, P, dec, inp, hb, prompt_y(t - 1))
                    conv(t, P, P, xrb, True)
                    gelu_in(t, P)
                    rotate(t, P)
                    ch.restart()
                dve.wait_ge(s["stT"], 1)
                for c in range(RC):
                    ch.add(dve.tensor_copy(xrs[:, c, :, 0:CW - 1], Rb[:, c * 32:c * 32 + DB * (CW - 1)]
                                           .rearrange("p (g j) -> p g j", g=DB)))
                last = dve.tensor_copy(inps[:, :, :, 0:1].rearrange("p c g o -> p c (g o)"),
                                       Rb[:, 256:256 + RC * DB].rearrange("p (c g) -> p c g", c=RC))
                last.then_inc(s["stc"], 1)
                x_turned(NT, SR)
                rg_tail(NT - 1, P, P, dec, inp, hb, prompt_y(NT - 1))
                conv(NT, SR, DS, xrs, False)
                gelu_in(NT, SR)
                rotate(NT, SR)
                ch.sync()
                dve.wait_ge(s["y"], NT)
                ch.add(dve.tensor_copy(cst[:, :, 0:CW - 1], xrb[:, :, 0, 0:CW - 1]))
                dve.tensor_copy(hst[:, :, 0:1], hb[:, :, 0, P:P + 1]).then_inc(s["stc"], 1)
                rg_tail(NT, SR, DS, decs, inps, hbs,
                        lambda c: mixS[:, RC + c, :].rearrange("p (g l) -> p g l", g=DB))
                dve.wait_ge(s["hT"], 2)
                for c in range(RC):
                    ch.add(dve.tensor_copy(cst[:, c, :].rearrange("p (g j) -> p g j", g=DB),
                                           xrs[:, c, :, DS:DS + CW - 1]))
                dve.tensor_copy(hst[:], hbs[:, :, :, DS:DS + 1].rearrange("p c g o -> p c (g o)")).then_inc(s["stc"], 1)


def prompt_attention(nc, maker, ident, nlam, g_row, causal, kT, qT, v_all, mixA):
    with ExitStack() as ctx:
        sb, ps, sem = maker(ctx)
        qz = sb("qz", [P, 2, SEQ])
        kh = sb("kh", [P, SEQ])
        vh = sb("vh", [P, NT, VD])
        pm = [sb(f"pm{n}", [P, 2, SEQ]) for n in range(2)]
        w = [sb(f"w{n}", [P, SEQ]) for n in range(2)]
        wT = [sb(f"wT{n}", [P, NT, P]) for n in range(2)]
        oh = sb("oh", [P, NT, VD])
        sq = sb("sq", [P, NT, VD])
        mx = sb("mx", [P, NT, 2])
        nb = sb("nb", [P, NT, 2])
        z = sb("z", [P, NT, 2])
        rz = sb("rz", [P, NT, 2])
        ss = sb("ss", [P, 3, NT])
        S = [ps(f"a_s{m}", (P, 2 * 512)) for m in range(2)]
        TB = [ps(f"a_t{n}") for n in range(2)]
        OB = [ps(f"a_o{n}") for n in range(2)]
        names = ("zero", "qh", "kh", "s", "nb", "exp", "w", "t", "te", "o", "oe", "ss", "sd", "on", "ot", "ote",
                 "ch", "tick")
        s = {n: sem("s_a_" + n) for n in names}
        groups = [i + 1 if i < 4 else 2 * i - 2 for i in range(NT)]
        NG = groups[-1]

        def blocks(i):
            return [range(0, min(i + 1, 4))] + ([range(4, i + 1)] if i >= 4 else [])

        with nc.Block() as block:
            @block.gpsimd
            def _(pool):
                pool.memset(qz[:], 0.0).then_inc(s["zero"], 1)
                with pool.Fori(0, H) as hd:
                    pool.wait_ge(s["o"], hd * NT)
                    pool.sem_inc(s["tick"], 1)
                    pool.tensor_copy(kh[:], kT[:, bass.ds(hd, 1), :].rearrange("p o n -> p (o n)"))
                    pool.tensor_copy(vh[:], v_all[:, :, bass.ds(hd * VD, VD)]).then_inc(s["kh"], 1)

            @block.tensor
            def _(pe):
                with pe.Fori(0, H) as hd:
                    pe.wait_ge(s["qh"], hd + 1)
                    pe.wait_ge(s["kh"], hd + 1)
                    for i in range(NT + 2):
                        if i < NT:
                            for m in range(2):
                                pe.wait_ge(s["exp"], hd * 2 * NT + (2 * i - 1 + m if i else 0))
                                for c in range(0, (i + 1) * P, 512):
                                    n = min(512, (i + 1) * P - c)
                                    last = pe.matmul(S[m][:, c:c + n], qz[:, m, i * P:i * P + P], kh[:, c:c + n],
                                                     start=True, stop=True)
                                last.then_inc(s["s"], 1)
                        if 1 <= i <= NT:
                            pe.wait_ge(s["w"], hd * NT + i)
                            for g, js in enumerate(blocks(i - 1)):
                                pe.wait_ge(s["te"], hd * NG + (groups[i - 2] if i > 1 else 0))
                                for j in js:
                                    last = pe.transpose(TB[g][:, (j - 4 * g) * P:(j - 4 * g) * P + P],
                                                        w[(i - 1) % 2][:, j * P:j * P + P], ident[:])
                                last.then_inc(s["t"], 1)
                        if i >= 2:
                            k = i - 2
                            pe.wait_ge(s["te"], hd * NG + groups[k])
                            pe.wait_ge(s["oe"], hd * NT + (k - 1 if k > 1 else 0))
                            for j in range(k + 1):
                                last = pe.matmul(OB[k % 2][:, 0:VD], wT[k % 2][:, j, :], vh[:, j, :],
                                                 start=(j == 0), stop=(j == k))
                            last.then_inc(s["o"], 1)
                    pe.wait_ge(s["on"], hd + 1)
                    for g in range(2):
                        for j in range(4):
                            last = pe.transpose(TB[g][:, j * P:j * P + P], oh[:, 4 * g + j, :], ident[:])
                        last.then_inc(s["ot"], 1)
                    pe.wait_ge(s["ote"], 2 * hd + 2)

            @block.scalar
            def _(act):
                act.wait_ge(s["zero"], 1)
                with act.Fori(0, H) as hd:
                    act.wait_ge(s["s"], hd * 2 * NT)
                    act.sem_inc(s["tick"], 1)
                    for m in range(2):
                        half = slice(QK * m, QK * m + QK)
                        last = act.activation(qz[half, m, :], qT[half, bass.ds(hd, 1), :].rearrange("p o n -> p (o n)"),
                                              ACT.Copy)
                        if m == 0:
                            last.then_inc(s["tick"], 1)
                    last.then_inc(s["qh"], 1)
                    for i in range(NT + 1):
                        if i < NT:
                            act.wait_ge(s["w"], hd * NT + (i - 1 if i > 1 else 0))
                            for m in range(2):
                                act.wait_ge(s["nb"], hd * 2 * NT + 2 * i + m + 1)
                                act.activation(pm[i % 2][:, m, 0:(i + 1) * P], S[m][:, 0:(i + 1) * P], ACT.Exp,
                                               bias=nb[:, i, m:m + 1], scale=QK ** -0.5,
                                               accum_out=z[:, i, m:m + 1]).then_inc(s["exp"], 1)
                        if i >= 1:
                            k = i - 1
                            act.wait_ge(s["o"], hd * NT + (k - 1 if k > 1 else 0))
                            for g, js in enumerate(blocks(k)):
                                act.wait_ge(s["t"], hd * NG + groups[k] - len(blocks(k)) + g + 1)
                                act.activation(wT[k % 2][:, 4 * g:4 * g + len(js), :],
                                               TB[g][:, 0:len(js) * P].rearrange("p (j q) -> p j q", q=P),
                                               ACT.Copy).then_inc(s["te"], 1)
                    act.wait_ge(s["ss"], hd + 1)
                    act.activation(ss[:, 2, :], ss[:, 1, :], ACT.Sqrt).then_inc(s["sd"], 1)
                    for g in range(2):
                        act.wait_ge(s["ot"], 2 * hd + g + 1)
                        act.sem_inc(s["tick"], 1)
                        act.activation(mixA[:, bass.ds(hd, 1), g * 512:g * 512 + 512].rearrange("p o n -> p (o n)"),
                                       TB[g][:], ACT.Copy).then_inc(s["ote"], 1)

            @block.vector
            def _(dve):
                ch = Chain(dve, s["ch"])
                with dve.Fori(0, H) as hd:
                    for i in range(NT + 2):
                        if i < NT:
                            for m in range(2):
                                dve.wait_ge(s["s"], hd * 2 * NT + 2 * i + m + 1)
                                dg = S[m][:, i * P:i * P + P]
                                ch.add(dve.tensor_tensor(dg, dg, causal[:], ALU.add))
                                ch.sync()
                                ch.add(dve.tensor_reduce(mx[:, i, m:m + 1], S[m][:, 0:(i + 1) * P], AX_X, ALU.max))
                                ch.sync()
                                dve.tensor_scalar(nb[:, i, m:m + 1], mx[:, i, m:m + 1], -QK ** -0.5, None,
                                                  ALU.mult).then_inc(s["nb"], 1)
                        if 1 <= i <= NT:
                            k = i - 1
                            n = (k + 1) * P
                            dve.wait_ge(s["exp"], hd * 2 * NT + 2 * k + 2)
                            ch.add(dve.reciprocal(rz[:, k, :], z[:, k, :]))
                            ch.sync()
                            ch.add(dve.tensor_tensor(rz[:, k, 1:2], rz[:, k, 1:2], nlam[:], ALU.mult))
                            dve.wait_ge(s["t"], hd * NG + (groups[k - 2] if k > 1 else 0))
                            ch.add(dve.tensor_scalar(w[k % 2][:, 0:n], pm[k % 2][:, 0, 0:n], rz[:, k, 0:1], None,
                                                     ALU.mult))
                            ch.sync()
                            dve.scalar_tensor_tensor(out=w[k % 2][:, 0:n], in0=pm[k % 2][:, 1, 0:n],
                                                     scalar=rz[:, k, 1:2], in1=w[k % 2][:, 0:n],
                                                     op0=ALU.mult, op1=ALU.add).then_inc(s["w"], 1)
                        if i == 2:
                            dve.wait_ge(s["ote"], 2 * hd)
                        if i >= 2:
                            k = i - 2
                            dve.wait_ge(s["o"], hd * NT + k + 1)
                            dve.tensor_copy(oh[:, k, :], OB[k % 2][:, 0:VD]).then_inc(s["oe"], 1)
                            dve.wait_ge(s["oe"], hd * NT + k + 1)
                            ch.add(dve.tensor_tensor_reduce(sq[:, k, :], oh[:, k, :], oh[:, k, :], 1.0, 0.0,
                                                            ALU.mult, ALU.add, ss[:, 0, k:k + 1]))
                    ch.sync()
                    dve.tensor_scalar(ss[:, 1, :], ss[:, 0, :], 1.0 / VD, EPS, ALU.mult, ALU.add).then_inc(s["ss"], 1)
                    dve.wait_ge(s["sd"], hd + 1)
                    ch.add(dve.reciprocal(ss[:, 0, :], ss[:, 2, :]))
                    ch.sync()
                    for k in range(NT):
                        last = dve.scalar_tensor_tensor(out=oh[:, k, :], in0=oh[:, k, :], scalar=ss[:, 0, k:k + 1],
                                                        in1=g_row[:], op0=ALU.mult, op1=ALU.mult)
                    last.then_inc(s["on"], 1)
                    ch.restart()


class LayerNorm:

    def __init__(self, sb, sem, tag, g, b):
        self.g, self.b = g, b
        self.st = sb(tag + "_st", [P, 2, 6])
        self.mv = sb(tag + "_mv", [P, 2])
        self.sd = sb(tag + "_sd", [P, 3])
        self.s_var = sem("s_" + tag + "_var")
        self.s_sd = sem("s_" + tag + "_sd")

    def deviation(self, act, n, R):
        act.wait_ge(self.s_var, n + 1)
        act.activation(self.sd[0:R, 1:2], self.sd[0:R, 0:1], ACT.Sqrt).then_inc(self.s_sd, 1)

    def run(self, dve, ch, n, R, r):
        ch.sync()
        for h in range(2):
            ch.add(dve.bn_stats(self.st[0:R, h, :], r[0:R, h * 512:h * 512 + 512]))
        ch.sync()
        ch.add(dve.bn_aggr(self.mv[0:R, :], self.st[0:R, :, :]))
        ch.sync()
        dve.tensor_scalar(self.sd[0:R, 0:1], self.mv[0:R, 1:2], EPS, None, ALU.add).then_inc(self.s_var, 1)
        dve.wait_ge(self.s_sd, n + 1)
        ch.add(dve.reciprocal(self.sd[0:R, 2:3], self.sd[0:R, 1:2]))
        ch.sync()
        ch.add(dve.tensor_scalar(r[0:R, :], r[0:R, :], self.mv[0:R, 0:1], self.sd[0:R, 2:3],
                                 ALU.subtract, ALU.mult))
        ch.sync()
        ch.add(dve.tensor_tensor(r[0:R, :], r[0:R, :], self.g[0:R, :], ALU.mult))
        ch.sync()
        return dve.tensor_tensor(r[0:R, :], r[0:R, :], self.b[0:R, :], ALU.add)


def mix_matmul(pe, banks, mc, w_out, R):
    for h in range(2):
        for k in range(KC):
            last = pe.matmul(banks[h][0:R, :], mc[:, k, 0:R], w_out[:, k, h * 512:h * 512 + 512],
                             start=(k == 0), stop=(k == KC - 1))
    return last


def prompt_mix(nc, a, maker, mixA, mixR, x1_d):
    with ExitStack() as ctx:
        sb, ps, sem = maker(ctx)
        w_out = sb("w_out", [P, KC, D])
        g1, b1 = sb("g1", [P, D]), sb("b1", [P, D])
        mc = [sb(f"mc{n}", [P, KC, P]) for n in range(2)]
        res = [sb(f"res{n}", [P, D]) for n in range(2)]
        B = [[ps(f"m_b{n}{h}") for h in range(2)] for n in range(2)]
        ln = LayerNorm(sb, sem, "ln1", g1, b1)
        s_w = sem("s_m_w")
        s_gb = sem("s_m_gb")
        s_res = [sem(f"s_m_res{n}") for n in range(2)]
        s_st = [sem(f"s_m_st{n}") for n in range(2)]
        names = ("ca", "cr", "mm", "sum", "x1", "ch", "tick")
        s = {n: sem("s_m_" + n) for n in names}
        with nc.Block() as block:
            @block.sync
            def _(sp):
                wv = a["w_out"].rearrange("(k p) n -> p k n", p=P)
                for k in range(KC):
                    sp.dma_start(w_out[:, k, :], wv[:, k, :]).then_inc(s_w, 16)
                sp.dma_start(g1[:], a["ln1_g"].to_broadcast([P, D])).then_inc(s_gb, 16)
                sp.dma_start(b1[:], a["ln1_b"].to_broadcast([P, D])).then_inc(s_gb, 16)
                for n in range(2):
                    sp.dma_start(res[n][:], rows(a["x_prompt"], n * P, P)).then_inc(s_res[n], 16)

                def store(g, n):
                    sp.wait_ge(s["x1"], 2 * g + n + 1)
                    sp.dma_start(rows(x1_d, (2 * g + n) * P, P), res[n][:]).then_inc(s_st[n], 16)
                    sp.wait_ge(s_st[n], 16 * g + 16)

                with sp.Fori(0, NT // 2 - 1) as g:
                    for n in range(2):
                        store(g, n)
                        sp.dma_start(res[n][:], rows(a["x_prompt"], (2 * g + 2 + n) * P, P)).then_inc(s_res[n], 16)
                for n in range(2):
                    store(NT // 2 - 1, n)

            @block.gpsimd
            def _(pool):
                with pool.Fori(0, NT // 2) as g:
                    for n in range(2):
                        pool.wait_ge(s["mm"], 2 * g)
                        pool.sem_inc(s["tick"], 1)
                        pool.tensor_copy(mc[n][:, H:KC, :], mixR[:, :, bass.ds((2 * g + n) * P, P)]).then_inc(s["cr"], 1)

            @block.tensor
            def _(pe):
                pe.wait_ge(s_w, 16 * KC)
                with pe.Fori(0, NT // 2) as g:
                    for n in range(2):
                        pe.wait_ge(s["ca"], 2 * g + n + 1)
                        pe.wait_ge(s["cr"], 2 * g + n + 1)
                        pe.wait_ge(s["sum"], 2 * g)
                        mix_matmul(pe, B[n], mc[n], w_out, P).then_inc(s["mm"], 1)

            @block.scalar
            def _(act):
                with act.Fori(0, NT // 2) as g:
                    for n in range(2):
                        act.wait_ge(s["mm"], 2 * g)
                        act.sem_inc(s["tick"], 1)
                        act.activation(mc[n][:, 0:H, :], mixA[:, :, bass.ds((2 * g + n) * P, P)],
                                       ACT.Copy).then_inc(s["ca"], 1)
                    for n in range(2):
                        ln.deviation(act, 2 * g + n, P)

            @block.vector
            def _(dve):
                ch = Chain(dve, s["ch"])
                dve.wait_ge(s_gb, 32)
                with dve.Fori(0, NT // 2) as g:
                    for n in range(2):
                        dve.wait_ge(s_res[n], 16 * g + 16)
                        dve.wait_ge(s["mm"], 2 * g + n + 1)
                        for h in range(2):
                            part = res[n][:, h * 512:h * 512 + 512]
                            last = dve.scalar_tensor_tensor(out=part, in0=part, scalar=ALPHA, in1=B[n][h][:],
                                                            op0=ALU.mult, op1=ALU.add)
                            if h == 0:
                                ch.add(last)
                        last.then_inc(s["sum"], 1)
                        dve.wait_ge(s["sum"], 2 * g + n + 1)
                        ln.run(dve, ch, 2 * g + n, P, res[n]).then_inc(s["x1"], 1)
                    ch.restart()


def peer(nc, a, o, maker, ident, cbase, smask, hmask, g_row, qTs, kTs, mixS, x1_d, ffn_d, upto):
    NU, NV, ND = 4, 8, 4
    PES, DVS = (0, 1, 3, 4, 6), (2, 5, 7)
    NPE, NDV = 2 * len(PES), 2 * len(DVS)
    CP = ((0, 2, 16), (2, 5, 5), (5, 16, 2))
    NC = sum((a1 - a0) * b for a0, a1, b in CP)
    GP = 4
    NG = NPG // GP
    KEYS = PAST + DS
    with ExitStack() as ctx:
        sb, ps, sem = maker(ctx)
        wq = sb("wq", [P, KC, 2 * PH * PK])
        keysT = sb("keysT", [P, 2 * PH, PK])
        u = [sb(f"u{n}", [P, D]) for n in range(NU)]
        v = [sb(f"v{n}", [P, D]) for n in range(NV)]
        x_cur, x1n, facc = sb("x_cur", [P, D]), sb("x1n", [P, D]), sb("facc", [P, D])
        x1T = sb("x1T", [P, KC, P])
        q_sb, qTt, sc, sc2 = sb("q_sb", [P, 2, P]), sb("qTt", [P, 2, P]), sb("sc", [P, 2, PK]), sb("sc2", [P, 2, PK])
        tv, ti, tif = sb("tv", [P, 2, TOPK]), sb("ti", [P, 2, TOPK], U32), sb("tif", [P, 2, TOPK])
        cand, cand2, cidx = sb("cand", [P, NC]), sb("cand2", [P, NC]), sb("cidx", [P, NC])
        ts, tpos, tposf = sb("ts", [P, TOPK]), sb("tpos", [P, TOPK], U32), sb("tposf", [P, TOPK])
        eq, eidx = sb("eq", [P, TOPK, NC]), sb("eidx", [P, TOPK])
        iota = sb("iota", [P, NC])
        nts, ex, zx = sb("nts", [P, 1]), sb("ex", [P, TOPK]), sb("zx", [P, 2])
        idx_all = sb("idx_all", [P, PH, TOPK], I32)
        gt_all = sb("gt_all", [P, PH, TOPK])
        idxU = [sb(f"idxU{n}", [P, TOPK], I32) for n in range(2)]
        idxV = [sb(f"idxV{n}", [P, TOPK], I32) for n in range(2)]
        gt = [sb(f"gt{n}", [P, TOPK]) for n in range(2)]
        act16 = [sb(f"act{n}", [P, TOPK]) for n in range(2)]
        gi = sb("gi", [P, TOPK])
        w16 = [sb(f"w16{n}", [P, TOPK]) for n in range(2)]
        diag = [sb(f"diag{n}", [P, P]) for n in range(ND)]
        oS = sb("oS", [H * DS, DB, VD])
        batch = ctx.enter_context(ExitStack())
        sb = maker(batch)[0]
        pt = sb("pt", [1, DB * NPG], I32)
        pg = [sb(f"pg{n}", [P, GP, AW]) for n in range(2)]
        kTp = sb("kTp", [P, H, GP * P])
        qst = sb("qst", [P, H, SR])
        S = sb("S", [SR, KEYS])
        sm = sb("sm", [SR, 4])
        cj = sb("cj", [SR, H * DS])
        wTs = sb("wTs", [P, GP * H * DS])
        wTn = sb("wTn", [DS, H * DS])
        vnew = sb("vnew", [DS, AW])
        om = sb("om", [H * DS, VD])
        B = [ps(f"e_b{n}") for n in range(8)]
        ACC, QB, TB, KB, SB_, OB = B[0:2], B[2], B[3], B[4:6], B[6], B[7]
        s_u = [sem(f"s_u{n}") for n in range(NU)]
        s_v = [sem(f"s_v{n}") for n in range(NV)]
        s_pg = [sem(f"s_pg{n}") for n in range(2)]
        names = ("wq", "kr", "kt", "kte", "zero", "x1n", "xt", "xTa", "xTd", "q", "qe", "qt", "qTe", "sc", "sce",
                 "tk", "ts", "ex", "prepU", "prepV", "ufree", "vpe", "vdve", "gi", "th", "w", "diag", "xcur",
                 "acc", "fo", "fst", "pt", "pgfree", "ktp", "ktpe", "S", "Se", "qst", "sn", "mx", "sx", "cj",
                 "wt", "wte", "wn", "wne", "vn", "O", "Oe", "ch", "tick", "atick", "ptick", "stick", "dtick",
                 "mm", "sum", "nsq", "nsd", "on", "ot", "om", "x1", "xst")
        s = {n: sem("s_e_" + n) for n in names}


        def keys_turn_pe(pe, n, R):
            pe.wait_ge(s["x1n"], 16 * n + 16)
            pe.wait_ge(s["sce"], PH * n)
            pe.wait_ge(s["qTe"], PH * n)
            for half, bank in enumerate((QB, TB)):
                for c in range(4):
                    k = 4 * half + c
                    last = pe.transpose(bank[:, c * P:c * P + R], x1n[0:R, k * P:k * P + P], ident[0:R, 0:R])
                last.then_inc(s["xt"], 1)

        def turned(bank, R):
            return bank[:].rearrange("p (c t) -> p c t", c=4)[:, :, 0:R]

        def keys_turn_act(act, n, R):
            act.wait_ge(s["q"], PH * n)
            act.wait_ge(s["xt"], 2 * n + 1)
            act.activation(x1T[:, 0:4, 0:R], turned(QB, R), ACT.Copy).then_inc(s["xTa"], 1)

        def keys_turn_dve(dve, n, R):
            dve.wait_ge(s["q"], PH * n)
            dve.wait_ge(s["xt"], 2 * n + 2)
            dve.tensor_copy(x1T[:, 4:8, 0:R], turned(TB, R)).then_inc(s["xTd"], 1)

        def keys_q_pe(pe, n, h, R):
            if h == 0:
                pe.wait_ge(s["xTa"], n + 1)
                pe.wait_ge(s["xTd"], n + 1)
            pe.wait_ge(s["sce"], PH * n + h)
            for k in range(KC):
                last = pe.matmul(QB[0:R, 0:2 * P], x1T[:, k, 0:R], wq[:, k, 2 * P * h:2 * P * h + 2 * P],
                                 start=(k == 0), stop=(k == KC - 1))
            last.then_inc(s["q"], 1)

        def keys_q_act(act, n, h, R):
            act.wait_ge(s["qt"], PH * n + h)
            act.wait_ge(s["q"], PH * n + h + 1)
            act.activation(q_sb[0:R, :, :], QB[0:R, 0:2 * P].rearrange("p (a d) -> p a d", a=2),
                           ACT.Copy).then_inc(s["qe"], 1)

        def keys_t_pe(pe, n, h, R):
            pe.wait_ge(s["qTe"], PH * n + h)
            pe.wait_ge(s["qe"], PH * n + h + 1)
            for m in range(2):
                last = pe.transpose(TB[:, m * P:m * P + R], q_sb[0:R, m, :], ident[0:R, 0:R])
            last.then_inc(s["qt"], 1)

        def keys_t_act(act, n, h, R):
            act.wait_ge(s["sc"], PH * n + h)
            act.wait_ge(s["qt"], PH * n + h + 1)
            act.activation(qTt[:, :, 0:R], TB[:, 0:2 * P].rearrange("p (a t) -> p a t", a=2)[:, :, 0:R],
                           ACT.Copy).then_inc(s["qTe"], 1)

        def keys_s_pe(pe, n, h, R):
            pe.wait_ge(s["qTe"], PH * n + h + 1)
            for m in range(2):
                last = pe.matmul(QB[0:R, 2 * P + m * PK:2 * P + m * PK + PK], qTt[:, m, 0:R], keysT[:, 2 * h + m, :],
                                 start=True, stop=True)
            last.then_inc(s["sc"], 1)

        def keys_s_act(act, n, h, R):
            act.wait_ge(s["tk"], PH * n + h)
            act.wait_ge(s["sc"], PH * n + h + 1)
            act.activation(sc[0:R, :, :], QB[0:R, 2 * P:4 * P].rearrange("p (a d) -> p a d", a=2),
                           ACT.Copy).then_inc(s["sce"], 1)

        def top16(ch, dve, R, src, spare, vals, pos):
            ch.add(dve.max(vals[:, 0:8], src))
            ch.sync()
            ch.add(dve.max_index(pos[:, 0:8], vals[:, 0:8], src))
            ch.add(dve.match_replace(spare, vals[:, 0:8], src, -3e38))
            ch.sync()
            ch.add(dve.max(vals[:, 8:16], spare))
            ch.sync()
            ch.add(dve.max_index(pos[:, 8:16], vals[:, 8:16], spare))

        def keys_rank_dve(dve, ch, n, h, R, m):
            if m == 0:
                dve.wait_ge(s["sce"], PH * n + h + 1)
                dve.sem_inc(s["dtick"], 1)
            top16(ch, dve, R, sc[0:R, m, :], sc2[0:R, m, :], tv[0:R, m, :], ti[0:R, m, :])

        def keys_pairs_dve(dve, ch, n, h, R):
            ch.sync()
            ch.add(dve.tensor_copy(tif[0:R], ti[0:R]))
            ch.sync()
            at = 0
            for a0, a1, b in CP:
                shape = [R, a1 - a0, b]
                out = lambda x: x[0:R, at:at + (a1 - a0) * b].rearrange("p (a b) -> p a b", b=b)
                row = lambda x: x[0:R, 0, a0:a1].unsqueeze(2).to_broadcast(shape)
                col = lambda x: x[0:R, 1, 0:b].unsqueeze(1).to_broadcast(shape)
                ch.add(dve.tensor_tensor(out(cand), row(tv), col(tv), ALU.add))
                ch.add(dve.scalar_tensor_tensor(out=out(cidx), in0=row(tif), scalar=float(PK), in1=col(tif),
                                                op0=ALU.mult, op1=ALU.add))
                at += (a1 - a0) * b
            ch.sync()
            top16(ch, dve, R, cand[0:R], cand2[0:R], ts[0:R], tpos[0:R])
            dve.wait_ge(s["ex"], PH * n + h)
            dve.tensor_scalar(nts[0:R], ts[0:R, 0:1], -1.0, None, ALU.mult).then_inc(s["ts"], 1)
            ch.sync()
            ch.add(dve.tensor_copy(tposf[0:R], tpos[0:R]))
            ch.sync()
            shape = [R, TOPK, NC]
            ch.add(dve.tensor_tensor(eq[0:R], iota[0:R].unsqueeze(1).to_broadcast(shape),
                                     tposf[0:R].unsqueeze(2).to_broadcast(shape), ALU.is_equal))
            ch.sync()
            ch.add(dve.tensor_tensor(eq[0:R], eq[0:R], cidx[0:R].unsqueeze(1).to_broadcast(shape), ALU.mult))
            ch.sync()
            ch.add(dve.tensor_reduce(eidx[0:R], eq[0:R], AX_X, ALU.add))
            ch.sync()
            ch.add(dve.tensor_copy(idx_all[0:R, h, :], eidx[0:R]))

        def keys_gate_act(act, n, h, R):
            act.wait_ge(s["ts"], PH * n + h + 1)
            act.activation(ex[0:R], ts[0:R], ACT.Exp, bias=nts[0:R], accum_out=zx[0:R, 0:1]).then_inc(s["ex"], 1)

        def keys_gate_dve(dve, ch, n, h, R):
            dve.wait_ge(s["ex"], PH * n + h + 1)
            ch.add(dve.reciprocal(zx[0:R, 1:2], zx[0:R, 0:1]))
            ch.sync()
            dve.tensor_scalar(gt_all[0:R, h, :], ex[0:R], zx[0:R, 1:2], 0.5, ALU.mult, ALU.mult).then_inc(s["tk"], 1)

        def round_pe(pe, n, R):
            keys_turn_pe(pe, n, R)
            for h in range(PH):
                keys_q_pe(pe, n, h, R)
                keys_t_pe(pe, n, h, R)
                keys_s_pe(pe, n, h, R)

        def round_act(act, n, R):
            keys_turn_act(act, n, R)
            act.activation(x_cur[0:R], x1n[0:R], ACT.Copy).then_inc(s["xcur"], 1)
            for h in range(PH):
                keys_q_act(act, n, h, R)
                keys_t_act(act, n, h, R)
                keys_s_act(act, n, h, R)
                keys_gate_act(act, n, h, R)

        def round_dve(dve, ch, n, R):
            keys_turn_dve(dve, n, R)
            for h in range(PH):
                keys_rank_dve(dve, ch, n, h, R, 0)
                keys_rank_dve(dve, ch, n, h, R, 1)
                keys_pairs_dve(dve, ch, n, h, R)
                keys_gate_dve(dve, ch, n, h, R)


        def u_ready(i, h, j):
            return s_u[j % NU], 16 * (i * (PH * TOPK // NU) + h * (TOPK // NU) + j // NU + 1)

        def v_ready(i, h, j):
            return s_v[j % NV], 16 * (i * (PH * TOPK // NV) + h * (TOPK // NV) + j // NV + 1)

        def nth(i, h, j, slots):
            n = len(slots)
            return i * (PH * 2 * n) + h * 2 * n + (j // NV) * n + slots.index(j % NV)

        def gathers(pool, i, R):
            for h in range(PH + 1):
                for j in range(TOPK):
                    if h < PH:
                        if j == 0:
                            pool.wait_ge(s["prepU"], i * PH + h + 1)
                        pool.wait_ge(s["ufree"], i * PH * TOPK + h * TOPK + j + 1)
                        pool.sem_inc(s["ptick"], 1)
                        pool.indirect_dma_start(u[j % NU][0:R, :], None, a["peer_u"],
                                                bass.IndirectOffsetOnAxis(ap=idxU[h % 2][0:R, j:j + 1], axis=0)
                                                ).then_inc(s_u[j % NU], 16)
                    if h > 0:
                        g = h - 1
                        if j == 0:
                            pool.wait_ge(s["prepV"], i * PH + g + 1)
                        name, slots = ("vpe", PES) if j % NV in PES else ("vdve", DVS)
                        pool.wait_ge(s[name], nth(i, g, j, slots) + 1)
                        pool.sem_inc(s["ptick"], 1)
                        pool.indirect_dma_start(v[j % NV][0:R, :], None, a["peer_v"],
                                                bass.IndirectOffsetOnAxis(ap=idxV[g % 2][0:R, j:j + 1], axis=0)
                                                ).then_inc(s_v[j % NV], 16)

        def experts_pe(pe, i, R, side):
            for h in range(PH + 1):
                for j in range(TOPK):
                    g = h - 1
                    if h > 0 and j % NV in PES:
                        c = nth(i, g, j, PES)
                        first, end = g == 0 and j == 0, g == PH - 1 and j == NV + PES[-1]
                        if first:
                            pe.wait_ge(s["fo"], i)
                        pe.wait_ge(*v_ready(i, g, j))
                        pe.wait_ge(s["diag"], c + 1)
                        for b in range(2):
                            last = pe.matmul(ACC[b][0:R, :], diag[nth(0, g, j, PES) % ND][0:R, 0:R],
                                             v[j % NV][0:R, b * 512:b * 512 + 512], start=first, stop=end)
                        last.then_inc(s["vpe"], 1)
                    side(h, j)

        def experts_act(act, i, R, side):
            for h in range(PH + 1):
                for j in range(TOPK):
                    g = h - 1
                    if h > 0 and j % NV in PES:
                        c = nth(i, g, j, PES)
                        if j == 0:
                            act.wait_ge(s["w"], i * PH + g + 1)
                        act.wait_ge(s["vpe"], c + len(PES) - ND + 1)
                        act.activation(diag[nth(0, g, j, PES) % ND][0:R, 0:R], ident[0:R, 0:R], ACT.Copy,
                                       scale=w16[g % 2][0:R, j:j + 1]).then_inc(s["diag"], 1)
                    side(h, j)
                    if h < PH and j == TOPK - 1:
                        act.wait_ge(s["gi"], i * PH + h + 1)
                        act.activation(gi[0:R], gi[0:R], ACT.Tanh, scale=GELU_B).then_inc(s["th"], 1)

        def experts_dve(dve, ch, i, R, side, n):
            dve.wait_ge(s["tk"], PH * n + PH)
            dve.tensor_copy(idxU[0][0:R], idx_all[0:R, 0, :]).then_inc(s["prepU"], 1)
            dve.wait_ge(s["xcur"], n + 1)
            for h in range(PH + 1):
                for j in range(TOPK):
                    if h < PH:
                        dve.wait_ge(*u_ready(i, h, j))
                        dve.tensor_tensor_reduce(u[j % NU][0:R], u[j % NU][0:R], x_cur[0:R], 1.0, 0.0, ALU.mult,
                                                 ALU.add, act16[h % 2][0:R, j:j + 1]).then_inc(s["ufree"], 1)
                    g = h - 1
                    if h > 0 and j % NV in DVS:
                        c = nth(i, g, j, DVS)
                        first = g == 0 and j == DVS[0]
                        if first:
                            dve.wait_ge(s["fst"], 16 * i)
                        dve.wait_ge(s["vdve"], c + len(DVS))
                        dve.wait_ge(*v_ready(i, g, j))
                        w = w16[g % 2][0:R, j:j + 1]
                        if first:
                            last = dve.tensor_scalar(facc[0:R], v[j % NV][0:R], w, None, ALU.mult)
                        else:
                            last = dve.scalar_tensor_tensor(out=facc[0:R], in0=v[j % NV][0:R], scalar=w,
                                                            in1=facc[0:R], op0=ALU.mult, op1=ALU.add)
                        last.then_inc(s["vdve"], 1)
                    if h < PH and j == 2:
                        dve.wait_ge(s["vpe"], i * PH * NPE + max(h - 1, 0) * NPE + len(PES))
                        if h < PH - 1:
                            dve.tensor_copy(idxU[(h + 1) % 2][0:R], idx_all[0:R, h + 1, :]).then_inc(s["prepU"], 1)
                        dve.tensor_copy(idxV[h % 2][0:R], idx_all[0:R, h, :]).then_inc(s["prepV"], 1)
                        ch.add(dve.tensor_copy(gt[h % 2][0:R], gt_all[0:R, h, :]))
                        ch.sync()
                    if h < PH and j == TOPK - 1:
                        A = act16[h % 2][0:R]
                        dve.wait_ge(s["ufree"], i * PH * TOPK + h * TOPK + TOPK + NU)
                        ch.add(dve.tensor_tensor(gi[0:R], A, A, ALU.mult))
                        ch.sync()
                        ch.add(dve.tensor_scalar(gi[0:R], gi[0:R], GELU_A, 1.0, ALU.mult, ALU.add))
                        ch.sync()
                        dve.tensor_tensor(gi[0:R], gi[0:R], A, ALU.mult).then_inc(s["gi"], 1)
                    side(h, j)
                    if h < PH and j == TOPK - 1:
                        W = w16[h % 2][0:R]
                        dve.wait_ge(s["diag"], i * PH * NPE + max(h - 1, 0) * NPE)
                        dve.wait_ge(s["th"], i * PH + h + 1)
                        ch.add(dve.scalar_tensor_tensor(out=W, in0=gi[0:R], scalar=1.0, in1=act16[h % 2][0:R],
                                                        op0=ALU.add, op1=ALU.mult))
                        ch.sync()
                        dve.tensor_tensor(W, W, gt[h % 2][0:R], ALU.mult).then_inc(s["w"], 1)
                        dve.wait_ge(s["w"], i * PH + h + 1)
            dve.wait_ge(s["vpe"], (i + 1) * PH * NPE + len(PES))
            dve.wait_ge(s["vdve"], (i + 1) * PH * NDV + len(DVS))
            for b in range(2):
                part = facc[0:R, b * 512:b * 512 + 512]
                last = dve.tensor_tensor(part, ACC[b][0:R, :], part, ALU.add)
            last.then_inc(s["fo"], 1)

        def next_rows_act(act, i, R):
            act.wait_ge(s["ufree"], (i + 1) * PH * TOPK + NU)
            act.wait_ge(s["x1n"], 16 * i + 32)
            act.activation(x_cur[0:R], x1n[0:R], ACT.Copy).then_inc(s["xcur"], 1)


        def pages(sp, i):
            sp.wait_ge(s["O"], i)
            sp.sem_inc(s["stick"], 1)
            sp.dma_start(vnew[:], rows(o["v_sample"], i * DS, DS)).then_inc(s["vn"], 16)
            for G in range(2 * NG):
                src = a["cache_k"] if G < NG else a["cache_v"]
                sp.wait_ge(s["pgfree"], i * 2 * NG + max(G - 1, 0))
                sp.sem_inc(s["stick"], 1)
                for n in range(GP):
                    page = sp.value_load(pt[0:1, bass.ds(i * NPG + (G % NG) * GP + n, 1)], min_val=0,
                                         max_val=src.shape[0] // PAGE - 1)
                    sp.dma_start(pg[G % 2][:, n, :], src[bass.ds(page * PAGE, PAGE), :]).then_inc(s_pg[G % 2], 16)

        def queries_act(act, i):
            act.wait_ge(s["S"], i * (NG + 1))
            act.sem_inc(s["atick"], 1)
            for h in range(H):
                for m in range(2):
                    half = slice(QK * m, QK * m + QK)
                    last = act.activation(qst[half, h, (2 * h + m) * DS:(2 * h + m + 1) * DS],
                                          qTs[half, h, bass.ds(i * DS, DS)], ACT.Copy)
            last.then_inc(s["qst"], 1)

        def page_turn_pe(pe, i, g, n):
            if n == 0:
                pe.wait_ge(s_pg[g % 2], 16 * GP * (i * NG + g // 2 + 1))
            c = g * GP + n
            pe.wait_ge(s["ktpe"], i * NPG + max(c - 1, 0))
            for h in range(H):
                last = pe.transpose(KB[c % 2][:, h * P:h * P + P], pg[g % 2][:, n, h * VD:h * VD + VD], ident[:])
            last.then_inc(s["ktp"], 1)

        def page_turn_act(act, i, g, n):
            c = g * GP + n
            if n == 0:
                act.wait_ge(s["S"], i * (NG + 1) + g)
            act.wait_ge(s["ktp"], i * NPG + c + 1)
            act.activation(kTp[:, :, n * P:n * P + P], KB[c % 2][:].rearrange("p (h t) -> p h t", h=H),
                           ACT.Copy).then_inc(s["ktpe"], 1)

        def scores_pe(pe, i, g):
            pe.wait_ge(s["ktpe"], i * NPG + (g + 1) * GP)
            if g == 0:
                pe.wait_ge(s["qst"], i + 1)
                pe.wait_ge(s["sn"], i)
            pe.wait_ge(s["Se"], i * NG + g)
            for h in range(H):
                last = pe.matmul(SB_[0:SR, :], qst[:, h, :], kTp[:, h, :], start=(h == 0), stop=(h == H - 1))
            last.then_inc(s["S"], 1)
            pe.wait_ge(s["S"], i * (NG + 1) + g + 1)
            pe.sem_inc(s["pgfree"], 1)

        def scores_act(act, i, g):
            if g == 0:
                act.wait_ge(s["O"], i)
            act.wait_ge(s["S"], i * (NG + 1) + g + 1)
            act.activation(S[:, g * GP * P:(g + 1) * GP * P], SB_[0:SR, :], ACT.Copy).then_inc(s["Se"], 1)

        def new_keys_pe(pe, i):
            pe.wait_ge(s["Se"], i * NG + NG)
            for h in range(H):
                last = pe.matmul(SB_[0:SR, 0:DS], qst[:, h, :], kTs[:, h, bass.ds(i * DS, DS)],
                                 start=(h == 0), stop=(h == H - 1))
            last.then_inc(s["S"], 1)

        def new_keys_dve(dve, i):
            dve.wait_ge(s["S"], i * (NG + 1) + NG + 1)
            dve.tensor_tensor(S[:, PAST:KEYS], SB_[0:SR, 0:DS], smask[:], ALU.add).then_inc(s["sn"], 1)

        def softmax_dve(dve, ch, i, part):
            if part == 0:
                dve.wait_ge(s["Se"], i * NG + NG)
                dve.wait_ge(s["sn"], i + 1)
                ch.add(dve.tensor_reduce(sm[:, 0:1], S[:], AX_X, ALU.max))
                ch.sync()
                dve.tensor_scalar(sm[:, 1:2], sm[:, 0:1], -QK ** -0.5, None, ALU.mult).then_inc(s["mx"], 1)
            else:
                dve.wait_ge(s["sx"], i + 1)
                ch.add(dve.reciprocal(sm[:, 3:4], sm[:, 2:3]))
                ch.sync()
                dve.tensor_scalar(cj[:], cbase[:], sm[:, 3:4], None, ALU.mult).then_inc(s["cj"], 1)

        def softmax_act(act, i):
            act.wait_ge(s["mx"], i + 1)
            act.activation(S[:], S[:], ACT.Exp, bias=sm[:, 1:2], scale=QK ** -0.5,
                           accum_out=sm[:, 2:3]).then_inc(s["sx"], 1)

        def weights_pe(pe, i, g):
            if g == 0:
                pe.wait_ge(s["cj"], i + 1)
                pe.wait_ge(s["ktpe"], i * NPG + NPG)
                pe.sem_inc(s["tick"], 1)
                pe.matmul(SB_[0:DS, 0:H * DS], S[:, PAST:KEYS], cj[:], start=True, stop=True).then_inc(s["wn"], 1)
            pe.wait_ge(s["wte"], i * NG + g)
            pe.sem_inc(s["tick"], 1)
            for n in range(GP):
                c = (g * GP + n) * P
                last = pe.matmul(KB[0][:, n * H * DS:(n + 1) * H * DS], S[:, c:c + P], cj[:], start=True, stop=True)
            last.then_inc(s["wt"], 1)

        def weights_act(act, i, g):
            if g == 0:
                act.wait_ge(s["wn"], i + 1)
                act.activation(wTn[:], SB_[0:DS, 0:H * DS], ACT.Copy).then_inc(s["wne"], 1)
            act.wait_ge(s["pgfree"], i * 2 * NG + NG + g)
            act.wait_ge(s["wt"], i * NG + g + 1)
            act.activation(wTs[:], KB[0][:, 0:GP * H * DS], ACT.Copy).then_inc(s["wte"], 1)

        def values_pe(pe, i, g):
            if g == 0:
                pe.wait_ge(s["Oe"], i)
                pe.wait_ge(s["wne"], i + 1)
                pe.wait_ge(s["vn"], 16 * i + 16)
                pe.sem_inc(s["tick"], 1)
                pe.matmul(OB[0:H * DS, :], wTn[:], vnew[:], start=True, stop=False)
            pe.wait_ge(s["wte"], i * NG + g + 1)
            pe.wait_ge(s_pg[g % 2], 16 * GP * (i * NG + NG // 2 + g // 2 + 1))
            for n in range(GP):
                last = pe.matmul(OB[0:H * DS, :], wTs[:, n * H * DS:(n + 1) * H * DS], pg[g % 2][:, n, :],
                                 start=False, stop=(g == NG - 1 and n == GP - 1))
            last.then_inc(s["pgfree"], 1)
            if g == NG - 1:
                pe.wait_ge(s["pgfree"], (i + 1) * 2 * NG)
                pe.sem_inc(s["O"], 1)

        def heads_dve(dve, ch, i):
            dve.wait_ge(s["O"], i + 1)
            head = lambda h: OB[0:H * DS, h * VD:h * VD + VD]
            ch.sync()
            ch.add(dve.tensor_scalar(om[:], head(0), hmask[:, 0:1], None, ALU.mult))
            for h in range(1, H):
                ch.sync()
                last = dve.scalar_tensor_tensor(out=om[:], in0=head(h), scalar=hmask[:, h:h + 1], in1=om[:],
                                                op0=ALU.mult, op1=ALU.add)
                if h < H - 1:
                    ch.add(last)
            last.then_inc(s["Oe"], 1)
            dve.wait_ge(s["Oe"], i + 1)
            ch.add(dve.tensor_copy(oS[:, bass.ds(i, 1), :].rearrange("p o d -> p (o d)"), om[:]))

        TURNS = {0: (0, 0), 1: (0, 1), 2: (0, 2), 3: (0, 3), 7: (1, 0), 9: (1, 1), 10: (1, 2), 11: (1, 3)}

        def side_pe(pe, i):
            def side(h, j):
                if h == PH:
                    return
                if h == 0 and j == 3:
                    keys_turn_pe(pe, i + 1, P)
                if j == 4:
                    keys_q_pe(pe, i + 1, h, P)
                if j == 6:
                    keys_t_pe(pe, i + 1, h, P)
                if j == 8:
                    keys_s_pe(pe, i + 1, h, P)
                if h < NG // 2:
                    if j in TURNS:
                        page_turn_pe(pe, i, 2 * h + TURNS[j][0], TURNS[j][1])
                    if j in (5, 13):
                        scores_pe(pe, i, 2 * h + j // 8)
                    if h == NG // 2 - 1 and j == 14:
                        new_keys_pe(pe, i)
                else:
                    g = 2 * (h - NG // 2)
                    if j in (7, 12):
                        weights_pe(pe, i, g + j // 9)
                    if j in (9, 14):
                        values_pe(pe, i, g + j // 12)
            return side

        def side_act(act, i):
            def side(h, j):
                if h == PH:
                    if j == 0:
                        next_rows_act(act, i, P)
                    return
                if h == 0 and j == 0:
                    queries_act(act, i)
                if h == 0 and j == 3:
                    keys_turn_act(act, i + 1, P)
                if j == 4:
                    keys_q_act(act, i + 1, h, P)
                if j == 6:
                    keys_t_act(act, i + 1, h, P)
                if j == 8:
                    keys_s_act(act, i + 1, h, P)
                if j == 14:
                    keys_gate_act(act, i + 1, h, P)
                if h < NG // 2:
                    if j in TURNS:
                        page_turn_act(act, i, 2 * h + TURNS[j][0], TURNS[j][1])
                    if j in (5, 13):
                        scores_act(act, i, 2 * h + j // 8)
                else:
                    g = 2 * (h - NG // 2)
                    if h == NG // 2 and j == 1:
                        softmax_act(act, i)
                    if j in (7, 12):
                        weights_act(act, i, g + j // 9)
            return side

        def side_dve(dve, ch, i):
            def side(h, j):
                if h == PH:
                    return
                if h == 0 and j == 3:
                    keys_turn_dve(dve, i + 1, P)
                if j == 9:
                    keys_rank_dve(dve, ch, i + 1, h, P, 0)
                if j == 11:
                    keys_rank_dve(dve, ch, i + 1, h, P, 1)
                if j == 13:
                    keys_pairs_dve(dve, ch, i + 1, h, P)
                if j == 15:
                    keys_gate_dve(dve, ch, i + 1, h, P)
                if h == NG // 2 - 1 and j == 14:
                    new_keys_dve(dve, i)
                if h == NG // 2 and j == 0:
                    softmax_dve(dve, ch, i, 0)
                if h == NG // 2 and j == 4:
                    softmax_dve(dve, ch, i, 1)
                if h == PH - 1 and j == 15:
                    heads_dve(dve, ch, i)
            return side

        with nc.Block() as block:
            @block.sync
            def _(sp):
                sp.dma_start(pt[:], a["page_table"]).then_inc(s["pt"], 16)
                sp.dma_start(x1n[:], rows(x1_d, 0, P)).then_inc(s["x1n"], 16)
                kv = a["peer_keys"].rearrange("(g q p) d -> g p q d", q=8, p=P)
                for g in range(2):
                    sp.dma_start(v[g][:].rearrange("p (q d) -> p q d", q=8), kv[g]).then_inc(s["kr"], 16)
                wv = a["peer_wq"].rearrange("(k p) n -> p k n", p=P)
                for k in range(KC):
                    sp.dma_start(wq[:, k, :], wv[:, k, :]).then_inc(s["wq"], 16)
                sp.wait_ge(s["pt"], 16)

            @block.gpsimd
            def _(pool):
                pool.memset(qst[:], 0.0)
                pool.iota(iota[:], pattern=[[1, NC]], base=0, channel_multiplier=0,
                          allow_small_or_imprecise_dtypes=True).then_inc(s["zero"], 1)

            @block.tensor
            def _(pe):
                pe.wait_ge(s["kr"], 32)
                for t in range(4):
                    pe.wait_ge(s["kte"], max(t - 1, 0))
                    for c in range(4):
                        m = 4 * t + c
                        last = pe.transpose(KB[t % 2][:, c * P:c * P + P],
                                            v[m // 8][:, (m % 8) * P:(m % 8) * P + P], ident[:])
                    last.then_inc(s["kt"], 1)
                pe.wait_ge(s["kte"], 4)
                pe.wait_ge(s["wq"], 16 * KC)
                round_pe(pe, 0, P)
                pe.sem_inc(s["vpe"], len(PES))

            @block.scalar
            def _(act):
                for t in range(4):
                    act.wait_ge(s["kt"], t + 1)
                    act.activation(keysT[:, 4 * t:4 * t + 4, :], KB[t % 2][:].rearrange("p (c n) -> p c n", c=4),
                                   ACT.Copy).then_inc(s["kte"], 1)
                round_act(act, 0, P)

            @block.vector
            def _(dve):
                ch = Chain(dve, s["ch"])
                dve.wait_ge(s["zero"], 1)
                round_dve(dve, ch, 0, P)
                dve.sem_inc(s["ufree"], NU)
                dve.sem_inc(s["vdve"], len(DVS))
                ch.restart()

        if upto <= 5:
            return
        with nc.Block() as block:
            @block.sync
            def _(sp):
                with sp.Fori(0, NT) as i:
                    sp.wait_ge(s["xcur"], i + 1)
                    sp.sem_inc(s["stick"], 1)
                    sp.dma_start(x1n[:], rows(x1_d, i * P + P, P)).then_inc(s["x1n"], 16)
                    pages(sp, i)
                    sp.wait_ge(s["fo"], i + 1)
                    sp.sem_inc(s["stick"], 1)
                    sp.dma_start(rows(ffn_d, i * P, P), facc[:]).then_inc(s["fst"], 16)
                sp.wait_ge(s["fst"], 16 * NT)

            @block.gpsimd
            def _(pool):
                with pool.Fori(0, NT) as i:
                    gathers(pool, i, P)

            @block.tensor
            def _(pe):
                with pe.Fori(0, NT) as i:
                    experts_pe(pe, i, P, side_pe(pe, i))

            @block.scalar
            def _(act):
                with act.Fori(0, NT) as i:
                    experts_act(act, i, P, side_act(act, i))

            @block.vector
            def _(dve):
                ch = Chain(dve, s["ch"])
                with dve.Fori(0, NT) as i:
                    experts_dve(dve, ch, i, P, side_dve(dve, ch, i), i)
                    ch.restart()

        batch.close()
        if upto <= 6:
            return
        sb = maker(ctx)[0]
        w_out = sb("w_out_s", [P, KC, D])
        g1, b1 = sb("g1_s", [P, D]), sb("b1_s", [P, D])
        rs = sb("rs", [H * DS, 3, DB])
        ln = LayerNorm(sb, sem, "ln1s", g1, b1)
        last_round = NT + 1
        osq = eq[0:H * DS].rearrange("p a b -> p (a b)")[:, 0:DB * VD].rearrange("p (b d) -> p b d", b=DB)
        nothing = lambda h, j: None
        with nc.Block() as block:
            @block.sync
            def _(sp):
                wv = a["w_out"].rearrange("(k p) n -> p k n", p=P)
                for k in range(KC):
                    sp.dma_start(w_out[:, k, :], wv[:, k, :]).then_inc(s["mm"], 16)
                sp.dma_start(x1n[0:SR, :], a["x_sample"]).then_inc(s["x1"], 16)
                sp.dma_start(g1[:], a["ln1_g"].to_broadcast([P, D])).then_inc(s["x1"], 16)
                sp.dma_start(b1[:], a["ln1_b"].to_broadcast([P, D])).then_inc(s["x1"], 16)
                sp.wait_ge(s["om"], 1)
                sp.dma_start(rows(x1_d, SEQ, SR), x1n[0:SR, :]).then_inc(s["xst"], 16)
                sp.wait_ge(s["xst"], 16)
                sp.dma_start(x1n[0:SR, :], rows(x1_d, SEQ, SR)).then_inc(s["x1n"], 16)
                sp.wait_ge(s["fo"], NT + 1)
                sp.dma_start(rows(ffn_d, SEQ, SR), facc[0:SR, :]).then_inc(s["fst"], 16)
                sp.wait_ge(s["fst"], 16 * (NT + 1))

            @block.gpsimd
            def _(pool):
                gathers(pool, NT, SR)

            @block.tensor
            def _(pe):
                pe.wait_ge(s["on"], 1)
                for b in range(DB):
                    last = pe.transpose(SB_[:, b * H * DS:(b + 1) * H * DS], oS[:, b, :], ident[0:H * DS, 0:H * DS])
                last.then_inc(s["ot"], 1)
                pe.wait_ge(s["sum"], 1)
                pe.wait_ge(s["mm"], 16 * KC)
                mix_matmul(pe, KB, mixS, w_out, SR).then_inc(s["ot"], 1)
                round_pe(pe, last_round, SR)
                experts_pe(pe, NT, SR, nothing)

            @block.scalar
            def _(act):
                act.wait_ge(s["nsq"], 1)
                act.activation(rs[:, 1, :], rs[:, 0, :], ACT.Sqrt).then_inc(s["nsd"], 1)
                ln.deviation(act, 0, SR)
                round_act(act, last_round, SR)
                experts_act(act, NT, SR, nothing)

            @block.vector
            def _(dve):
                ch = Chain(dve, s["ch"])
                ch.add(dve.tensor_tensor(osq, oS[:], oS[:], ALU.mult))
                ch.sync()
                ch.add(dve.tensor_reduce(rs[:, 2, :], osq, AX_X, ALU.add))
                ch.sync()
                dve.tensor_scalar(rs[:, 0, :], rs[:, 2, :], 1.0 / VD, EPS, ALU.mult, ALU.add).then_inc(s["nsq"], 1)
                dve.wait_ge(s["nsd"], 1)
                ch.add(dve.reciprocal(rs[:, 2, :], rs[:, 1, :]))
                ch.sync()
                ch.add(dve.tensor_tensor(oS[:], oS[:], rs[:, 2, :].unsqueeze(2).to_broadcast([H * DS, DB, VD]),
                                         ALU.mult))
                ch.sync()
                dve.tensor_tensor(oS[:], oS[:], g_row[0:H * DS].unsqueeze(1).to_broadcast([H * DS, DB, VD]),
                                  ALU.mult).then_inc(s["on"], 1)
                dve.wait_ge(s["ot"], 1)
                dve.tensor_copy(mixS[:, 0:H, :].rearrange("p h (b q) -> p h b q", b=DB),
                                SB_[:, 0:DB * H * DS].rearrange("p (b h q) -> p h b q", b=DB, h=H)
                                ).then_inc(s["sum"], 1)
                dve.wait_ge(s["x1"], 48)
                dve.wait_ge(s["ot"], 2)
                for h in range(2):
                    part = x1n[0:SR, h * 512:h * 512 + 512]
                    ch.add(dve.scalar_tensor_tensor(out=part, in0=part, scalar=ALPHA, in1=KB[h][0:SR, :],
                                                    op0=ALU.mult, op1=ALU.add))
                ln.run(dve, ch, 0, SR, x1n).then_inc(s["om"], 1)
                round_dve(dve, ch, last_round, SR)
                experts_dve(dve, ch, NT, SR, nothing, last_round)


def output(nc, a, o, maker, ident, x1_d, ffn_d):
    PC = PLE // P
    with ExitStack() as ctx:
        sb, ps, sem = maker(ctx)
        wg, wp = sb("wg", [P, KC, D]), sb("wp", [P, PC, D])
        g2, b2, gb = sb("g2", [P, D]), sb("b2", [P, D]), sb("gb", [P, D])
        x2 = [sb(f"x2{n}", [P, D]) for n in range(2)]
        f = [sb(f"f{n}", [P, D]) for n in range(2)]
        pr = [sb(f"pr{n}", [P, PLE]) for n in range(2)]
        x2T, prT = sb("x2T", [P, KC, P]), sb("prT", [P, PC, P])
        TB, PB = [ps(f"o_t{n}") for n in range(2)], ps("o_p")
        Z, L = [ps(f"o_z{n}") for n in range(2)], [ps(f"o_l{n}") for n in range(2)]
        ln = LayerNorm(sb, sem, "ln2", g2, b2)
        s_in = [sem(f"s_o_in{n}") for n in range(2)]
        s_st = [sem(f"s_o_st{n}") for n in range(2)]
        names = ("w", "gb", "x2", "pp", "pT", "tp", "xT", "z", "l", "zr", "lr", "th", "y", "ch", "tick")
        s = {n: sem("s_o_" + n) for n in names}

        with nc.Block() as block:
            @block.sync
            def _(sp):
                def load(n, at, R, src, sat):
                    sp.dma_start(x2[n][0:R, :], rows(x1_d, at, R)).then_inc(s_in[n], 16)
                    sp.dma_start(f[n][0:R, :], rows(ffn_d, at, R)).then_inc(s_in[n], 16)
                    sp.dma_start(pr[n][0:R, :], rows(src, sat, R)).then_inc(s_in[n], 16)

                def store(T, n, times, dst, at, R):
                    sp.wait_ge(s["y"], T + 1)
                    sp.sem_inc(s["tick"], 1)
                    sp.dma_start(rows(dst, at, R), f[n][0:R, :]).then_inc(s_st[n], 16)
                    sp.wait_ge(s_st[n], 16 * times)

                load(0, 0, P, a["p_prompt"], 0)
                for name, dst in (("ln2_g", g2), ("ln2_b", b2), ("ple_gate_b", gb)):
                    sp.dma_start(dst[:], a[name].to_broadcast([P, D])).then_inc(s["gb"], 16)
                sp.dma_start(wp[:], a["ple_w"].rearrange("(k p) n -> p k n", p=P)).then_inc(s["w"], 16)
                wv = a["ple_gate_w"].rearrange("(k p) n -> p k n", p=P)
                for k in range(KC):
                    sp.dma_start(wg[:, k, :], wv[:, k, :]).then_inc(s["w"], 16)
                load(1, P, P, a["p_prompt"], P)
                with sp.Fori(0, NT // 2 - 1) as g:
                    for n in range(2):
                        store(2 * g + n, n, g + 1, o["y_prompt"], (2 * g + n) * P, P)
                        load(n, (2 * g + 2 + n) * P, P, a["p_prompt"], (2 * g + 2 + n) * P)
                store(NT - 2, 0, NT // 2, o["y_prompt"], (NT - 2) * P, P)
                load(0, SEQ, SR, a["p_sample"], 0)
                store(NT - 1, 1, NT // 2, o["y_prompt"], (NT - 1) * P, P)
                store(NT, 0, NT // 2 + 1, o["y_sample"], 0, SR)

            def turned(bank, n, R):
                return bank[:, 0:n * P].rearrange("p (c t) -> p c t", c=n)[:, :, 0:R]

            @block.tensor
            def _(pe):
                def tile(T, n, R):
                    pe.wait_ge(s["x2"], T + 1)
                    pe.wait_ge(s["pT"], T)
                    for c in range(PC):
                        last = pe.transpose(PB[:, c * P:c * P + R], pr[n][0:R, c * P:c * P + P], ident[0:R, 0:R])
                    last.then_inc(s["pp"], 1)
                    pe.wait_ge(s["xT"], 2 * T)
                    for h in range(2):
                        for c in range(4):
                            k = 4 * h + c
                            last = pe.transpose(TB[h][:, c * P:c * P + R], x2[n][0:R, k * P:k * P + P],
                                                ident[0:R, 0:R])
                        last.then_inc(s["tp"], 1)
                    pe.wait_ge(s["pT"], T + 1)
                    pe.wait_ge(s["lr"], T)
                    for h in range(2):
                        for k in range(PC):
                            last = pe.matmul(L[h][0:R, :], prT[:, k, 0:R], wp[:, k, h * 512:h * 512 + 512],
                                             start=(k == 0), stop=(k == PC - 1))
                    last.then_inc(s["l"], 1)
                    pe.wait_ge(s["xT"], 2 * T + 2)
                    pe.wait_ge(s["zr"], T)
                    mix_matmul(pe, Z, x2T, wg, R).then_inc(s["z"], 1)

                pe.wait_ge(s["w"], 16 * (KC + 1))
                with pe.Fori(0, NT // 2) as g:
                    for n in range(2):
                        tile(2 * g + n, n, P)
                tile(NT, 0, SR)

            @block.scalar
            def _(act):
                def tile(T, R, following):
                    act.wait_ge(s["l"], T)
                    act.wait_ge(s["pp"], T + 1)
                    act.activation(prT[:, :, 0:R], turned(PB, PC, R), ACT.Copy).then_inc(s["pT"], 1)
                    act.wait_ge(s["z"], T)
                    for h in range(2):
                        act.wait_ge(s["tp"], 2 * T + h + 1)
                        act.activation(x2T[:, 4 * h:4 * h + 4, 0:R], turned(TB[h], 4, R),
                                       ACT.Copy).then_inc(s["xT"], 1)
                    if following:
                        ln.deviation(act, T + 1, following)

                def gate(T, n, R):
                    act.wait_ge(s["zr"], T + 1)
                    act.activation(f[n][0:R], f[n][0:R], ACT.Tanh, scale=0.5).then_inc(s["th"], 1)

                ln.deviation(act, 0, P)
                with act.Fori(0, NT // 2 - 1) as g:
                    for n in range(2):
                        tile(2 * g + n, P, P)
                        gate(2 * g + n, n, P)
                tile(NT - 2, P, P)
                gate(NT - 2, 0, P)
                tile(NT - 1, P, SR)
                gate(NT - 1, 1, P)
                tile(NT, SR, 0)
                gate(NT, 0, SR)

            @block.vector
            def _(dve):
                ch = Chain(dve, s["ch"])

                def norm(T, n, times, R):
                    dve.wait_ge(s_in[n], 48 * times)
                    ch.add(dve.scalar_tensor_tensor(out=x2[n][0:R], in0=x2[n][0:R], scalar=ALPHA, in1=f[n][0:R],
                                                    op0=ALU.mult, op1=ALU.add))
                    ln.run(dve, ch, T, R, x2[n]).then_inc(s["x2"], 1)

                def gate(T, n, R):
                    dve.wait_ge(s["z"], T + 1)
                    for h in range(2):
                        last = dve.tensor_tensor(f[n][0:R, h * 512:h * 512 + 512], Z[h][0:R, :],
                                                 gb[0:R, h * 512:h * 512 + 512], ALU.add)
                    last.then_inc(s["zr"], 1)
                    dve.wait_ge(s["th"], T + 1)
                    dve.wait_ge(s["l"], T + 1)
                    for h in range(2):
                        part = f[n][0:R, h * 512:h * 512 + 512]
                        last = dve.scalar_tensor_tensor(out=part, in0=part, scalar=1.0, in1=L[h][0:R, :],
                                                        op0=ALU.add, op1=ALU.mult)
                    last.then_inc(s["lr"], 1)
                    dve.wait_ge(s["lr"], T + 1)
                    dve.scalar_tensor_tensor(out=f[n][0:R], in0=f[n][0:R], scalar=0.5, in1=x2[n][0:R],
                                             op0=ALU.mult, op1=ALU.add).then_inc(s["y"], 1)

                dve.wait_ge(s["gb"], 48)
                norm(0, 0, 1, P)
                ch.restart()
                with dve.Fori(0, NT // 2 - 1) as g:
                    norm(2 * g + 1, 1, g + 1, P)
                    gate(2 * g, 0, P)
                    norm(2 * g + 2, 0, g + 2, P)
                    gate(2 * g + 1, 1, P)
                    ch.restart()
                norm(NT - 1, 1, NT // 2, P)
                gate(NT - 2, 0, P)
                norm(NT, 0, NT // 2 + 1, SR)
                gate(NT - 1, 1, P)
                gate(NT, 0, SR)


_ROWS = {
    "x_prompt": (SEQ, D), "x_sample": (SR, D), "p_prompt": (SEQ, PLE), "p_sample": (SR, PLE),
    "cache_k": None, "cache_v": None, "state_h": (DB, RW), "state_conv": (DB * (CW - 1), RW),
    "page_table": (1, DB * NPG), "w_in": (D, IN), "lambda_q1": (1, QK), "lambda_k1": (1, QK),
    "lambda_q2": (1, QK), "lambda_k2": (1, QK), "subln_g": (1, VD), "conv_w": (CW, RW), "conv_b": (1, RW),
    "rg_wa": (8, 64, 64), "rg_ba": (1, RW), "rg_wx": (8, 64, 64), "rg_bx": (1, RW), "rg_lambda": (1, RW),
    "w_out": (D, D), "ln1_g": (1, D), "ln1_b": (1, D), "peer_wq": (D, 2 * PH * PK),
    "peer_keys": (PH * 2 * PK, P), "peer_u": (PK * PK, D), "peer_v": (PK * PK, D),
    "ln2_g": (1, D), "ln2_b": (1, D), "ple_w": (PLE, D), "ple_gate_w": (D, D), "ple_gate_b": (1, D),
}
_OUTS = [
    ("y_prompt", (SEQ, D), (1, SEQ, D)), ("y_sample", (SR, D), (DB, DS, D)),
    ("k_prompt", (SEQ, AW), (1, 1, SEQ, H, VD)), ("v_prompt", (SEQ, AW), (1, 1, SEQ, H, VD)),
    ("h_prompt", (1, RW), (1, 1, RW)), ("conv_prompt", (CW - 1, RW), (1, 1, CW - 1, RW)),
    ("k_sample", (SR, AW), (1, DB, DS, H, VD)), ("v_sample", (SR, AW), (1, DB, DS, H, VD)),
    ("h_sample", (DB, RW), (1, DB, RW)), ("conv_sample", (DB * (CW - 1), RW), (1, DB, CW - 1, RW)),
]


def rope_table():
    import numpy as np

    freq = np.float32(500000.0) ** (-np.arange(0, ROT, 2, dtype=np.float32) / np.float32(ROT))
    pos = np.concatenate([np.arange(SEQ), np.tile(PAST + np.arange(DS), DB)]).astype(np.float32)
    ang = pos[:, None] * freq[None, :]
    return np.stack([np.cos(ang), np.sin(ang)], 1).astype(np.float32)


def kernel(**inputs):
    import numpy as np
    import concourse.bacc as bacc
    from concourse.bass_utils import run_bass_kernel_spmd

    nc = bacc.Bacc("TRN2", target_bir_lowering=False, num_devices=1)
    arrays, a, o = {}, {}, {}
    for name, shape in _ROWS.items():
        x = np.ascontiguousarray(inputs[name])
        if shape is None:
            shape = (x.shape[1] * x.shape[2], AW)
        arrays["in_" + name] = x.reshape(shape)
    arrays["in_rope"] = rope_table()
    for name, x in arrays.items():
        a[name[3:]] = nc.dram_tensor(name, x.shape, mybir.dt.from_np(x.dtype), kind="ExternalInput").ap()
    for name, shape, _ in _OUTS:
        o[name] = nc.dram_tensor("out_" + name, shape, F32, kind="ExternalOutput").ap()
    program(nc, a, o)
    r = run_bass_kernel_spmd(nc, [arrays], core_ids=[0])
    return tuple(r.results[0]["out_" + name].reshape(shape) for name, _, shape in _OUTS)
```

```python
import math
from contextlib import ExitStack

import concourse.bass as bass
from concourse import mybir

F32 = mybir.dt.float32
I32 = mybir.dt.int32
U32 = mybir.dt.uint32
ALU = mybir.AluOpType
ACT = mybir.ActivationFunctionType
AX_X = mybir.AxisListType.X

P = 128
D = 1024
KC = D // P
SEQ = 1024
NT = SEQ // P
DB, DS = 8, 8
SR = DB * DS
PAST, PAGE = 4096, 128
NPG = PAST // PAGE
H, QK, VD = 4, 64, 128
AW = H * VD
RW = D - AW
RC = RW // P
IN = 3 * AW + 2 * RW
ROT = QK // 4
HALF = ROT // 2
CW = 4
PH, PK, TOPK = 8, 128, 16
PLE = 256
EPS = 1e-5
ALPHA = 2.0 ** 0.25
LAM_INIT = 0.8 - 0.6 * math.exp(0.0)
NEG = -1e30
W_ORDER = (3 * AW + RW, 3 * AW, 0, AW, 2 * AW)
GELU_A, GELU_B = 0.044715, math.sqrt(2.0 / math.pi)


class Chain:

    def __init__(self, eng, sem):
        self.eng, self.sem, self.n = eng, sem, 0

    def add(self, ins):
        ins.then_inc(self.sem, 1)
        self.n += 1

    def sync(self):
        self.eng.wait_ge(self.sem, self.n)

    def restart(self):
        self.sync()
        self.eng.sem_clear(self.sem)
        self.n = 0


def rows(dram, start, n):
    return dram[bass.ds(start, n), :]


def program(nc, a, o):
    top = ExitStack()

    def maker(ctx):
        def sb(name, shape, dt=F32):
            return ctx.enter_context(nc.sbuf_tensor(name, shape, dt))

        def ps(name, shape=(P, 512)):
            return ctx.enter_context(nc.psum_tensor(name, list(shape), F32))

        sems = []

        def sem(name):
            sems.append(nc.alloc_semaphore(name=name))
            return sems[-1]

        def give_back():
            if sems:
                nc.clear_and_free_semaphores(sems)
                nc.all_engine_barrier()

        ctx.callback(give_back)
        return sb, ps, sem

    with top:
        sb, _, sem = maker(top)
        ident = sb("ident", [P, P])
        nlam = sb("nlam", [P, 1])
        g_row = sb("g_row", [P, VD])
        causal = sb("causal", [P, P])
        smask = sb("smask", [SR, DS])
        cbase = sb("cbase", [SR, H * DS])
        hmask = sb("hmask", [H * DS, H])
        rgp = sb("rgp", [P, 8 * RC])
        hba = sb("hba", [P, 2, RC])
        sp4 = sb("sp4", [P, 2, RC])
        rope = sb("rope", [P, NT + 1, 2, HALF])
        qTs = sb("qTs", [P, H, SR])
        kTs = sb("kTs", [P, H, SR])
        mixS = sb("mixS", [P, KC, SR])
        x1_d = nc.dram_tensor("x1_scratch", (SEQ + SR, D), F32, kind="Internal").ap()
        ffn_d = nc.dram_tensor("ffn_scratch", (SEQ, D), F32, kind="Internal").ap()

        wq = sb("wq", [P, KC, 2 * PH * PK])
        s_wq = sem("s_wq")
        room = wq[:].rearrange("p k n -> p (k n)")
        kT, qT, v_all, spare = [room[:, n * 4 * D:(n + 1) * 4 * D] for n in range(4)]
        kT = kT.rearrange("p (h t) -> p h t", h=H)
        qT = qT.rearrange("p (h t) -> p h t", h=H)
        v_all = v_all.rearrange("p (t d) -> p t d", t=NT)

        with ExitStack() as c1:
            sb1, _, _ = maker(c1)
            mixR = sb1("mixR", [P, RC, SEQ])
            with ExitStack() as c2:
                sb2, _, sem2 = maker(c2)
                w_in = sb2("w_in", [P, KC, IN])
                s_w = [sem2(f"s_w{n}") for n in range(len(W_ORDER))]
                s_x = sem2("s_x")
                xrow = spare[:, 0:D]

                def load_w_in(sp):
                    sp.dma_start(xrow, rows(a["x_prompt"], 0, P)).then_inc(s_x, 16)
                    win = a["w_in"].rearrange("(k p) n -> p k n", p=P)
                    for n, col in enumerate(W_ORDER):
                        for k in range(0, KC, 2):
                            sp.dma_start(w_in[:, k:k + 2, col:col + AW], win[:, k:k + 2, col:col + AW]
                                         ).then_inc(s_w[n], 16)

                constants(nc, a, maker, ident, nlam, g_row, causal, smask, cbase, hmask, rgp, hba, sp4, rope,
                          load_w_in)
                projection(nc, a, o, maker, ident, rgp, hba, sp4, rope, qTs, kTs, mixS, mixR, kT, qT, v_all,
                           w_in, s_w, xrow, s_x, spare)
            mixA = sb1("mixA", [P, H, SEQ])
            sb1, _, sem1 = maker(c1)
            w_out, g1, b1 = sb1("w_out", [P, KC, D]), sb1("g1", [P, D]), sb1("b1", [P, D])
            s_wo = sem1("s_wo")

            def load_w_out(sp):
                wv = a["w_out"].rearrange("(k p) n -> p k n", p=P)
                for k in range(KC):
                    sp.dma_start(w_out[:, k, :], wv[:, k, :]).then_inc(s_wo, 16)
                sp.dma_start(g1[:], a["ln1_g"].to_broadcast([P, D])).then_inc(s_wo, 16)
                sp.dma_start(b1[:], a["ln1_b"].to_broadcast([P, D])).then_inc(s_wo, 16)

            def load_wq(sp):
                wv = a["peer_wq"].rearrange("(k p) n -> p k n", p=P)
                for k in range(KC):
                    sp.dma_start(wq[:, k, :], wv[:, k, :]).then_inc(s_wq, 16)

            prompt_attention(nc, maker, ident, nlam, g_row, causal, kT, qT, v_all, mixA, spare, load_w_out)
            prompt_mix(nc, a, maker, mixA, mixR, x1_d, w_out, g1, b1, s_wo, load_wq)
        peer(nc, a, o, maker, ident, cbase, smask, hmask, g_row, qTs, kTs, mixS, x1_d, ffn_d, wq, s_wq)


def constants(nc, a, maker, ident, nlam, g_row, causal, smask, cbase, hmask, rgp, hba, sp4, rope, ahead):
    with ExitStack() as ctx:
        sb, ps, sem = maker(ctx)
        lq = sb("lq", [P, 4, QK])
        raw = sb("raw", [8 * RC, P])
        smT = sb("smT", [DS, SR])
        w = sb("w", [P, 12, RC])
        e = sb("e", [P, 4])
        bank = ps("c_bank")
        bank2 = ps("c_bank2")
        s_ld = sem("s_ld")
        s_rope = sem("s_rope")
        s_pool = sem("s_pool")
        s_ch = sem("s_ch")
        s_pe = sem("s_pe")
        s_act = sem("s_act")
        s_dve = sem("s_dve")
        with nc.Block() as block:
            @block.sync
            def _(sp):
                for n, name in enumerate(("lambda_q1", "lambda_k1", "lambda_q2", "lambda_k2")):
                    sp.dma_start(lq[:, n, :], a[name].to_broadcast([P, QK])).then_inc(s_ld, 16)
                sp.dma_start(g_row[:], a["subln_g"].to_broadcast([P, VD])).then_inc(s_ld, 16)
                sp.dma_start(raw[0:CW * RC, :], a["conv_w"].rearrange("j (c p) -> (j c) p", p=P)).then_inc(s_ld, 16)
                for n, name in enumerate(("conv_b", "rg_ba", "rg_bx", "rg_lambda")):
                    sp.dma_start(raw[(CW + n) * RC:(CW + n + 1) * RC, :],
                                 a[name].rearrange("o (c p) -> (o c) p", p=P)).then_inc(s_ld, 16)
                table = a["rope"]
                sp.dma_start(rope[:, 0:NT, :, :], table[0:SEQ].rearrange("(t p) a c -> p t a c", p=P)).then_inc(s_rope, 16)
                sp.dma_start(rope[0:SR, NT, :, :], table[SEQ:SEQ + SR]).then_inc(s_rope, 16)
                ahead(sp)
                sp.wait_ge(s_rope, 32)

            @block.gpsimd
            def _(pool):
                pool.memset(ident[:], 0.0).then_inc(s_pool, 1)
                pool.memset(causal[:], 0.0).then_inc(s_pool, 1)
                pool.memset(smT[:], 0.0).then_inc(s_pool, 1)
                pool.memset(hmask[:], 1.0).then_inc(s_pool, 1)
                pool.wait_ge(s_pool, 4)
                pool.affine_select(out=ident[:], in_=ident[:], compare_op=ALU.not_equal, fill=1.0, base=0,
                                   pattern=[[-1, P]], channel_multiplier=1).then_inc(s_pool, 1)
                pool.affine_select(out=causal[:], in_=causal[:], compare_op=ALU.is_ge, fill=NEG, base=0,
                                   pattern=[[-1, P]], channel_multiplier=1)
                pool.affine_select(out=smT[:], in_=smT[:], compare_op=ALU.is_ge, fill=NEG, base=0,
                                   pattern=[[0, 2 * H], [1, DS]], channel_multiplier=-1)
                pool.affine_select(out=hmask[:], in_=hmask[:], compare_op=ALU.is_ge, fill=0.0, base=0,
                                   pattern=[[-DS, H]], channel_multiplier=1).then_inc(s_pool, 1)
                pool.wait_ge(s_pool, 6)
                pool.affine_select(out=hmask[:], in_=hmask[:], compare_op=ALU.is_ge, fill=0.0, base=DS - 1,
                                   pattern=[[DS, H]], channel_multiplier=-1).then_inc(s_pool, 1)

            @block.tensor
            def _(pe):
                pe.wait_ge(s_pool, 7)
                pe.wait_ge(s_ld, 160)
                pe.transpose(bank[:, 0:8 * RC], raw[:], ident[0:8 * RC, 0:8 * RC]).then_inc(s_pe, 1)
                pe.transpose(bank2[0:SR, 0:DS], smT[:], ident[0:DS, 0:DS]).then_inc(s_pe, 1)

            @block.scalar
            def _(act):
                act.wait_ge(s_dve, 1)
                act.activation(e[:, 2:4], e[:, 0:2], ACT.Exp).then_inc(s_act, 1)
                act.wait_ge(s_dve, 2)
                act.activation(w[:, 1, :], w[:, 0, :], ACT.Exp).then_inc(s_act, 1)
                act.wait_ge(s_dve, 3)
                act.activation(w[:, 3, :], w[:, 2, :], ACT.Ln).then_inc(s_act, 1)

            @block.vector
            def _(dve):
                ch = Chain(dve, s_ch)
                dve.wait_ge(s_ld, 160)
                for n in range(2):
                    last = dve.tensor_tensor_reduce(lq[:, 2 * n, :], lq[:, 2 * n, :], lq[:, 2 * n + 1, :],
                                                    1.0, 0.0, ALU.mult, ALU.add, e[:, n:n + 1])
                last.then_inc(s_dve, 1)
                ch.add(dve.tensor_scalar(g_row[:], g_row[:], 1.0 - LAM_INIT, None, ALU.mult))
                dve.wait_ge(s_pe, 2)
                ch.add(dve.tensor_copy(rgp[:], bank[:, 0:8 * RC]))
                ch.add(dve.tensor_copy(smask[:], bank2[0:SR, 0:DS]))
                ch.sync()
                dve.tensor_scalar(hba[:, 0, :], rgp[:, 5 * RC:6 * RC], 0.5, None, ALU.mult)
                dve.tensor_scalar(hba[:, 1, :], rgp[:, 6 * RC:7 * RC], 0.5, None, ALU.mult)
                lam = rgp[:, 7 * RC:8 * RC]
                ch.add(dve.tensor_scalar(w[:, 4, :], lam, -1.0, None, ALU.mult))
                ch.sync()
                dve.tensor_scalar(w[:, 5, :], w[:, 4, :], 0.0, None, ALU.max)
                dve.tensor_tensor(w[:, 0, :], lam, w[:, 4, :], ALU.min).then_inc(s_dve, 1)
                dve.wait_ge(s_act, 2)
                dve.tensor_scalar(w[:, 2, :], w[:, 1, :], 1.0, None, ALU.add).then_inc(s_dve, 1)
                dve.wait_ge(s_act, 3)
                ch.add(dve.tensor_scalar(w[:, 6, :], w[:, 2, :], 1.0, None, ALU.subtract))
                ch.add(dve.tensor_tensor(w[:, 7, :], w[:, 3, :], w[:, 1, :], ALU.mult))
                ch.sync()
                ch.add(dve.tensor_scalar(w[:, 8, :], w[:, 6, :], 0.0, None, ALU.is_equal))
                ch.sync()
                ch.add(dve.tensor_tensor(w[:, 6, :], w[:, 6, :], w[:, 8, :], ALU.add))
                ch.add(dve.tensor_tensor(w[:, 9, :], w[:, 8, :], w[:, 1, :], ALU.mult))
                ch.sync()
                ch.add(dve.reciprocal(w[:, 10, :], w[:, 6, :]))
                ch.sync()
                ch.add(dve.tensor_tensor(w[:, 7, :], w[:, 7, :], w[:, 10, :], ALU.mult))
                ch.sync()
                ch.add(dve.tensor_tensor(w[:, 7, :], w[:, 7, :], w[:, 9, :], ALU.add))
                ch.sync()
                ch.add(dve.tensor_tensor(w[:, 7, :], w[:, 7, :], w[:, 5, :], ALU.add))
                ch.sync()
                dve.tensor_scalar(sp4[:, 0, :], w[:, 7, :], 4.0, None, ALU.mult)
                dve.tensor_scalar(sp4[:, 1, :], w[:, 7, :], -4.0, None, ALU.mult)
                ch.add(dve.tensor_tensor(nlam[:], e[:, 3:4], e[:, 2:3], ALU.subtract))
                ch.sync()
                ch.add(dve.tensor_scalar(nlam[:], nlam[:], LAM_INIT, None, ALU.subtract))
                ch.sync()
                i4 = ident[0:SR, 0:SR].rearrange("p (h m q) -> p h m q", h=H, m=2)
                dve.scalar_tensor_tensor(out=cbase[:].rearrange("p (h q) -> p h q", h=H), in0=i4[:, :, 1, :],
                                         scalar=nlam[0:SR, :], in1=i4[:, :, 0, :], op0=ALU.mult, op1=ALU.add)


def projection(nc, a, o, maker, ident, rgp, hba, sp4, rope, qTs, kTs, mixS, mixR, kT, qT, v_all,
               w_in, s_w, xrow, s_x, spare):
    with ExitStack() as ctx:
        sb, ps, sem = maker(ctx)
        wab = sb("wab", [P, 2, RC, P])
        xT = spare[:, D:2 * D].rearrange("p (k t) -> p k t", k=KC)
        qk = spare[:, 2 * D:3 * D]
        rt = sb("rt", [P, 4, 16, HALF])
        xrb = sb("xrb", [P, RC, 1, CW - 1 + P])
        xrs = sb("xrs", [P, RC, DB, CW - 1 + DS])
        gate, xc = [spare[:, 3 * D + n * 512:3 * D + n * 512 + 512].rearrange("p (c t) -> p c t", c=RC)
                    for n in range(2)]
        thr = sb("thr", [P, RC, P])
        thi = sb("thi", [P, RC, P])
        tu = sb("tu", [P, RC, P])
        gin = sb("gin", [P, RC, P])
        dec = sb("dec", [P, RC, 1, 1 + P])
        inp = sb("inp", [P, RC, 1, 1 + P])
        hb = sb("hb", [P, RC, 1, 1 + P])
        decs = sb("decs", [P, RC, DB, 1 + DS])
        inps = sb("inps", [P, RC, DB, 1 + DS])
        hbs = sb("hbs", [P, RC, DB, 1 + DS])
        tail = sb("tail", [DB * (CW - 1), 4, RW])
        tail_v = sb("tail_v", [SR, AW])
        cst = sb("cst", [P, RC, DB * (CW - 1)])
        hst = sb("hst", [P, RC, DB])
        B = [ps(f"p_bank{n}") for n in range(8)]
        s_rg = sem("s_rg")
        s_zero = sem("s_zero")
        s_st = sem("s_st")
        names = ("xps", "xTa", "xTd", "gate", "xr", "q", "k", "v", "xrev", "gev", "kev", "vev", "rope",
                 "qTp", "kTp", "qTev", "kTev", "xc", "carry", "r", "i", "thr", "thi", "tu", "in", "tg", "s2",
                 "sq", "y", "kout", "vout", "stT", "stc", "hT", "hc", "tout", "gdone", "dch", "ach", "tick")
        s = {n: sem("s_p_" + n) for n in names}
        s["x"] = s_x
        GATE, XR, Rb, Ib = B[4], B[3], B[7], B[3]
        t4 = lambda x, R: x[:].rearrange("p (c t) -> p c t", c=RC)[:, :, 0:R]
        xrow_d = (a["x_prompt"], a["x_sample"])

        with nc.Block() as block:
            @block.sync
            def _(sp):
                sp.wait_ge(s_zero, 2)
                for m, name in enumerate(("rg_wa", "rg_wx")):
                    src = a[name].rearrange("(c two) i j -> two i c j", two=2)
                    for h in range(2):
                        sp.dma_start(wab[64 * h:64 * h + 64, m, :, 64 * h:64 * h + 64], src[h]).then_inc(s_rg, 16)
                sp.dma_start(tail[:, 0, :], a["state_conv"]).then_inc(s_st, 16)
                sp.dma_start(tail[0:DB, 1, :], a["state_h"]).then_inc(s_st, 16)

                def out_tile(t, R, kd, vd, v_src, at):
                    sp.wait_ge(s["rope"], t + 1)
                    sp.dma_start(rows(kd, at, R), qk[0:R, AW:2 * AW]).then_inc(s["kout"], 16)
                    sp.wait_ge(s["vev"], t + 1)
                    sp.dma_start(rows(vd, at, R), v_src).then_inc(s["vout"], 16)

                def prompt_tile(t):
                    sp.wait_ge(s["xps"], 2 * t + 2)
                    sp.dma_start(xrow[:], rows(xrow_d[0], t * P + P, P)).then_inc(s["x"], 16)
                    out_tile(t, P, o["k_prompt"], o["v_prompt"], v_all[:, bass.ds(t, 1), :], t * P)

                with sp.Fori(0, NT - 1) as t:
                    prompt_tile(t)
                sp.wait_ge(s["xps"], 2 * NT)
                sp.dma_start(xrow[0:SR, :], xrow_d[1]).then_inc(s["x"], 16)
                out_tile(NT - 1, P, o["k_prompt"], o["v_prompt"], v_all[:, NT - 1:NT, :], (NT - 1) * P)
                out_tile(NT, SR, o["k_sample"], o["v_sample"], tail_v[:], 0)
                sp.wait_ge(s["hc"], 2)
                sp.dma_start(o["conv_prompt"], tail[0:CW - 1, 2, :]).then_inc(s["tout"], 16)
                sp.dma_start(o["h_prompt"], tail[0:1, 3, :]).then_inc(s["tout"], 16)
                sp.wait_ge(s["tout"], 32)
                sp.sem_inc(s["gdone"], 1)
                sp.wait_ge(s["hc"], 4)
                sp.dma_start(o["conv_sample"], tail[:, 2, :]).then_inc(s["tout"], 16)
                sp.dma_start(o["h_sample"], tail[0:DB, 3, :]).then_inc(s["tout"], 16)
                sp.wait_ge(s["tout"], 64)
                sp.wait_ge(s["kout"], 16 * (NT + 1))
                sp.wait_ge(s["vout"], 16 * (NT + 1))

            @block.gpsimd
            def _(pool):
                pool.memset(wab[:], 0.0).then_inc(s_zero, 1)
                pool.memset(xrb[:], 0.0)
                pool.memset(dec[:], 0.0)
                pool.memset(decs[:], 0.0)
                pool.memset(hb[:], 0.0).then_inc(s_zero, 1)

            @block.tensor
            def _(pe):
                def turn_x(t, R):
                    pe.wait_ge(s["qTev"], t)
                    pe.wait_ge(s["kTev"], t)
                    pe.wait_ge(s["x"], 16 * t + 16)
                    for half in range(2):
                        for c in range(4):
                            k = 4 * half + c
                            last = pe.transpose(B[5 + half][:, c * P:c * P + R], xrow[0:R, k * P:k * P + P],
                                                ident[0:R, 0:R])
                        last.then_inc(s["xps"], 1)

                def rg_gates(t, R):
                    pe.wait_ge(s["thr"], t)
                    pe.wait_ge(s["thi"], t)
                    pe.wait_ge(s["xrev"], t + 1)
                    pe.wait_ge(s["xc"], t + 1)
                    for m, (bank, done) in enumerate(((Rb, "r"), (Ib, "i"))):
                        for c in range(RC):
                            last = pe.matmul(bank[:, c * P:c * P + R], wab[:, m, c, :], xc[:, c, 0:R],
                                             start=True, stop=True)
                        last.then_inc(s[done], 1)

                def channel_major(t, R, bank, col, done):
                    for c in range(RC):
                        for k in range(KC):
                            last = pe.matmul(bank[:, c * P:c * P + R], w_in[:, k, col + c * P:col + c * P + P],
                                             xT[:, k, 0:R], start=(k == 0), stop=(k == KC - 1))
                    last.then_inc(s[done], 1)

                def token_major(R, bank, col, done):
                    for k in range(KC):
                        last = pe.matmul(bank[0:R, :], xT[:, k, 0:R], w_in[:, k, col:col + AW],
                                         start=(k == 0), stop=(k == KC - 1))
                    last.then_inc(s[done], 1)

                def tile(t, R, before):
                    turn_x(t, R)
                    if before:
                        rg_gates(t - 1, P)
                    pe.wait_ge(s["xTa"], t + 1)
                    pe.wait_ge(s["xTd"], t + 1)
                    arrived = lambda n: before or pe.wait_ge(s_w[n], 16 * KC // 2)
                    arrived(0)
                    pe.wait_ge(s["gev"], t)
                    channel_major(t, R, GATE, 3 * AW + RW, "gate")
                    pe.wait_ge(s["thi"], t)
                    arrived(1)
                    channel_major(t, R, XR, 3 * AW, "xr")
                    pe.wait_ge(s["kev"], t)
                    arrived(2)
                    token_major(R, B[0], 0, "q")
                    arrived(3)
                    token_major(R, B[1], AW, "k")
                    pe.wait_ge(s["vev"], t)
                    arrived(4)
                    token_major(R, B[2], 2 * AW, "v")
                    pe.wait_ge(s["rope"], t + 1)
                    for bank, at, done in ((B[5], 0, "qTp"), (B[6], AW, "kTp")):
                        for h in range(H):
                            last = pe.transpose(bank[:, h * P:h * P + R], qk[0:R, at + h * P:at + h * P + P],
                                                ident[0:R, 0:R])
                        last.then_inc(s[done], 1)

                def states_out(src_x, src_h, G, n):
                    L = src_x.shape[3] - (CW - 1)
                    pe.wait_ge(s["y"], NT + n)
                    if n:
                        pe.wait_ge(s["hc"], 2)
                    for c in range(RC):
                        last = pe.transpose(B[0][0:G * (CW - 1), c * P:c * P + P], cst[:, c, 0:G * (CW - 1)],
                                            ident[:])
                    last.then_inc(s["hT"], 1)
                    for c in range(RC):
                        last = pe.transpose(B[1][0:G, c * P:c * P + P], hst[:, c, 0:G], ident[:])
                    last.then_inc(s["hT"], 1)

                pe.wait_ge(s_zero, 2)
                tile(0, P, False)
                pe.wait_ge(s_rg, 64)
                with pe.Fori(1, NT) as t:
                    tile(t, P, True)
                pe.wait_ge(s_st, 32)
                pe.wait_ge(s["thr"], NT - 1)
                for c in range(RC):
                    pe.transpose(Rb[:, c * 32:c * 32 + DB * (CW - 1)], tail[:, 0, c * P:c * P + P],
                                 ident[0:DB * (CW - 1), 0:DB * (CW - 1)])
                    last = pe.transpose(Rb[:, 256 + c * DB:256 + c * DB + DB], tail[0:DB, 1, c * P:c * P + P],
                                        ident[0:DB, 0:DB])
                last.then_inc(s["stT"], 1)
                pe.wait_ge(s["stc"], 1)
                tile(NT, SR, True)
                rg_gates(NT, SR)
                pe.wait_ge(s["stc"], 2)
                states_out(xrb, hb, 1, 0)
                pe.wait_ge(s["stc"], 3)
                states_out(xrs, hbs, DB, 1)

            @block.scalar
            def _(act):
                ch = Chain(act, s["ach"])

                def x_turned(t, R):
                    act.wait_ge(s["v"], t)
                    act.wait_ge(s["xps"], 2 * t + 1)
                    act.activation(xT[:, 0:4, 0:R], t4(B[5], R), ACT.Copy).then_inc(s["xTa"], 1)

                def rg_tail(t, R, L, dec_t):
                    G = R // L
                    act.wait_ge(s["r"], t + 1)
                    act.wait_ge(s["y"], t)
                    for c in range(RC):
                        last = act.activation(thr[:, c, 0:R], Rb[:, c * P:c * P + R], ACT.Tanh,
                                              bias=hba[:, 0, c:c + 1], scale=0.5)
                    last.then_inc(s["thr"], 1)
                    act.wait_ge(s["i"], t + 1)
                    for c in range(RC):
                        last = act.activation(thi[:, c, 0:R], Ib[:, c * P:c * P + R], ACT.Tanh,
                                              bias=hba[:, 1, c:c + 1], scale=0.5)
                    last.then_inc(s["thi"], 1)
                    act.wait_ge(s["thr"], t + 1)
                    for c in range(RC):
                        act.activation(tu[:, c, 0:R], thr[:, c, 0:R], ACT.Tanh,
                                       bias=sp4[:, 0, c:c + 1], scale=sp4[:, 0, c:c + 1])
                        last = act.activation(dec_t[:, c, :, 1:], thr[:, c, 0:R].rearrange("p (g l) -> p g l", g=G),
                                              ACT.Exp, bias=sp4[:, 1, c:c + 1], scale=sp4[:, 1, c:c + 1])
                    last.then_inc(s["tu"], 1)
                    act.wait_ge(s["in"], t + 1)
                    act.activation(gin[:, :, 0:R], gin[:, :, 0:R], ACT.Tanh, scale=GELU_B).then_inc(s["tg"], 1)
                    act.wait_ge(s["s2"], t + 1)
                    act.activation(tu[:, :, 0:R], tu[:, :, 0:R], ACT.Sqrt).then_inc(s["sq"], 1)

                def evacuate(t, R, L, xr_t, v_dst, q_dst, k_dst):
                    act.wait_ge(s["carry"], t)
                    act.wait_ge(s["xr"], t + 1)
                    src = XR[:].rearrange("p (c t) -> p c t", c=RC)[:, :, 0:R].rearrange("p c (g l) -> p c g l", l=L)
                    act.activation(xr_t[:, :, :, CW - 1:], src, ACT.Copy).then_inc(s["xrev"], 1)
                    act.wait_ge(s["y"], t)
                    act.wait_ge(s["gate"], t + 1)
                    act.activation(gate[:, :, 0:R], t4(GATE, R), ACT.Copy).then_inc(s["gev"], 1)
                    act.wait_ge(s["qTp"], t)
                    act.wait_ge(s["kTp"], t)
                    act.wait_ge(s["kout"], 16 * t)
                    act.wait_ge(s["k"], t + 1)
                    act.activation(qk[0:R, 0:AW], B[0][0:R, :], ACT.Copy)
                    act.activation(qk[0:R, AW:2 * AW], B[1][0:R, :], ACT.Copy).then_inc(s["kev"], 1)
                    act.wait_ge(s["v"], t + 1)
                    act.sem_inc(s["tick"], 1)
                    act.activation(v_dst, B[2][0:R, :], ACT.Copy).then_inc(s["vev"], 1)
                    act.wait_ge(s["qTp"], t + 1)
                    act.sem_inc(s["tick"], 1)
                    act.activation(q_dst, t4(B[5], R), ACT.Copy).then_inc(s["qTev"], 1)
                    act.wait_ge(s["kTp"], t + 1)
                    act.sem_inc(s["tick"], 1)
                    act.activation(k_dst, t4(B[6], R), ACT.Copy).then_inc(s["kTev"], 1)

                def prompt_evacuate(t):
                    evacuate(t, P, P, xrb, v_all[:, bass.ds(t, 1), :].rearrange("p o n -> p (o n)"),
                             qT[:, :, bass.ds(t * P, P)], kT[:, :, bass.ds(t * P, P)])

                act.wait_ge(s_zero, 2)
                x_turned(0, P)
                prompt_evacuate(0)
                with act.Fori(1, NT) as t:
                    x_turned(t, P)
                    rg_tail(t - 1, P, P, dec)
                    prompt_evacuate(t)
                x_turned(NT, SR)
                rg_tail(NT - 1, P, P, dec)
                evacuate(NT, SR, DS, xrs, tail_v[:], qTs[:], kTs[:])
                rg_tail(NT, SR, DS, decs)
                for n, G in enumerate((1, DB)):
                    act.wait_ge(s["hT"], 2 * n + 2)
                    if n:
                        act.wait_ge(s["gdone"], 1)
                    act.activation(tail[0:G * (CW - 1), 2, :], B[0][0:G * (CW - 1), :], ACT.Copy).then_inc(s["hc"], 1)
                    act.activation(tail[0:G, 3, :], B[1][0:G, :], ACT.Copy).then_inc(s["hc"], 1)

            @block.vector
            def _(dve):
                ch = Chain(dve, s["dch"])
                tap = lambda j, c: rgp[:, j * RC + c:j * RC + c + 1]

                def x_turned(t, R):
                    dve.wait_ge(s["v"], t)
                    dve.wait_ge(s["xps"], 2 * t + 2)
                    dve.tensor_copy(xT[:, 4:8, 0:R], t4(B[6], R)).then_inc(s["xTd"], 1)

                def rg_tail(t, R, L, dec_t, inp_t, hb_t, y_dst):
                    G = R // L
                    v = lambda x: x[:, :, 0:R]
                    g3 = lambda x, c: x[:, c, 0:R].rearrange("p (g l) -> p g l", g=G)
                    ch.sync()
                    dve.wait_ge(s["tu"], t + 1)
                    ch.add(dve.tensor_scalar(v(thr), v(tu), 1.0, None, ALU.add))
                    ch.add(dve.scalar_tensor_tensor(out=v(xc), in0=v(thi), scalar=1.0, in1=v(xc),
                                                    op0=ALU.add, op1=ALU.mult))
                    ch.sync()
                    ch.add(dve.reciprocal(v(thr), v(thr)))
                    ch.sync()
                    dve.scalar_tensor_tensor(out=v(tu), in0=v(tu), scalar=2.0, in1=v(thr),
                                             op0=ALU.mult, op1=ALU.mult).then_inc(s["s2"], 1)
                    dve.wait_ge(s["tg"], t + 1)
                    ch.add(dve.scalar_tensor_tensor(out=v(gate), in0=v(gin), scalar=1.0, in1=v(gate),
                                                    op0=ALU.add, op1=ALU.mult))
                    dve.wait_ge(s["sq"], t + 1)
                    for c in range(RC):
                        ch.add(dve.scalar_tensor_tensor(out=inp_t[:, c, :, 1:], in0=g3(xc, c), scalar=0.5,
                                                        in1=g3(tu, c), op0=ALU.mult, op1=ALU.mult))
                    ch.sync()
                    flat = lambda x: x[:].rearrange("p c g l -> p (c g l)")
                    ch.add(dve.tensor_tensor_scan(flat(hb_t), flat(dec_t), flat(inp_t), 0.0, ALU.mult, ALU.add))
                    ch.sync()
                    ch.add(dve.tensor_copy(inp_t[:, :, :, 0:1], hb_t[:, :, :, L:L + 1]))
                    for c in range(RC):
                        last = dve.scalar_tensor_tensor(out=y_dst(c), in0=hb_t[:, c, :, 1:], scalar=0.5,
                                                        in1=g3(gate, c), op0=ALU.mult, op1=ALU.mult)
                    last.then_inc(s["y"], 1)

                def conv(t, R, L, xr_t, carry):
                    G = R // L
                    g3 = lambda c: xc[:, c, 0:R].rearrange("p (g l) -> p g l", g=G)
                    dve.wait_ge(s["i"], t)
                    dve.wait_ge(s["xrev"], t + 1)
                    for c in range(RC):
                        ch.add(dve.tensor_scalar(g3(c), xr_t[:, c, :, 3:3 + L], tap(3, c), tap(4, c),
                                                 ALU.mult, ALU.add))
                    for j in range(CW - 1):
                        ch.sync()
                        for c in range(RC):
                            last = dve.scalar_tensor_tensor(out=g3(c), in0=xr_t[:, c, :, j:j + L], scalar=tap(j, c),
                                                            in1=g3(c), op0=ALU.mult, op1=ALU.add)
                            if (j, c) == (CW - 2, RC - 1):
                                last.then_inc(s["xc"], 1)
                            else:
                                ch.add(last)
                    dve.wait_ge(s["xc"], t + 1)
                    if carry:
                        dve.tensor_copy(xr_t[:, :, :, 0:CW - 1], xr_t[:, :, :, L:L + CW - 1]).then_inc(s["carry"], 1)

                def gelu_in(t, R):
                    v = lambda x: x[:, :, 0:R]
                    dve.wait_ge(s["gev"], t + 1)
                    ch.add(dve.tensor_tensor(v(gin), v(gate), v(gate), ALU.mult))
                    ch.sync()
                    ch.add(dve.tensor_scalar(v(gin), v(gin), GELU_A, 1.0, ALU.mult, ALU.add))
                    ch.sync()
                    dve.tensor_tensor(v(gin), v(gin), v(gate), ALU.mult).then_inc(s["in"], 1)

                def rotate(t, R):
                    x = qk[0:R, :].rearrange("p (g d) -> p g d", d=QK)
                    lo, hi = x[:, :, 0:HALF], x[:, :, HALF:ROT]
                    shape = [R, 16, HALF]
                    angle = lambda n: rope[0:R, bass.ds(t, 1), n, :].to_broadcast(shape)
                    cos, sin = angle(0), angle(1)
                    dve.wait_ge(s["kev"], t + 1)
                    for n, (half, f) in enumerate(((lo, cos), (hi, sin), (hi, cos), (lo, sin))):
                        ch.add(dve.tensor_tensor(rt[0:R, n], half, f, ALU.mult))
                    ch.sync()
                    ch.add(dve.tensor_tensor(lo, rt[0:R, 0], rt[0:R, 1], ALU.subtract))
                    dve.tensor_tensor(hi, rt[0:R, 2], rt[0:R, 3], ALU.add).then_inc(s["rope"], 1)

                def prompt_y(t):
                    return lambda c: mixR[:, c, bass.ds(t * P, P)].rearrange("p (g l) -> p g l", g=1)

                dve.wait_ge(s_zero, 2)
                ch.add(dve.memset(inp[:, :, :, 0:1], 0.0))
                x_turned(0, P)
                conv(0, P, P, xrb, True)
                gelu_in(0, P)
                rotate(0, P)
                ch.restart()
                with dve.Fori(1, NT) as t:
                    x_turned(t, P)
                    rg_tail(t - 1, P, P, dec, inp, hb, prompt_y(t - 1))
                    conv(t, P, P, xrb, True)
                    gelu_in(t, P)
                    rotate(t, P)
                    ch.restart()
                dve.wait_ge(s["stT"], 1)
                for c in range(RC):
                    ch.add(dve.tensor_copy(xrs[:, c, :, 0:CW - 1], Rb[:, c * 32:c * 32 + DB * (CW - 1)]
                                           .rearrange("p (g j) -> p g j", g=DB)))
                last = dve.tensor_copy(inps[:, :, :, 0:1].rearrange("p c g o -> p c (g o)"),
                                       Rb[:, 256:256 + RC * DB].rearrange("p (c g) -> p c g", c=RC))
                last.then_inc(s["stc"], 1)
                x_turned(NT, SR)
                rg_tail(NT - 1, P, P, dec, inp, hb, prompt_y(NT - 1))
                conv(NT, SR, DS, xrs, False)
                gelu_in(NT, SR)
                rotate(NT, SR)
                ch.sync()
                dve.wait_ge(s["y"], NT)
                ch.add(dve.tensor_copy(cst[:, :, 0:CW - 1], xrb[:, :, 0, 0:CW - 1]))
                dve.tensor_copy(hst[:, :, 0:1], hb[:, :, 0, P:P + 1]).then_inc(s["stc"], 1)
                rg_tail(NT, SR, DS, decs, inps, hbs,
                        lambda c: mixS[:, RC + c, :].rearrange("p (g l) -> p g l", g=DB))
                dve.wait_ge(s["hT"], 2)
                for c in range(RC):
                    ch.add(dve.tensor_copy(cst[:, c, :].rearrange("p (g j) -> p g j", g=DB),
                                           xrs[:, c, :, DS:DS + CW - 1]))
                dve.tensor_copy(hst[:], hbs[:, :, :, DS:DS + 1].rearrange("p c g o -> p c (g o)")).then_inc(s["stc"], 1)


def prompt_attention(nc, maker, ident, nlam, g_row, causal, kT, qT, v_all, mixA, spare, ahead):
    with ExitStack() as ctx:
        sb, ps, sem = maker(ctx)
        NQ = 4
        qz = sb("qz", [P, NQ, 2, P])
        pm = [spare[:, n * 2 * SEQ:(n + 1) * 2 * SEQ].rearrange("p (m t) -> p m t", m=2) for n in range(2)]
        squares = spare.rearrange("p (n d) -> p n d", d=VD)
        w = [sb(f"w{n}", [P, SEQ]) for n in range(2)]
        wT = [sb(f"wT{n}", [P, NT, P]) for n in range(2)]
        oh = sb("oh", [P, H * NT, VD])
        mx = sb("mx", [P, NT, 2])
        nb = sb("nb", [P, NT, 2])
        z = sb("z", [P, NT, 2])
        rz = sb("rz", [P, NT, 2])
        ss = sb("ss", [P, 3, H * NT])
        S = [ps(f"a_s{m}", (P, 2 * 512)) for m in range(2)]
        TB = [ps(f"a_t{n}") for n in range(2)]
        OB = [ps(f"a_o{n}") for n in range(2)]
        names = ("zero", "qh", "s", "nb", "exp", "w", "t", "te", "o", "oe", "sq", "ss", "sd", "on", "ot", "ote",
                 "ch", "tick", "ptick")
        s = {n: sem("s_a_" + n) for n in names}
        groups = [i + 1 if i < 4 else 2 * i - 2 for i in range(NT)]
        NG = groups[-1]

        def blocks(i):
            return [range(0, min(i + 1, 4))] + ([range(4, i + 1)] if i >= 4 else [])

        def wait(eng, sm, value):
            if not isinstance(value, int) or value > 0:
                eng.wait_ge(sm, value)

        def walk(eng, steps):
            for i in range(NT):
                steps(lambda lag: (0, i - lag) if i >= lag else None)
            with eng.Fori(0, H - 1) as r:
                for i in range(NT):
                    steps(lambda lag: (r + 1, i - lag) if i >= lag else (r, NT + i - lag))
            for i in range(3):
                steps(lambda lag: (H - 1, NT + i - lag) if lag > i else None)

        with nc.Block() as block:
            @block.sync
            def _(sp):
                ahead(sp)

            @block.gpsimd
            def _(pool):
                def take(hd, i):
                    for m in range(2):
                        half = slice(QK * m, QK * m + QK)
                        src = qT[half, bass.ds(hd, 1), i * P:i * P + P].rearrange("p o n -> p (o n)")
                        last = pool.tensor_copy(qz[half, i % NQ, m, :], src)
                    last.then_inc(s["qh"], 1)

                pool.memset(qz[:], 0.0).then_inc(s["zero"], 1)
                pool.wait_ge(s["zero"], 1)
                for i in range(NT):
                    wait(pool, s["s"], 2 * (i - NQ + 1))
                    take(0, i)
                with pool.Fori(0, H - 1) as r:
                    for i in range(NT):
                        pool.wait_ge(s["s"], 2 * (r * NT + NT + i - NQ + 1))
                        pool.sem_inc(s["ptick"], 1)
                        take(r + 1, i)

            @block.tensor
            def _(pe):
                def scores(hd, i):
                    G = hd * NT + i
                    pe.wait_ge(s["qh"], G + 1)
                    for m in range(2):
                        wait(pe, s["exp"], 2 * G - 1 + m if not (isinstance(hd, int) and hd + i == 0) else 0)
                        for c in range(0, (i + 1) * P, 512):
                            n = min(512, (i + 1) * P - c)
                            pe.matmul(S[m][:, c:c + n], qz[:, i % NQ, m, :],
                                      kT[:, bass.ds(hd, 1), c:c + n].rearrange("p o n -> p (o n)"),
                                      start=True, stop=(c + n < (i + 1) * P))
                        pe.matmul(S[m][:, i * P:i * P + P], ident[:], causal[:], start=False,
                                  stop=True).then_inc(s["s"], 1)

                def turn(hd, k):
                    pe.wait_ge(s["w"], hd * NT + k + 1)
                    for g, js in enumerate(blocks(k)):
                        wait(pe, s["te"], hd * NG + (groups[k - 1] if k else 0))
                        for j in js:
                            last = pe.transpose(TB[g][:, (j - 4 * g) * P:(j - 4 * g) * P + P],
                                                w[k % 2][:, j * P:j * P + P], ident[:])
                        last.then_inc(s["t"], 1)

                def values(hd, k):
                    pe.wait_ge(s["te"], hd * NG + groups[k])
                    wait(pe, s["oe"], hd * NT + k - 1)
                    for j in range(k + 1):
                        last = pe.matmul(OB[k % 2][:, 0:VD], wT[k % 2][:, j, :],
                                         v_all[:, j, bass.ds(hd * VD, VD)], start=(j == 0), stop=(j == k))
                    last.then_inc(s["o"], 1)

                def steps(at):
                    for lag, part in ((0, scores), (2, turn), (3, values)):
                        if at(lag):
                            part(*at(lag))

                walk(pe, steps)
                for n in range(2 * H):
                    if n > 1:
                        pe.wait_ge(s["ote"], n - 1)
                    pe.wait_ge(s["on"], n + 1)
                    for j in range(4):
                        last = pe.transpose(TB[n % 2][:, j * P:j * P + P], oh[:, 4 * n + j, :], ident[:])
                    last.then_inc(s["ot"], 1)

            @block.scalar
            def _(act):
                def exps(hd, i):
                    G = hd * NT + i
                    wait(act, s["w"], G - 1)
                    for m in range(2):
                        act.wait_ge(s["nb"], 2 * G + m + 1)
                        act.activation(pm[i % 2][:, m, 0:(i + 1) * P], S[m][:, 0:(i + 1) * P], ACT.Exp,
                                       bias=nb[:, i, m:m + 1], scale=QK ** -0.5,
                                       accum_out=z[:, i, m:m + 1]).then_inc(s["exp"], 1)

                def turned(hd, k):
                    wait(act, s["o"], hd * NT + k - 1)
                    for g, js in enumerate(blocks(k)):
                        act.wait_ge(s["t"], hd * NG + groups[k] - len(blocks(k)) + g + 1)
                        act.activation(wT[k % 2][:, 4 * g:4 * g + len(js), :],
                                       TB[g][:, 0:len(js) * P].rearrange("p (j q) -> p j q", q=P),
                                       ACT.Copy).then_inc(s["te"], 1)

                def outputs(hd, k):
                    act.wait_ge(s["o"], hd * NT + k + 1)
                    act.sem_inc(s["tick"], 1)
                    act.activation(oh[:, bass.ds(hd * NT + k, 1), :].rearrange("p o d -> p (o d)"),
                                   OB[k % 2][:, 0:VD], ACT.Copy).then_inc(s["oe"], 1)

                def steps(at):
                    for lag, part in ((0, exps), (2, turned), (3, outputs)):
                        if at(lag):
                            part(*at(lag))

                walk(act, steps)
                act.wait_ge(s["oe"], H * NT)
                for n in range(H * NT):
                    last = act.activation(squares[:, n, :], oh[:, n, :], ACT.Square, accum_out=ss[:, 0, n:n + 1])
                last.then_inc(s["sq"], 1)
                act.wait_ge(s["ss"], 1)
                act.activation(ss[:, 2, :], ss[:, 1, :], ACT.Sqrt).then_inc(s["sd"], 1)
                for n in range(2 * H):
                    act.wait_ge(s["ot"], n + 1)
                    act.activation(mixA[:, n // 2, (n % 2) * 512:(n % 2) * 512 + 512], TB[n % 2][:],
                                   ACT.Copy).then_inc(s["ote"], 1)

            @block.vector
            def _(dve):
                ch = Chain(dve, s["ch"])

                def maxima(hd, i):
                    for m in range(2):
                        dve.wait_ge(s["s"], 2 * (hd * NT + i) + m + 1)
                        ch.add(dve.tensor_reduce(mx[:, i, m:m + 1], S[m][:, 0:(i + 1) * P], AX_X, ALU.max))
                        ch.sync()
                        dve.tensor_scalar(nb[:, i, m:m + 1], mx[:, i, m:m + 1], -QK ** -0.5, None,
                                          ALU.mult).then_inc(s["nb"], 1)

                def join(hd, k):
                    n = (k + 1) * P
                    dve.wait_ge(s["exp"], 2 * (hd * NT + k) + 2)
                    ch.add(dve.reciprocal(rz[:, k, :], z[:, k, :]))
                    ch.sync()
                    ch.add(dve.tensor_tensor(rz[:, k, 1:2], rz[:, k, 1:2], nlam[:], ALU.mult))
                    wait(dve, s["t"], hd * NG + groups[k - 2] if k > 1 else
                         (hd * NG + groups[k - 2 + NT] - NG if not isinstance(hd, int) or hd else 0))
                    ch.add(dve.tensor_scalar(w[k % 2][:, 0:n], pm[k % 2][:, 0, 0:n], rz[:, k, 0:1], None, ALU.mult))
                    ch.sync()
                    dve.scalar_tensor_tensor(out=w[k % 2][:, 0:n], in0=pm[k % 2][:, 1, 0:n],
                                             scalar=rz[:, k, 1:2], in1=w[k % 2][:, 0:n],
                                             op0=ALU.mult, op1=ALU.add).then_inc(s["w"], 1)

                def steps(at):
                    for lag, part in ((0, maxima), (1, join)):
                        if at(lag):
                            part(*at(lag))

                for i in range(NT):
                    steps(lambda lag: (0, i - lag) if i >= lag else None)
                ch.restart()
                with dve.Fori(0, H - 1) as r:
                    for i in range(NT):
                        steps(lambda lag: (r + 1, i - lag) if i >= lag else (r, NT + i - lag))
                    ch.restart()
                join(H - 1, NT - 1)
                dve.wait_ge(s["sq"], 1)
                dve.tensor_scalar(ss[:, 1, :], ss[:, 0, :], 1.0 / VD, EPS, ALU.mult, ALU.add).then_inc(s["ss"], 1)
                dve.wait_ge(s["sd"], 1)
                ch.add(dve.reciprocal(ss[:, 0, :], ss[:, 2, :]))
                ch.sync()
                for n in range(H * NT):
                    last = dve.scalar_tensor_tensor(out=oh[:, n, :], in0=oh[:, n, :], scalar=ss[:, 0, n:n + 1],
                                                    in1=g_row[:], op0=ALU.mult, op1=ALU.mult)
                    if n % 4 == 3:
                        last.then_inc(s["on"], 1)


class LayerNorm:

    def __init__(self, sb, sem, tag, g, b):
        self.g, self.b = g, b
        self.st = sb(tag + "_st", [P, 2, 6])
        self.mv = sb(tag + "_mv", [P, 2])
        self.sd = sb(tag + "_sd", [P, 3])
        self.s_var = sem("s_" + tag + "_var")
        self.s_sd = sem("s_" + tag + "_sd")

    def deviation(self, act, n, R):
        act.wait_ge(self.s_var, n + 1)
        act.activation(self.sd[0:R, 1:2], self.sd[0:R, 0:1], ACT.Sqrt).then_inc(self.s_sd, 1)

    def run(self, dve, ch, n, R, r):
        ch.sync()
        for h in range(2):
            ch.add(dve.bn_stats(self.st[0:R, h, :], r[0:R, h * 512:h * 512 + 512]))
        ch.sync()
        ch.add(dve.bn_aggr(self.mv[0:R, :], self.st[0:R, :, :]))
        ch.sync()
        dve.tensor_scalar(self.sd[0:R, 0:1], self.mv[0:R, 1:2], EPS, None, ALU.add).then_inc(self.s_var, 1)
        dve.wait_ge(self.s_sd, n + 1)
        ch.add(dve.reciprocal(self.sd[0:R, 2:3], self.sd[0:R, 1:2]))
        ch.sync()
        ch.add(dve.tensor_scalar(r[0:R, :], r[0:R, :], self.mv[0:R, 0:1], self.sd[0:R, 2:3],
                                 ALU.subtract, ALU.mult))
        ch.sync()
        ch.add(dve.tensor_tensor(r[0:R, :], r[0:R, :], self.g[0:R, :], ALU.mult))
        ch.sync()
        return dve.tensor_tensor(r[0:R, :], r[0:R, :], self.b[0:R, :], ALU.add)


def mix_matmul(pe, banks, mc, w_out, R):
    for h in range(2):
        for k in range(KC):
            last = pe.matmul(banks[h][0:R, :], mc[:, k, 0:R], w_out[:, k, h * 512:h * 512 + 512],
                             start=(k == 0), stop=(k == KC - 1))
    return last


def prompt_mix(nc, a, maker, mixA, mixR, x1_d, w_out, g1, b1, s_wo, ahead):
    with ExitStack() as ctx:
        sb, ps, sem = maker(ctx)
        mc = [sb(f"mc{n}", [P, KC, P]) for n in range(2)]
        res = [sb(f"res{n}", [P, D]) for n in range(2)]
        B = [[ps(f"m_b{n}{h}") for h in range(2)] for n in range(2)]
        ln = LayerNorm(sb, sem, "ln1", g1, b1)
        s_res = [sem(f"s_m_res{n}") for n in range(2)]
        s_st = [sem(f"s_m_st{n}") for n in range(2)]
        names = ("c", "mm", "sum", "x1", "ch", "tick")
        s = {n: sem("s_m_" + n) for n in names}
        with nc.Block() as block:
            @block.sync
            def _(sp):
                for n in range(2):
                    sp.dma_start(res[n][:], rows(a["x_prompt"], n * P, P)).then_inc(s_res[n], 16)

                ahead(sp)

                def store(g, n):
                    sp.wait_ge(s["x1"], 2 * g + n + 1)
                    sp.dma_start(rows(x1_d, (2 * g + n) * P, P), res[n][:]).then_inc(s_st[n], 16)
                    sp.wait_ge(s_st[n], 16 * g + 16)

                with sp.Fori(0, NT // 2 - 1) as g:
                    for n in range(2):
                        store(g, n)
                        sp.dma_start(res[n][:], rows(a["x_prompt"], (2 * g + 2 + n) * P, P)).then_inc(s_res[n], 16)
                for n in range(2):
                    store(NT // 2 - 1, n)

            def pairs(eng, tile):
                for n in range(2):
                    tile(n, n)
                with eng.Fori(0, NT // 2 - 1) as r:
                    for n in range(2):
                        tile(2 * r + 2 + n, n)

            @block.gpsimd
            def _(pool):
                def tile(T, n):
                    if not isinstance(T, int):
                        pool.wait_ge(s["mm"], T - 1)
                        pool.sem_inc(s["tick"], 1)
                    at = T * P
                    pool.tensor_copy(mc[n][:, 0:H, :], mixA[:, :, bass.ds(at, P)])
                    pool.tensor_copy(mc[n][:, H:KC, :], mixR[:, :, bass.ds(at, P)]).then_inc(s["c"], 1)

                pairs(pool, tile)

            @block.tensor
            def _(pe):
                def tile(T, n):
                    pe.wait_ge(s["c"], T + 1)
                    if not isinstance(T, int):
                        pe.wait_ge(s["sum"], T - 1)
                    mix_matmul(pe, B[n], mc[n], w_out, P).then_inc(s["mm"], 1)

                pe.wait_ge(s_wo, 16 * (KC + 2))
                pairs(pe, tile)

            @block.scalar
            def _(act):
                pairs(act, lambda T, n: ln.deviation(act, T, P))

            @block.vector
            def _(dve):
                ch = Chain(dve, s["ch"])
                dve.wait_ge(s_wo, 16 * (KC + 2))
                with dve.Fori(0, NT // 2) as g:
                    for n in range(2):
                        dve.wait_ge(s_res[n], 16 * g + 16)
                        dve.wait_ge(s["mm"], 2 * g + n + 1)
                        for h in range(2):
                            part = res[n][:, h * 512:h * 512 + 512]
                            last = dve.scalar_tensor_tensor(out=part, in0=part, scalar=ALPHA, in1=B[n][h][:],
                                                            op0=ALU.mult, op1=ALU.add)
                            if h == 0:
                                ch.add(last)
                        last.then_inc(s["sum"], 1)
                        dve.wait_ge(s["sum"], 2 * g + n + 1)
                        ln.run(dve, ch, 2 * g + n, P, res[n]).then_inc(s["x1"], 1)
                    ch.restart()


def peer(nc, a, o, maker, ident, cbase, smask, hmask, g_row, qTs, kTs, mixS, x1_d, ffn_d, wq, s_wq):
    NU, NV, ND = 4, 8, 4
    PES, DVS = (0, 2, 4, 6), (1, 3, 5, 7)
    NPE, NDV = 2 * len(PES), 2 * len(DVS)
    CP = ((0, 2, 16), (2, 5, 5), (5, 16, 2))
    NC = sum((a1 - a0) * b for a0, a1, b in CP)
    GP = 4
    NG = NPG // GP
    KEYS = PAST + DS
    with ExitStack() as ctx:
        sb, ps, sem = maker(ctx)
        keysT = sb("keysT", [P, 2 * PH, PK])
        u = [sb(f"u{n}", [P, D]) for n in range(NU)]
        v = [sb(f"v{n}", [P, D]) for n in range(NV)]
        x_cur, x1n, facc = sb("x_cur", [P, D]), sb("x1n", [P, D]), sb("facc", [P, D])
        x1T = sb("x1T", [P, KC, P])
        q_sb, qTt, sc, sc2 = sb("q_sb", [P, 2, P]), sb("qTt", [P, 2, P]), sb("sc", [P, 2, PK]), sb("sc2", [P, 2, PK])
        tv, ti, tif = sb("tv", [P, 2, TOPK]), sb("ti", [P, 2, TOPK], U32), sb("tif", [P, 2, TOPK])
        cand, cand2, cidx = sb("cand", [P, NC]), sb("cand2", [P, NC]), sb("cidx", [P, NC])
        ts, tpos, tposf = sb("ts", [P, TOPK]), sb("tpos", [P, TOPK], U32), sb("tposf", [P, TOPK])
        eq, eidx = sb("eq", [P, TOPK, NC]), sb("eidx", [P, TOPK])
        iota = sb("iota", [P, NC])
        nts, ex, zx = sb("nts", [P, 1]), sb("ex", [P, TOPK]), sb("zx", [P, 2])
        idx_all = sb("idx_all", [P, PH, TOPK], I32)
        gt_all = sb("gt_all", [P, PH, TOPK])
        idxU = [sb(f"idxU{n}", [P, TOPK], I32) for n in range(2)]
        idxV = [sb(f"idxV{n}", [P, TOPK], I32) for n in range(2)]
        gt = [sb(f"gt{n}", [P, TOPK]) for n in range(2)]
        act16 = [sb(f"act{n}", [P, TOPK]) for n in range(2)]
        gi = sb("gi", [P, TOPK])
        w16 = [sb(f"w16{n}", [P, TOPK]) for n in range(2)]
        diag = [sb(f"diag{n}", [P, P]) for n in range(ND)]
        w_out = sb("w_out_s", [P, KC, D])
        flat = w_out[:].rearrange("p k n -> p (k n)")
        room = [0]

        def carve(shape):
            n = math.prod(shape[1:])
            part = flat[0:shape[0], room[0]:room[0] + n]
            room[0] += n
            return part if len(shape) == 2 else part.rearrange("p (a b) -> p a b", a=shape[1])

        pg = [carve([P, GP, AW]) for n in range(2)]
        kTp = carve([P, H, GP * P])
        qst = carve([P, H, SR])
        wTs = carve([P, GP * H * DS])
        wTn = carve([DS, H * DS])
        vnew = carve([DS, AW])
        oS = carve([H * DS, DB, VD])
        pt = sb("pt", [1, DB * NPG], I32)
        S = sb("S", [SR, KEYS])
        g1, b1 = S[:, 0:D], S[:, D:2 * D]
        sm = sb("sm", [SR, 4])
        cj = sb("cj", [SR, H * DS])
        om = sb("om", [H * DS, VD])
        rs = sb("rs", [H * DS, 3, DB])
        ln = LayerNorm(sb, sem, "ln1s", g1, b1)
        wg = wq[:, :, 0:D]
        wp = wq[:, 0:2, D:2 * D]
        g2, b2, gb = [wq[:, n, D:2 * D] for n in range(2, 5)]
        room[0] = 0
        x2 = [carve([P, D]) for n in range(2)]
        f = [carve([P, D]) for n in range(2)]
        pr = [carve([P, PLE]) for n in range(2)]
        x2T, prT = carve([P, KC, P]), carve([P, PLE // P, P])
        ln2 = LayerNorm(sb, sem, "ln2", g2, b2)
        ident2 = sb("ident2", [P, SR])
        B = [ps(f"e_b{n}") for n in range(8)]
        ACC, QB, TB, KB, SB_, OB = B[0:2], B[2], B[3], B[4:6], B[6], B[7]
        s_u = [sem(f"s_u{n}") for n in range(NU)]
        s_v = [sem(f"s_v{n}") for n in range(NV)]
        s_pg = [sem(f"s_pg{n}") for n in range(2)]
        s_in = [sem(f"s_in{n}") for n in range(2)]
        s_st = [sem(f"s_st{n}") for n in range(2)]
        names = ("kr", "kt", "kte", "zero", "x1n", "xt", "xTa", "xTd", "q", "qe", "qt", "qTe", "sc", "sce",
                 "tk", "ts", "ex", "prepU", "prepV", "ufree", "vpe", "vdve", "gi", "th", "w", "diag", "xcur",
                 "acc", "fo", "fst", "pt", "pgfree", "ktp", "ktpe", "S", "Se", "qst", "sn", "mx", "sx", "cj",
                 "wt", "wte", "wn", "wne", "vn", "O", "Oe", "ch", "tick", "atick", "ptick", "stick", "dtick",
                 "half", "xh", "fs", "wo", "mm", "sum", "nsq", "nsd", "on", "ot", "x1", "xg", "xst", "gb", "w2", "x2", "pp", "pT", "tp",
                 "xT", "z", "l", "zr", "lr", "tg", "y")
        s = {n: sem("s_e_" + n) for n in names}


        def keys_turn_pe(pe, n, R):
            pe.wait_ge(s["x1n"], 16 * n + 16)
            pe.wait_ge(s["sce"], PH * n)
            pe.wait_ge(s["qTe"], PH * n)
            for half, bank in enumerate((QB, TB)):
                for c in range(4):
                    k = 4 * half + c
                    last = pe.transpose(bank[:, c * P:c * P + R], x1n[0:R, k * P:k * P + P], ident[0:R, 0:R])
                last.then_inc(s["xt"], 1)

        def turned(bank, R):
            return bank[:].rearrange("p (c t) -> p c t", c=4)[:, :, 0:R]

        def keys_turn_act(act, n, R):
            act.wait_ge(s["q"], PH * n)
            act.wait_ge(s["xt"], 2 * n + 1)
            act.activation(x1T[:, 0:4, 0:R], turned(QB, R), ACT.Copy).then_inc(s["xTa"], 1)

        def keys_turn_dve(dve, n, R):
            dve.wait_ge(s["q"], PH * n)
            dve.wait_ge(s["xt"], 2 * n + 2)
            dve.tensor_copy(x1T[:, 4:8, 0:R], turned(TB, R)).then_inc(s["xTd"], 1)

        def keys_q_pe(pe, n, h, R):
            if h == 0:
                pe.wait_ge(s["xTa"], n + 1)
                pe.wait_ge(s["xTd"], n + 1)
            pe.wait_ge(s["sce"], PH * n + h)
            for k in range(KC):
                last = pe.matmul(QB[0:R, 0:2 * P], x1T[:, k, 0:R], wq[:, k, 2 * P * h:2 * P * h + 2 * P],
                                 start=(k == 0), stop=(k == KC - 1))
            last.then_inc(s["q"], 1)

        def keys_q_act(act, n, h, R):
            act.wait_ge(s["qt"], PH * n + h)
            act.wait_ge(s["q"], PH * n + h + 1)
            act.activation(q_sb[0:R, :, :], QB[0:R, 0:2 * P].rearrange("p (a d) -> p a d", a=2),
                           ACT.Copy).then_inc(s["qe"], 1)

        def keys_t_pe(pe, n, h, R):
            pe.wait_ge(s["qTe"], PH * n + h)
            pe.wait_ge(s["qe"], PH * n + h + 1)
            for m in range(2):
                last = pe.transpose(TB[:, m * P:m * P + R], q_sb[0:R, m, :], ident[0:R, 0:R])
            last.then_inc(s["qt"], 1)

        def keys_t_act(act, n, h, R):
            act.wait_ge(s["sc"], PH * n + h)
            act.wait_ge(s["qt"], PH * n + h + 1)
            act.activation(qTt[:, :, 0:R], TB[:, 0:2 * P].rearrange("p (a t) -> p a t", a=2)[:, :, 0:R],
                           ACT.Copy).then_inc(s["qTe"], 1)

        def keys_s_pe(pe, n, h, R):
            pe.wait_ge(s["qTe"], PH * n + h + 1)
            for m in range(2):
                last = pe.matmul(QB[0:R, 2 * P + m * PK:2 * P + m * PK + PK], qTt[:, m, 0:R], keysT[:, 2 * h + m, :],
                                 start=True, stop=True)
            last.then_inc(s["sc"], 1)

        def keys_s_act(act, n, h, R):
            act.wait_ge(s["tk"], PH * n + h)
            act.wait_ge(s["sc"], PH * n + h + 1)
            act.activation(sc[0:R, :, :], QB[0:R, 2 * P:4 * P].rearrange("p (a d) -> p a d", a=2),
                           ACT.Copy).then_inc(s["sce"], 1)

        def top16(ch, dve, R, src, spare, vals, pos):
            ch.add(dve.max(vals[:, 0:8], src))
            ch.sync()
            ch.add(dve.max_index(pos[:, 0:8], vals[:, 0:8], src))
            ch.add(dve.match_replace(spare, vals[:, 0:8], src, -3e38))
            ch.sync()
            ch.add(dve.max(vals[:, 8:16], spare))
            ch.sync()
            ch.add(dve.max_index(pos[:, 8:16], vals[:, 8:16], spare))

        def keys_rank_dve(dve, ch, n, h, R, m):
            if m == 0:
                dve.wait_ge(s["sce"], PH * n + h + 1)
                dve.sem_inc(s["dtick"], 1)
            top16(ch, dve, R, sc[0:R, m, :], sc2[0:R, m, :], tv[0:R, m, :], ti[0:R, m, :])

        def keys_pairs_dve(dve, ch, n, h, R):
            ch.sync()
            ch.add(dve.tensor_copy(tif[0:R], ti[0:R]))
            ch.sync()
            at = 0
            for a0, a1, b in CP:
                shape = [R, a1 - a0, b]
                out = lambda x: x[0:R, at:at + (a1 - a0) * b].rearrange("p (a b) -> p a b", b=b)
                row = lambda x: x[0:R, 0, a0:a1].unsqueeze(2).to_broadcast(shape)
                col = lambda x: x[0:R, 1, 0:b].unsqueeze(1).to_broadcast(shape)
                ch.add(dve.tensor_tensor(out(cand), row(tv), col(tv), ALU.add))
                ch.add(dve.scalar_tensor_tensor(out=out(cidx), in0=row(tif), scalar=float(PK), in1=col(tif),
                                                op0=ALU.mult, op1=ALU.add))
                at += (a1 - a0) * b
            ch.sync()
            top16(ch, dve, R, cand[0:R], cand2[0:R], ts[0:R], tpos[0:R])
            dve.wait_ge(s["ex"], PH * n + h)
            dve.tensor_scalar(nts[0:R], ts[0:R, 0:1], -1.0, None, ALU.mult).then_inc(s["ts"], 1)
            ch.sync()
            ch.add(dve.tensor_copy(tposf[0:R], tpos[0:R]))
            ch.sync()
            shape = [R, TOPK, NC]
            ch.add(dve.tensor_tensor(eq[0:R], iota[0:R].unsqueeze(1).to_broadcast(shape),
                                     tposf[0:R].unsqueeze(2).to_broadcast(shape), ALU.is_equal))
            ch.sync()
            ch.add(dve.tensor_tensor(eq[0:R], eq[0:R], cidx[0:R].unsqueeze(1).to_broadcast(shape), ALU.mult))
            ch.sync()
            ch.add(dve.tensor_reduce(eidx[0:R], eq[0:R], AX_X, ALU.add))
            ch.sync()
            ch.add(dve.tensor_copy(idx_all[0:R, h, :], eidx[0:R]))

        def keys_gate_act(act, n, h, R):
            act.wait_ge(s["ts"], PH * n + h + 1)
            act.activation(ex[0:R], ts[0:R], ACT.Exp, bias=nts[0:R], accum_out=zx[0:R, 0:1]).then_inc(s["ex"], 1)

        def keys_gate_dve(dve, ch, n, h, R):
            dve.wait_ge(s["ex"], PH * n + h + 1)
            ch.add(dve.reciprocal(zx[0:R, 1:2], zx[0:R, 0:1]))
            ch.sync()
            dve.tensor_scalar(gt_all[0:R, h, :], ex[0:R], zx[0:R, 1:2], 0.5, ALU.mult, ALU.mult).then_inc(s["tk"], 1)


        HS = PH * SR // P

        def heads_of(t):
            return HS if isinstance(t, int) and t == NT else PH

        def u_ready(k, j):
            return s_u[j % NU], 16 * (k * (TOPK // NU) + j // NU + 1)

        def v_ready(k, j):
            return s_v[j % NV], 16 * (k * (TOPK // NV) + j // NV + 1)

        def nth(k, j, slots):
            n = len(slots)
            return k * 2 * n + (j // NV) * n + slots.index(j % NV)

        def step_pool(pool, U, V):
            for j in range(TOPK):
                if U:
                    t, k, h = U
                    if j == 0:
                        pool.wait_ge(s["prepU"], k + 1)
                    pool.wait_ge(s["ufree"], k * TOPK + j + 1)
                    pool.sem_inc(s["ptick"], 1)
                    pool.indirect_dma_start(u[j % NU][:], None, a["peer_u"],
                                            bass.IndirectOffsetOnAxis(ap=idxU[h % 2][:, j:j + 1], axis=0)
                                            ).then_inc(s_u[j % NU], 16)
                if V:
                    t, k, g = V
                    if j == 0:
                        pool.wait_ge(s["prepV"], k + 1)
                    name, slots = ("vpe", PES) if j % NV in PES else ("vdve", DVS)
                    pool.wait_ge(s[name], nth(k, j, slots) + 1)
                    pool.sem_inc(s["ptick"], 1)
                    pool.indirect_dma_start(v[j % NV][:], None, a["peer_v"],
                                            bass.IndirectOffsetOnAxis(ap=idxV[g % 2][:, j:j + 1], axis=0)
                                            ).then_inc(s_v[j % NV], 16)

        def step_pe(pe, U, V, side):
            for j in range(TOPK):
                if V and j % NV in PES:
                    t, k, g = V
                    c = nth(k, j, PES)
                    sample = heads_of(t) == HS
                    R = SR if sample else P
                    first, end = g == 0 and j == 0, g == PH - 1 and j == NV + PES[-1]
                    if first:
                        pe.wait_ge(s["fo"], t)
                    pe.wait_ge(*v_ready(k, j))
                    pe.wait_ge(s["diag"], c + 1)
                    for b in range(2):
                        last = pe.matmul(ACC[b][0:R, :], diag[nth(g, j, PES) % ND][:, 0:R],
                                         v[j % NV][:, b * 512:b * 512 + 512], start=first, stop=end)
                    last.then_inc(s["vpe"], 1)
                side(j)
            if V and heads_of(V[0]) == HS and V[2] == HS - 1:
                pe.wait_ge(s["vdve"], (V[1] + 1) * NDV + len(DVS))
                for b in range(2):
                    last = pe.matmul(ACC[b][0:SR, :], ident2[:], facc[:, b * 512:b * 512 + 512],
                                     start=False, stop=True)
                last.then_inc(s["fs"], 1)

        def step_act(act, U, V, side):
            if U and U[2] == 0 and not (isinstance(U[0], int) and U[0] == 0):
                act.wait_ge(s["ufree"], U[1] * TOPK + NU)
                act.wait_ge(s["x1n"], 16 * U[0] + 16)
                if heads_of(U[0]) == HS:
                    act.wait_ge(s["xh"], 16)
                act.sem_inc(s["atick"], 1)
                act.activation(x_cur[:], x1n[:], ACT.Copy).then_inc(s["xcur"], 1)
            for j in range(TOPK):
                if V and j % NV in PES:
                    t, k, g = V
                    c = nth(k, j, PES)
                    of = ident2[:] if heads_of(t) == HS else ident[:]
                    if j == 0:
                        act.wait_ge(s["w"], k + 1)
                    act.wait_ge(s["vpe"], c + len(PES) - ND + 1)
                    act.activation(diag[nth(g, j, PES) % ND][:, 0:of.shape[1]], of, ACT.Copy,
                                   scale=w16[g % 2][:, j:j + 1]).then_inc(s["diag"], 1)
                side(j)
                if U and j == TOPK - 1:
                    act.wait_ge(s["gi"], U[1] + 1)
                    act.activation(gi[:], gi[:], ACT.Tanh, scale=GELU_B).then_inc(s["th"], 1)

        def step_dve(dve, ch, U, V, side):
            if U and U[2] == 0:
                dve.wait_ge(s["xcur"], U[0] + 1)
            for j in range(TOPK):
                if U:
                    t, k, h = U
                    dve.wait_ge(*u_ready(k, j))
                    dve.tensor_tensor_reduce(u[j % NU][:], u[j % NU][:], x_cur[:], 1.0, 0.0, ALU.mult,
                                             ALU.add, act16[h % 2][:, j:j + 1]).then_inc(s["ufree"], 1)
                if V and j % NV in DVS:
                    t, k, g = V
                    first = g == 0 and j == DVS[0]
                    if first:
                        dve.wait_ge(s["fst"], 16 * t)
                    dve.wait_ge(s["vdve"], nth(k, j, DVS) + len(DVS))
                    dve.wait_ge(*v_ready(k, j))
                    w = w16[g % 2][:, j:j + 1]
                    if first:
                        last = dve.tensor_scalar(facc[:], v[j % NV][:], w, None, ALU.mult)
                    else:
                        last = dve.scalar_tensor_tensor(out=facc[:], in0=v[j % NV][:], scalar=w,
                                                        in1=facc[:], op0=ALU.mult, op1=ALU.add)
                    last.then_inc(s["vdve"], 1)
                if U and j == 2:
                    t, k, h = U
                    if V:
                        dve.wait_ge(s["vpe"], V[1] * NPE + len(PES))
                    heads = heads_of(t)
                    if h == 0:
                        dve.wait_ge(s["tk"], PH * t + PH)
                        if heads == HS:
                            dve.wait_ge(s["half"], 32 * HS)
                    if h == heads - 1 and heads == PH:
                        dve.wait_ge(s["tk"], PH * t + PH + 1)
                        if isinstance(t, int) and t == NT - 1:
                            dve.wait_ge(s["half"], 32)
                    if h < heads - 1 or heads == PH:
                        dve.tensor_copy(idxU[(h + 1) % 2][:], idx_all[:, (h + 1) % PH, :]).then_inc(s["prepU"], 1)
                    dve.tensor_copy(idxV[h % 2][:], idx_all[:, h, :]).then_inc(s["prepV"], 1)
                    ch.add(dve.tensor_copy(gt[h % 2][:], gt_all[:, h, :]))
                    ch.sync()
                if U and j == TOPK - 1:
                    t, k, h = U
                    A = act16[h % 2][:]
                    dve.wait_ge(s["ufree"], k * TOPK + TOPK + NU)
                    ch.add(dve.tensor_tensor(gi[:], A, A, ALU.mult))
                    ch.sync()
                    ch.add(dve.tensor_scalar(gi[:], gi[:], GELU_A, 1.0, ALU.mult, ALU.add))
                    ch.sync()
                    dve.tensor_tensor(gi[:], gi[:], A, ALU.mult).then_inc(s["gi"], 1)
                side(j)
                if U and j == TOPK - 1:
                    t, k, h = U
                    W = w16[h % 2][:]
                    if V:
                        dve.wait_ge(s["diag"], V[1] * NPE)
                    dve.wait_ge(s["th"], k + 1)
                    ch.add(dve.scalar_tensor_tensor(out=W, in0=gi[:], scalar=1.0, in1=act16[h % 2][:],
                                                    op0=ALU.add, op1=ALU.mult))
                    ch.sync()
                    dve.tensor_tensor(W, W, gt[h % 2][:], ALU.mult).then_inc(s["w"], 1)
                    dve.wait_ge(s["w"], k + 1)
            if V and V[2] == heads_of(V[0]) - 1:
                t, k, g = V
                if heads_of(t) == PH:
                    dve.wait_ge(s["vpe"], (k + 1) * NPE + len(PES))
                    dve.wait_ge(s["vdve"], (k + 1) * NDV + len(DVS))
                    for b in range(2):
                        part = facc[:, b * 512:b * 512 + 512]
                        last = dve.tensor_tensor(part, ACC[b][:], part, ALU.add)
                    last.then_inc(s["fo"], 1)

        def experts(step, turn, side_first, side_loop, side_sample, side_out):
            K = PH
            at = lambda side, h: (lambda j: side(h, j))
            step((0, 0, 0), None, at(side_first, 0))

            def steps(t, to, this, following):
                for h in range(1, PH):
                    step((t, t * K + h, h), (t, t * K + h - 1, h - 1), at(this, h))
                step((to, t * K + K, 0), (t, t * K + K - 1, K - 1), at(following, 0))

            turn(lambda i: steps(i, i + 1, side_loop(i + 1), side_loop(i + 2)))
            steps(NT - 2, NT - 1, side_loop(NT - 1), side_sample)
            steps(NT - 1, NT, side_sample, side_out)
            for h in range(1, HS + 1):
                step((NT, NT * K + h, h) if h < HS else None, (NT, NT * K + h - 1, h - 1), at(side_out, h))


        def pages(sp, i, store=None):
            sp.wait_ge(s["O"], i)
            sp.sem_inc(s["stick"], 1)
            sp.dma_start(vnew[:], rows(o["v_sample"], i * DS, DS)).then_inc(s["vn"], 16)
            for G in range(2 * NG):
                src = a["cache_k"] if G < NG else a["cache_v"]
                if G == 3 and store:
                    store()
                sp.wait_ge(s["pgfree"], i * 2 * NG + max(G - 1, 0))
                sp.sem_inc(s["stick"], 1)
                for n in range(GP):
                    page = sp.value_load(pt[0:1, bass.ds(i * NPG + (G % NG) * GP + n, 1)], min_val=0,
                                         max_val=src.shape[0] // PAGE - 1)
                    sp.dma_start(pg[G % 2][:, n, :], src[bass.ds(page * PAGE, PAGE), :]).then_inc(s_pg[G % 2], 16)

        def queries_act(act, i):
            act.wait_ge(s["S"], i * (NG + 1))
            act.sem_inc(s["atick"], 1)
            for h in range(H):
                for m in range(2):
                    half = slice(QK * m, QK * m + QK)
                    last = act.activation(qst[half, h, (2 * h + m) * DS:(2 * h + m + 1) * DS],
                                          qTs[half, h, bass.ds(i * DS, DS)], ACT.Copy)
            last.then_inc(s["qst"], 1)

        def page_turn_pe(pe, i, g, n):
            if n == 0:
                pe.wait_ge(s_pg[g % 2], 16 * GP * (i * NG + g // 2 + 1))
            c = g * GP + n
            pe.wait_ge(s["ktpe"], i * NPG + max(c - 1, 0))
            for h in range(H):
                last = pe.transpose(KB[c % 2][:, h * P:h * P + P], pg[g % 2][:, n, h * VD:h * VD + VD], ident[:])
            last.then_inc(s["ktp"], 1)

        def page_turn_act(act, i, g, n):
            c = g * GP + n
            if n == 0:
                act.wait_ge(s["S"], i * (NG + 1) + g)
            act.wait_ge(s["ktp"], i * NPG + c + 1)
            act.activation(kTp[:, :, n * P:n * P + P], KB[c % 2][:].rearrange("p (h t) -> p h t", h=H),
                           ACT.Copy).then_inc(s["ktpe"], 1)

        def scores_pe(pe, i, g):
            pe.wait_ge(s["ktpe"], i * NPG + (g + 1) * GP)
            if g == 0:
                pe.wait_ge(s["qst"], i + 1)
                pe.wait_ge(s["sn"], i)
            pe.wait_ge(s["Se"], i * NG + g)
            for h in range(H):
                last = pe.matmul(SB_[0:SR, :], qst[:, h, :], kTp[:, h, :], start=(h == 0), stop=(h == H - 1))
            last.then_inc(s["S"], 1)
            pe.wait_ge(s["S"], i * (NG + 1) + g + 1)
            pe.sem_inc(s["pgfree"], 1)

        def scores_act(act, i, g):
            if g == 0:
                act.wait_ge(s["O"], i)
            act.wait_ge(s["S"], i * (NG + 1) + g + 1)
            act.activation(S[:, g * GP * P:(g + 1) * GP * P], SB_[0:SR, :], ACT.Copy).then_inc(s["Se"], 1)

        def new_keys_pe(pe, i):
            pe.wait_ge(s["Se"], i * NG + NG)
            for h in range(H):
                last = pe.matmul(SB_[0:SR, 0:DS], qst[:, h, :], kTs[:, h, bass.ds(i * DS, DS)],
                                 start=(h == 0), stop=(h == H - 1))
            last.then_inc(s["S"], 1)

        def new_keys_dve(dve, i):
            dve.wait_ge(s["S"], i * (NG + 1) + NG + 1)
            dve.tensor_tensor(S[:, PAST:KEYS], SB_[0:SR, 0:DS], smask[:], ALU.add).then_inc(s["sn"], 1)

        def softmax_dve(dve, ch, i, part):
            if part == 0:
                dve.wait_ge(s["Se"], i * NG + NG)
                dve.wait_ge(s["sn"], i + 1)
                ch.add(dve.tensor_reduce(sm[:, 0:1], S[:], AX_X, ALU.max))
                ch.sync()
                dve.tensor_scalar(sm[:, 1:2], sm[:, 0:1], -QK ** -0.5, None, ALU.mult).then_inc(s["mx"], 1)
            else:
                dve.wait_ge(s["sx"], i + 1)
                ch.add(dve.reciprocal(sm[:, 3:4], sm[:, 2:3]))
                ch.sync()
                dve.tensor_scalar(cj[:], cbase[:], sm[:, 3:4], None, ALU.mult).then_inc(s["cj"], 1)

        def softmax_act(act, i):
            act.wait_ge(s["mx"], i + 1)
            act.activation(S[:], S[:], ACT.Exp, bias=sm[:, 1:2], scale=QK ** -0.5,
                           accum_out=sm[:, 2:3]).then_inc(s["sx"], 1)

        def weights_pe(pe, i, g):
            if g == 0:
                pe.wait_ge(s["cj"], i + 1)
                pe.wait_ge(s["ktpe"], i * NPG + NPG)
                pe.sem_inc(s["tick"], 1)
                pe.matmul(SB_[0:DS, 0:H * DS], S[:, PAST:KEYS], cj[:], start=True, stop=True).then_inc(s["wn"], 1)
            pe.wait_ge(s["wte"], i * NG + g)
            pe.sem_inc(s["tick"], 1)
            for n in range(GP):
                c = (g * GP + n) * P
                last = pe.matmul(KB[0][:, n * H * DS:(n + 1) * H * DS], S[:, c:c + P], cj[:], start=True, stop=True)
            last.then_inc(s["wt"], 1)

        def weights_act(act, i, g):
            if g == 0:
                act.wait_ge(s["wn"], i + 1)
                act.activation(wTn[:], SB_[0:DS, 0:H * DS], ACT.Copy).then_inc(s["wne"], 1)
            act.wait_ge(s["pgfree"], i * 2 * NG + NG + g)
            act.wait_ge(s["wt"], i * NG + g + 1)
            act.activation(wTs[:], KB[0][:, 0:GP * H * DS], ACT.Copy).then_inc(s["wte"], 1)

        def values_pe(pe, i, g):
            if g == 0:
                pe.wait_ge(s["Oe"], i)
                pe.wait_ge(s["wne"], i + 1)
                pe.wait_ge(s["vn"], 16 * i + 16)
                pe.sem_inc(s["tick"], 1)
                pe.matmul(OB[0:H * DS, :], wTn[:], vnew[:], start=True, stop=False)
            pe.wait_ge(s["wte"], i * NG + g + 1)
            pe.wait_ge(s_pg[g % 2], 16 * GP * (i * NG + NG // 2 + g // 2 + 1))
            for n in range(GP):
                last = pe.matmul(OB[0:H * DS, :], wTs[:, n * H * DS:(n + 1) * H * DS], pg[g % 2][:, n, :],
                                 start=False, stop=(g == NG - 1 and n == GP - 1))
            last.then_inc(s["pgfree"], 1)
            if g == NG - 1:
                pe.wait_ge(s["pgfree"], (i + 1) * 2 * NG)
                pe.sem_inc(s["O"], 1)

        def heads_dve(dve, ch, i):
            dve.wait_ge(s["O"], i + 1)
            head = lambda h: OB[0:H * DS, h * VD:h * VD + VD]
            ch.sync()
            ch.add(dve.tensor_scalar(om[:], head(0), hmask[:, 0:1], None, ALU.mult))
            for h in range(1, H):
                ch.sync()
                last = dve.scalar_tensor_tensor(out=om[:], in0=head(h), scalar=hmask[:, h:h + 1], in1=om[:],
                                                op0=ALU.mult, op1=ALU.add)
                if h < H - 1:
                    ch.add(last)
            last.then_inc(s["Oe"], 1)
            dve.wait_ge(s["Oe"], i + 1)
            ch.add(dve.tensor_copy(oS[:, bass.ds(i, 1), :].rearrange("p o d -> p (o d)"), om[:]))

        TURNS = {0: (0, 0), 1: (0, 1), 2: (0, 2), 3: (0, 3), 7: (1, 0), 9: (1, 1), 10: (1, 2), 11: (1, 3)}

        def side_pe(pe, i):
            def side(h, j):
                if h == 0 and j == 3:
                    keys_turn_pe(pe, i, P)
                if j == 4:
                    keys_q_pe(pe, i, h, P)
                if j == 6:
                    keys_t_pe(pe, i, h, P)
                if j == 8:
                    keys_s_pe(pe, i, h, P)
                if h < NG // 2:
                    if j in TURNS:
                        page_turn_pe(pe, i, 2 * h + TURNS[j][0], TURNS[j][1])
                    if j in (5, 13):
                        scores_pe(pe, i, 2 * h + j // 8)
                    if h == NG // 2 - 1 and j == 14:
                        new_keys_pe(pe, i)
                else:
                    g = 2 * (h - NG // 2)
                    if j in (7, 12):
                        weights_pe(pe, i, g + j // 9)
                    if j in (9, 14):
                        values_pe(pe, i, g + j // 12)
            return side

        def side_act(act, i):
            def side(h, j):
                if h == 0 and j == 0:
                    queries_act(act, i)
                if h == 0 and j == 3:
                    keys_turn_act(act, i, P)
                if j == 4:
                    keys_q_act(act, i, h, P)
                if j == 6:
                    keys_t_act(act, i, h, P)
                if j == 8:
                    keys_s_act(act, i, h, P)
                if j == 14:
                    keys_gate_act(act, i, h, P)
                if h < NG // 2:
                    if j in TURNS:
                        page_turn_act(act, i, 2 * h + TURNS[j][0], TURNS[j][1])
                    if j in (5, 13):
                        scores_act(act, i, 2 * h + j // 8)
                else:
                    g = 2 * (h - NG // 2)
                    if h == NG // 2 and j == 1:
                        softmax_act(act, i)
                    if j in (7, 12):
                        weights_act(act, i, g + j // 9)
            return side

        def side_dve(dve, ch, i):
            def side(h, j):
                if h == 0 and j == 3:
                    keys_turn_dve(dve, i, P)
                if j == 9:
                    keys_rank_dve(dve, ch, i, h, P, 0)
                if j == 11:
                    keys_rank_dve(dve, ch, i, h, P, 1)
                if j == 13:
                    keys_pairs_dve(dve, ch, i, h, P)
                if j == 15:
                    keys_gate_dve(dve, ch, i, h, P)
                if h == NG // 2 - 1 and j == 14:
                    new_keys_dve(dve, i)
                if h == NG // 2 and j == 0:
                    softmax_dve(dve, ch, i, 0)
                if h == NG // 2 and j == 4:
                    softmax_dve(dve, ch, i, 1)
                if h == PH - 1 and j == 15:
                    heads_dve(dve, ch, i)
            return side

        KEYS_AT = {0: "q", 1: "t", 2: "s", 3: "rank0", 4: "rank1", 5: "pairs", 6: "exp", 7: "gate"}
        MIX_AT = 2

        def sample_pe(pe):
            def side(h, j):
                if h == 0 and j == 0:
                    pe.wait_ge(s["on"], 1)
                    for b in range(DB):
                        last = pe.transpose(SB_[:, b * H * DS:(b + 1) * H * DS], oS[:, b, :],
                                            ident[0:H * DS, 0:H * DS])
                    last.then_inc(s["ot"], 1)
                if h == MIX_AT and j == 0:
                    pe.wait_ge(s["sum"], 1)
                    pe.wait_ge(s["wo"], 16 * KC)
                    mix_matmul(pe, KB, mixS, w_out, SR).then_inc(s["mm"], 1)
                if h == 4 and j == 0:
                    keys_turn_pe(pe, NT, SR)
                if 4 <= h < PH:
                    step, k = KEYS_AT[j % 8], 2 * (h - 4) + j // 8
                    if step == "q":
                        keys_q_pe(pe, NT, k, SR)
                    if step == "t":
                        keys_t_pe(pe, NT, k, SR)
                    if step == "s":
                        keys_s_pe(pe, NT, k, SR)
            return side

        def sample_act(act):
            def side(h, j):
                if h == 0 and j == 0:
                    act.wait_ge(s["nsq"], 1)
                    act.activation(rs[:, 1, :], rs[:, 0, :], ACT.Sqrt).then_inc(s["nsd"], 1)
                if h == MIX_AT and j == 4:
                    ln.deviation(act, 0, SR)
                if h == 4 and j == 0:
                    keys_turn_act(act, NT, SR)
                if 4 <= h:
                    step, k = KEYS_AT[j % 8], 2 * (h - 4) + j // 8
                    if step == "q":
                        keys_q_act(act, NT, k, SR)
                    if step == "t":
                        keys_t_act(act, NT, k, SR)
                    if step == "s":
                        keys_s_act(act, NT, k, SR)
                    if step == "exp":
                        keys_gate_act(act, NT, k, SR)
            return side

        def sample_dve(dve, ch):
            osq = eq[0:H * DS].rearrange("p a b -> p (a b)")[:, 0:DB * VD].rearrange("p (b d) -> p b d", b=DB)
            wide = [H * DS, DB, VD]

            def side(h, j):
                if h == 0 and j == 0:
                    ch.sync()
                    ch.add(dve.tensor_tensor(osq, oS[:], oS[:], ALU.mult))
                    ch.sync()
                    ch.add(dve.tensor_reduce(rs[:, 2, :], osq, AX_X, ALU.add))
                    ch.sync()
                    dve.tensor_scalar(rs[:, 0, :], rs[:, 2, :], 1.0 / VD, EPS, ALU.mult,
                                      ALU.add).then_inc(s["nsq"], 1)
                    dve.wait_ge(s["nsd"], 1)
                    ch.add(dve.reciprocal(rs[:, 2, :], rs[:, 1, :]))
                    ch.sync()
                    ch.add(dve.tensor_tensor(oS[:], oS[:], rs[:, 2, :].unsqueeze(2).to_broadcast(wide), ALU.mult))
                    ch.sync()
                    dve.tensor_tensor(oS[:], oS[:], g_row[0:H * DS].unsqueeze(1).to_broadcast(wide),
                                      ALU.mult).then_inc(s["on"], 1)
                if h == 0 and j == 2:
                    dve.wait_ge(s["ot"], 1)
                    dve.tensor_copy(mixS[:, 0:H, :].rearrange("p h (b q) -> p h b q", b=DB),
                                    SB_[:, 0:DB * H * DS].rearrange("p (b h q) -> p h b q", b=DB, h=H)
                                    ).then_inc(s["sum"], 1)
                if h == MIX_AT and j == 4:
                    dve.wait_ge(s["xg"], 32)
                    dve.wait_ge(s["x1"], 16)
                    dve.wait_ge(s["mm"], 1)
                    for b in range(2):
                        part = x1n[0:SR, b * 512:b * 512 + 512]
                        ch.add(dve.scalar_tensor_tensor(out=part, in0=part, scalar=ALPHA, in1=KB[b][0:SR, :],
                                                        op0=ALU.mult, op1=ALU.add))
                    ln.run(dve, ch, 0, SR, x1n).then_inc(s["xst"], 1)
                if h == 4 and j == 0:
                    keys_turn_dve(dve, NT, SR)
                if 4 <= h < PH:
                    step, k = KEYS_AT[j % 8], 2 * (h - 4) + j // 8
                    if step == "rank0":
                        keys_rank_dve(dve, ch, NT, k, SR, 0)
                    if step == "rank1":
                        keys_rank_dve(dve, ch, NT, k, SR, 1)
                    if step == "pairs":
                        keys_pairs_dve(dve, ch, NT, k, SR)
                    if step == "gate":
                        keys_gate_dve(dve, ch, NT, k, SR)
            return side

        PC = PLE // P
        Z, L, XB = KB, [SB_, OB], [QB, TB]

        def out_load(sp, T):
            n, R = T % 2, P if T < NT else SR
            if T == NT - 1:
                sp.wait_ge(s["fst"], 16 * (T + 1))
            src, at = (a["p_prompt"], T * P) if T < NT else (a["p_sample"], 0)
            sp.dma_start(x2[n][0:R, :], rows(x1_d, T * P, R)).then_inc(s_in[n], 16)
            if T < NT:
                sp.dma_start(f[n][0:R, :], rows(ffn_d, T * P, R)).then_inc(s_in[n], 16)
            sp.dma_start(pr[n][0:R, :], rows(src, at, R)).then_inc(s_in[n], 16)

        def out_store(sp, T):
            n, R = T % 2, P if T < NT else SR
            dst, at = (o["y_prompt"], T * P) if T < NT else (o["y_sample"], 0)
            sp.wait_ge(s["y"], T + 1)
            sp.dma_start(rows(dst, at, R), f[n][0:R, :]).then_inc(s_st[n], 16)
            sp.wait_ge(s_st[n], 16 * (T // 2 + 1))

        def loaded(T):
            return 48 * (T // 2) + (48 if T < NT else 32)

        def out_turn_p_pe(pe, T, R):
            n = T % 2
            pe.wait_ge(s_in[n], loaded(T))
            pe.wait_ge(s["xT"], 2 * T)
            for c in range(PC):
                last = pe.transpose(XB[0][:, c * P:c * P + R], pr[n][0:R, c * P:c * P + P], ident[0:R, 0:R])
            last.then_inc(s["pp"], 1)

        def out_turn_pe(pe, T, R):
            n = T % 2
            pe.wait_ge(s["x2"], T + 1)
            pe.wait_ge(s["pT"], T + 1)
            for h in range(2):
                for c in range(4):
                    k = 4 * h + c
                    last = pe.transpose(XB[h][:, c * P:c * P + R], x2[n][0:R, k * P:k * P + P], ident[0:R, 0:R])
                last.then_inc(s["tp"], 1)

        def out_p_pe(pe, T, R):
            if T == 0:
                pe.wait_ge(s["w2"], 16 * 9)
            pe.wait_ge(s["pT"], T + 1)
            pe.wait_ge(s["lr"], T)
            for h in range(2):
                for k in range(PC):
                    last = pe.matmul(L[h][0:R, :], prT[:, k, 0:R], wp[:, k, h * 512:h * 512 + 512],
                                     start=(k == 0), stop=(k == PC - 1))
            last.then_inc(s["l"], 1)

        def out_z_pe(pe, T, R, h):
            if h == 0:
                pe.wait_ge(s["xT"], 2 * T + 2)
                pe.wait_ge(s["zr"], T)
            for k in range(KC):
                last = pe.matmul(Z[h][0:R, :], x2T[:, k, 0:R], wg[:, k, h * 512:h * 512 + 512],
                                 start=(k == 0), stop=(k == KC - 1))
            last.then_inc(s["z"], 1)

        def out_turn_p_act(act, T, R):
            act.wait_ge(s["pp"], T + 1)
            act.activation(prT[:, :, 0:R], XB[0][:, 0:PC * P].rearrange("p (c t) -> p c t", c=PC)[:, :, 0:R],
                           ACT.Copy).then_inc(s["pT"], 1)

        def out_turn_act(act, T, R):
            for h in range(2):
                act.wait_ge(s["tp"], 2 * T + h + 1)
                act.activation(x2T[:, 4 * h:4 * h + 4, 0:R], turned(XB[h], R), ACT.Copy).then_inc(s["xT"], 1)

        def out_gate_act(act, T, R):
            act.wait_ge(s["zr"], T + 1)
            act.activation(f[T % 2][0:R], f[T % 2][0:R], ACT.Tanh, scale=0.5).then_inc(s["tg"], 1)

        def out_norm_dve(dve, ch, T, R):
            n = T % 2
            if T == 0:
                dve.wait_ge(s["gb"], 48)
            dve.wait_ge(s_in[n], loaded(T))
            if T < NT:
                ch.add(dve.scalar_tensor_tensor(out=x2[n][0:R], in0=x2[n][0:R], scalar=ALPHA, in1=f[n][0:R],
                                                op0=ALU.mult, op1=ALU.add))
            else:
                dve.wait_ge(s["fs"], 1)
                for b in range(2):
                    part = x2[n][0:R, b * 512:b * 512 + 512]
                    ch.add(dve.scalar_tensor_tensor(out=part, in0=part, scalar=ALPHA, in1=ACC[b][0:R, :],
                                                    op0=ALU.mult, op1=ALU.add))
            ln2.run(dve, ch, T, R, x2[n]).then_inc(s["x2"], 1)

        def out_bias_dve(dve, T, R):
            dve.wait_ge(s["z"], 2 * T + 2)
            for h in range(2):
                last = dve.tensor_tensor(f[T % 2][0:R, h * 512:h * 512 + 512], Z[h][0:R, :],
                                         gb[0:R, h * 512:h * 512 + 512], ALU.add)
            last.then_inc(s["zr"], 1)

        def out_gate_dve(dve, T, R):
            n = T % 2
            dve.wait_ge(s["tg"], T + 1)
            dve.wait_ge(s["l"], T + 1)
            for h in range(2):
                part = f[n][0:R, h * 512:h * 512 + 512]
                last = dve.scalar_tensor_tensor(out=part, in0=part, scalar=1.0, in1=L[h][0:R, :],
                                                op0=ALU.add, op1=ALU.mult)
            last.then_inc(s["lr"], 1)
            dve.wait_ge(s["lr"], T + 1)
            dve.scalar_tensor_tensor(out=f[n][0:R], in0=f[n][0:R], scalar=0.5, in1=x2[n][0:R],
                                     op0=ALU.mult, op1=ALU.add).then_inc(s["y"], 1)

        def half_steps(h, j):
            return 2 * h + j // 8 - 1, j % 8

        def out_pe(pe):
            def side(h, j):
                T, at = half_steps(h, j)
                if 0 <= T < NT:
                    if at == 0:
                        out_turn_p_pe(pe, T, P)
                        out_turn_pe(pe, T, P)
                    if at == 1:
                        out_p_pe(pe, T, P)
                    if at == 2:
                        out_z_pe(pe, T, P, 0)
                    if at == 5:
                        out_z_pe(pe, T, P, 1)
            return side

        def out_act(act):
            def side(h, j):
                T, at = half_steps(h, j)
                if at == 3 and T + 1 < NT:
                    ln2.deviation(act, T + 1, P)
                if 0 <= T < NT:
                    if at == 0:
                        out_turn_p_act(act, T, P)
                        out_turn_act(act, T, P)
                    if at == 6:
                        out_gate_act(act, T, P)
            return side

        def out_dve(dve, ch):
            def side(h, j):
                T, at = half_steps(h, j)
                if at == 3 and T + 1 < NT:
                    out_norm_dve(dve, ch, T + 1, P)
                if 0 <= T < NT:
                    if at == 6:
                        out_bias_dve(dve, T, P)
                    if at == 7:
                        out_gate_dve(dve, T, P)
            return side

        none = lambda h, j: None

        def side_only(side):
            for h in range(PH):
                for j in range(TOPK):
                    side(h, j)

        with nc.Block() as block:
            @block.sync
            def _(sp):
                sp.dma_start(pt[:], a["page_table"]).then_inc(s["pt"], 16)
                sp.dma_start(x1n[:], rows(x1_d, 0, P)).then_inc(s["x1n"], 16)
                kv = a["peer_keys"].rearrange("(g q p) d -> g p q d", q=8, p=P)
                for g in range(2):
                    sp.dma_start(v[g][:].rearrange("p (q d) -> p q d", q=8), kv[g]).then_inc(s["kr"], 16)
                sp.wait_ge(s["pt"], 16)
                pages(sp, 0)

            @block.gpsimd
            def _(pool):
                pool.memset(qst[:], 0.0)
                pool.iota(iota[:], pattern=[[1, NC]], base=0, channel_multiplier=0,
                          allow_small_or_imprecise_dtypes=True).then_inc(s["zero"], 1)

            @block.tensor
            def _(pe):
                pe.wait_ge(s["kr"], 32)
                for t in range(4):
                    if t > 1:
                        pe.wait_ge(s["kte"], t - 1)
                    for c in range(4):
                        m = 4 * t + c
                        last = pe.transpose(KB[t % 2][:, c * P:c * P + P],
                                            v[m // 8][:, (m % 8) * P:(m % 8) * P + P], ident[:])
                    last.then_inc(s["kt"], 1)
                pe.wait_ge(s["kte"], 4)
                pe.wait_ge(s_wq, 16 * KC)
                side_only(side_pe(pe, 0))
                pe.sem_inc(s["vpe"], len(PES))

            @block.scalar
            def _(act):
                for t in range(4):
                    act.wait_ge(s["kt"], t + 1)
                    act.activation(keysT[:, 4 * t:4 * t + 4, :], KB[t % 2][:].rearrange("p (c n) -> p c n", c=4),
                                   ACT.Copy).then_inc(s["kte"], 1)
                act.wait_ge(s["zero"], 1)
                act.wait_ge(s["x1n"], 16)
                act.activation(x_cur[:], x1n[:], ACT.Copy).then_inc(s["xcur"], 1)
                side_only(side_act(act, 0))

            @block.vector
            def _(dve):
                ch = Chain(dve, s["ch"])
                dve.wait_ge(s["zero"], 1)
                side_only(side_dve(dve, ch, 0))
                dve.tensor_copy(idxU[0][:], idx_all[:, 0, :]).then_inc(s["prepU"], 1)
                ch.add(dve.tensor_tensor(ident2[:], ident[:, 0:SR], ident[:, SR:P], ALU.add))
                dve.sem_inc(s["ufree"], NU)
                dve.sem_inc(s["vdve"], len(DVS))
                ch.restart()

        with nc.Block() as block:
            @block.sync
            def _(sp):
                def store(t):
                    sp.wait_ge(s["fo"], t + 1)
                    sp.sem_inc(s["stick"], 1)
                    sp.dma_start(rows(ffn_d, t * P, P), facc[:]).then_inc(s["fst"], 16)

                sp.wait_ge(s["xcur"], 1)
                sp.dma_start(x1n[:], rows(x1_d, P, P)).then_inc(s["x1n"], 16)
                pages(sp, 1)
                with sp.Fori(0, NT - 2) as i:
                    sp.wait_ge(s["xcur"], i + 2)
                    sp.sem_inc(s["stick"], 1)
                    sp.dma_start(x1n[:], rows(x1_d, (i + 2) * P, P)).then_inc(s["x1n"], 16)
                    pages(sp, i + 2, lambda: store(i))
                sp.wait_ge(s["xcur"], NT)
                sp.dma_start(x1n[0:SR, :], a["x_sample"]).then_inc(s["x1"], 16)
                sp.wait_ge(s["ot"], 1)
                wv = a["w_out"].rearrange("(k p) n -> p k n", p=P)
                for k in range(KC):
                    sp.dma_start(w_out[:, k, :], wv[:, k, :]).then_inc(s["wo"], 16)
                sp.dma_start(g1, a["ln1_g"].to_broadcast([SR, D])).then_inc(s["xg"], 16)
                sp.dma_start(b1, a["ln1_b"].to_broadcast([SR, D])).then_inc(s["xg"], 16)
                store(NT - 2)
                sp.wait_ge(s["xst"], 1)
                sp.dma_start(rows(x1_d, SEQ, SR), x1n[0:SR, :]).then_inc(s["x1"], 16)
                sp.wait_ge(s["x1"], 32)
                sp.dma_start(x1n[0:SR, :], rows(x1_d, SEQ, SR)).then_inc(s["x1n"], 16)
                sp.dma_start(x1n[SR:P, :], rows(x1_d, SEQ, SR)).then_inc(s["xh"], 16)
                sp.wait_ge(s["q"], PH * NT + PH // 2)
                wv = a["ple_gate_w"].rearrange("(k p) n -> p k n", p=P)
                for k in range(KC):
                    sp.dma_start(wg[:, k, :], wv[:, k, :]).then_inc(s["w2"], 16)
                out_load(sp, 0)
                out_load(sp, 1)
                for h in range(HS):
                    sp.wait_ge(s["tk"], PH * NT + HS + h + 1)
                    sp.dma_start(idx_all[SR:P, h, :], idx_all[0:SR, HS + h, :]).then_inc(s["half"], 16)
                    sp.dma_start(gt_all[SR:P, h, :], gt_all[0:SR, HS + h, :]).then_inc(s["half"], 16)
                    sp.wait_ge(s["half"], 32 * h + 32)
                sp.wait_ge(s["q"], PH * (NT + 1))
                for name, dst in (("ln2_g", g2), ("ln2_b", b2), ("ple_gate_b", gb)):
                    sp.dma_start(dst, a[name].to_broadcast([P, D])).then_inc(s["gb"], 16)
                sp.dma_start(wp, a["ple_w"].rearrange("(k p) n -> p k n", p=P)).then_inc(s["w2"], 16)
                store(NT - 1)
                for T in range(2, NT):
                    out_store(sp, T - 2)
                    out_load(sp, T)
                out_store(sp, NT - 2)
                out_load(sp, NT)
                out_store(sp, NT - 1)
                out_store(sp, NT)

            @block.gpsimd
            def _(pool):
                def turn(body):
                    with pool.Fori(0, NT - 2) as i:
                        body(i)

                experts(lambda U, V, side: step_pool(pool, U, V), turn, none, lambda i: none, none, none)

            @block.tensor
            def _(pe):
                def turn(body):
                    with pe.Fori(0, NT - 2) as i:
                        body(i)

                experts(lambda U, V, side: step_pe(pe, U, V, side), turn, side_pe(pe, 1),
                        lambda i: side_pe(pe, i), sample_pe(pe), out_pe(pe))
                out_turn_p_pe(pe, NT, SR)
                out_p_pe(pe, NT, SR)
                out_turn_pe(pe, NT, SR)
                out_z_pe(pe, NT, SR, 0)
                out_z_pe(pe, NT, SR, 1)

            @block.scalar
            def _(act):
                def turn(body):
                    with act.Fori(0, NT - 2) as i:
                        body(i)

                experts(lambda U, V, side: step_act(act, U, V, side), turn, side_act(act, 1),
                        lambda i: side_act(act, i), sample_act(act), out_act(act))
                out_turn_p_act(act, NT, SR)
                ln2.deviation(act, NT, SR)
                out_turn_act(act, NT, SR)
                out_gate_act(act, NT, SR)

            @block.vector
            def _(dve):
                ch = Chain(dve, s["ch"])

                def turn(body):
                    ch.restart()
                    with dve.Fori(0, NT - 2) as i:
                        body(i)
                        ch.restart()

                experts(lambda U, V, side: step_dve(dve, ch, U, V, side), turn, side_dve(dve, ch, 1),
                        lambda i: side_dve(dve, ch, i), sample_dve(dve, ch), out_dve(dve, ch))
                out_norm_dve(dve, ch, NT, SR)
                out_bias_dve(dve, NT, SR)
                out_gate_dve(dve, NT, SR)


_ROWS = {
    "x_prompt": (SEQ, D), "x_sample": (SR, D), "p_prompt": (SEQ, PLE), "p_sample": (SR, PLE),
    "cache_k": None, "cache_v": None, "state_h": (DB, RW), "state_conv": (DB * (CW - 1), RW),
    "page_table": (1, DB * NPG), "w_in": (D, IN), "lambda_q1": (1, QK), "lambda_k1": (1, QK),
    "lambda_q2": (1, QK), "lambda_k2": (1, QK), "subln_g": (1, VD), "conv_w": (CW, RW), "conv_b": (1, RW),
    "rg_wa": (8, 64, 64), "rg_ba": (1, RW), "rg_wx": (8, 64, 64), "rg_bx": (1, RW), "rg_lambda": (1, RW),
    "w_out": (D, D), "ln1_g": (1, D), "ln1_b": (1, D), "peer_wq": (D, 2 * PH * PK),
    "peer_keys": (PH * 2 * PK, P), "peer_u": (PK * PK, D), "peer_v": (PK * PK, D),
    "ln2_g": (1, D), "ln2_b": (1, D), "ple_w": (PLE, D), "ple_gate_w": (D, D), "ple_gate_b": (1, D),
}
_OUTS = [
    ("y_prompt", (SEQ, D), (1, SEQ, D)), ("y_sample", (SR, D), (DB, DS, D)),
    ("k_prompt", (SEQ, AW), (1, 1, SEQ, H, VD)), ("v_prompt", (SEQ, AW), (1, 1, SEQ, H, VD)),
    ("h_prompt", (1, RW), (1, 1, RW)), ("conv_prompt", (CW - 1, RW), (1, 1, CW - 1, RW)),
    ("k_sample", (SR, AW), (1, DB, DS, H, VD)), ("v_sample", (SR, AW), (1, DB, DS, H, VD)),
    ("h_sample", (DB, RW), (1, DB, RW)), ("conv_sample", (DB * (CW - 1), RW), (1, DB, CW - 1, RW)),
]


def rope_table():
    import numpy as np

    freq = np.float32(500000.0) ** (-np.arange(0, ROT, 2, dtype=np.float32) / np.float32(ROT))
    pos = np.concatenate([np.arange(SEQ), np.tile(PAST + np.arange(DS), DB)]).astype(np.float32)
    ang = pos[:, None] * freq[None, :]
    return np.stack([np.cos(ang), np.sin(ang)], 1).astype(np.float32)


def kernel(**inputs):
    import numpy as np
    import concourse.bacc as bacc
    from concourse.bass_utils import run_bass_kernel_spmd

    nc = bacc.Bacc("TRN2", target_bir_lowering=False, num_devices=1)
    arrays, a, o = {}, {}, {}
    for name, shape in _ROWS.items():
        x = np.ascontiguousarray(inputs[name])
        if shape is None:
            shape = (x.shape[1] * x.shape[2], AW)
        arrays["in_" + name] = x.reshape(shape)
    arrays["in_rope"] = rope_table()
    for name, x in arrays.items():
        a[name[3:]] = nc.dram_tensor(name, x.shape, mybir.dt.from_np(x.dtype), kind="ExternalInput").ap()
    for name, shape, _ in _OUTS:
        o[name] = nc.dram_tensor("out_" + name, shape, F32, kind="ExternalOutput").ap()
    program(nc, a, o)
    r = run_bass_kernel_spmd(nc, [arrays], core_ids=[0])
    return tuple(r.results[0]["out_" + name].reshape(shape) for name, _, shape in _OUTS)
```
